# Optimizing a Trainium2 kernel written in Bass

```python
import jax, jax.numpy as jnp
from jax import lax
import numpy as np

D_MODEL = 1024
BATCH = 1
SEQ = 1024
DEPTH = 1

RET_HEADS = 4
RET_DK = 128
RET_DV = 256
RET_CHUNK = 128
SWA_HEADS = 8
SWA_KV_HEADS = 2
SWA_DH = 64
WINDOW = 128
D_FF = 4 * D_MODEL
EPS = 1e-6

RET_QK = RET_HEADS * RET_DK
RET_V = RET_HEADS * RET_DV
SWA_Q = SWA_HEADS * SWA_DH
SWA_KV = SWA_KV_HEADS * SWA_DH
IN_SPLITS = (RET_QK, RET_QK, RET_V, RET_V, SWA_Q, SWA_KV, SWA_KV, D_MODEL, D_MODEL)
D_IN = sum(IN_SPLITS)
SPLIT_IDX = tuple(int(i) for i in np.cumsum(IN_SPLITS)[:-1])


def rmsnorm(x, g):
    xf = x.astype(jnp.float32)
    y = xf * lax.rsqrt(jnp.mean(xf * xf, axis=-1, keepdims=True) + EPS)
    return (y * g.astype(jnp.float32)).astype(x.dtype)

def retention_chunkwise(q, k, v):
    B, T, H, dk = q.shape
    dv = v.shape[-1]
    C = RET_CHUNK
    N = T // C
    f32 = jnp.float32
    log_gamma = jnp.log(1.0 - jnp.exp2(-5.0 - jnp.arange(H, dtype=f32)))
    q = q.astype(f32).reshape(B, N, C, H, dk)
    k = k.astype(f32).reshape(B, N, C, H, dk) * (dk ** -0.5)
    v = v.astype(f32).reshape(B, N, C, H, dv)
    pos = jnp.arange(C, dtype=f32)
    diff = pos[:, None] - pos[None, :]
    causal = diff >= 0
    decay = jnp.where(causal[None], jnp.exp(log_gamma[:, None, None] * jnp.where(causal, diff, 0.0)[None]), 0.0)
    qk = jnp.einsum('bnihd,bnjhd->bnhij', q, k) * decay[None, None]
    o_inner = jnp.einsum('bnhij,bnjhe->bnihe', qk, v)
    k_dec = k * jnp.exp(log_gamma[None, :] * (C - 1.0 - pos)[:, None])[None, None, :, :, None]
    kv = jnp.einsum('bnjhd,bnjhe->nbhde', k_dec, v)
    chunk_decay = jnp.exp(log_gamma * C)[None, :, None, None]

    def step(s, kv_n):
        return chunk_decay * s + kv_n, s

    _, s_prev = lax.scan(step, jnp.zeros((B, H, dk, dv), f32), kv)
    q_dec = q * jnp.exp(log_gamma[None, :] * (pos + 1.0)[:, None])[None, None, :, :, None]
    o_cross = jnp.einsum('bnihd,nbhde->bnihe', q_dec, s_prev)
    o = (o_inner + o_cross).reshape(B, T, H, dv)
    mu = jnp.mean(o, axis=-1, keepdims=True)
    var = jnp.mean(jnp.square(o - mu), axis=-1, keepdims=True)
    return (o - mu) * lax.rsqrt(var + EPS)

def swa_gqa_sinks(q, k, v, sinks):
    B, T, Hq, dh = q.shape
    G = k.shape[2]
    R = Hq // G
    W = WINDOW
    N = T // W
    f32 = jnp.float32
    qb = q.reshape(B, N, W, G, R, dh)
    kb = k.reshape(B, N, W, G, dh)
    vb = v.reshape(B, N, W, G, dh)
    pad = ((0, 0), (1, 0), (0, 0), (0, 0), (0, 0))
    kk = jnp.concatenate([jnp.pad(kb, pad)[:, :-1], kb], axis=2)
    vv = jnp.concatenate([jnp.pad(vb, pad)[:, :-1], vb], axis=2)
    s = jnp.einsum('bnigrd,bnjgd->bgrnij', qb, kk).astype(f32) * (dh ** -0.5)
    qpos = jnp.arange(W)[:, None] + W
    kpos = jnp.arange(2 * W)[None, :]
    dist = qpos - kpos
    valid = (dist >= 0) & (dist < W)
    blk_valid = valid[None] & ((jnp.arange(N)[:, None, None] > 0) | (kpos >= W)[None])
    slopes = jnp.exp2(-8.0 / Hq * jnp.arange(1, Hq + 1, dtype=f32)).reshape(G, R)
    s = s - slopes[None, :, :, None, None, None] * dist.astype(f32)[None, None, None, None]
    s = jnp.where(blk_valid[None, None, None], s, -jnp.inf)
    sink = sinks.astype(f32).reshape(G, R)[None, :, :, None, None, None]
    m = jnp.maximum(jnp.max(s, axis=-1, keepdims=True), sink)
    p = jnp.exp(s - m)
    p = p / (jnp.sum(p, axis=-1, keepdims=True) + jnp.exp(sink - m))
    out = jnp.einsum('bgrnij,bnjgd->bnigrd', p, vv.astype(f32))
    return out.reshape(B, T, Hq * dh)

def first_inputs(seed: int = 0) -> dict:
    key = jax.random.key(seed)
    ks = jax.random.split(key, 13)
    f32 = jnp.float32

    def dense(k, fan_in, fan_out):
        return jax.random.normal(k, (DEPTH, fan_in, fan_out), f32) * (fan_in ** -0.5)

    def gain(k):
        return 1.0 + 0.02 * jax.random.normal(k, (DEPTH, D_MODEL), f32)

    return {
        "x": jax.random.normal(ks[0], (BATCH, SEQ, D_MODEL), f32),
        "pre_mix_norm": gain(ks[1]),
        "w_in": dense(ks[2], D_MODEL, D_IN),
        "w_ret_out": dense(ks[3], RET_V, D_MODEL),
        "w_swa_out": dense(ks[4], SWA_Q, D_MODEL),
        "w_out": dense(ks[5], D_MODEL, D_MODEL),
        "sinks": 0.5 * jax.random.normal(ks[6], (DEPTH, SWA_HEADS), f32),
        "post_mix_norm": gain(ks[7]),
        "pre_mlp_norm": gain(ks[8]),
        "w_up": dense(ks[9], D_MODEL, D_FF),
        "w_down": dense(ks[10], D_FF, D_MODEL),
        "post_mlp_norm": gain(ks[11]),
    }

def first_block(x, pre_mix_norm, w_in, w_ret_out, w_swa_out, w_out, sinks, post_mix_norm, pre_mlp_norm, w_up, w_down, post_mlp_norm):
    B, T, _ = x.shape
    dt = x.dtype
    for l in range(DEPTH):
        h = rmsnorm(x, pre_mix_norm[l])
        proj = h @ w_in[l]
        q_r, k_r, v_r, g_r, q_s, k_s, v_s, gate_r, gate_s = jnp.split(proj, SPLIT_IDX, axis=-1)
        ret = retention_chunkwise(q_r.reshape(B, T, RET_HEADS, RET_DK),
                                  k_r.reshape(B, T, RET_HEADS, RET_DK),
                                  v_r.reshape(B, T, RET_HEADS, RET_DV)).reshape(B, T, RET_V)
        ret = (jax.nn.silu(g_r.astype(jnp.float32)) * ret).astype(dt)
        y_r = ret @ w_ret_out[l]
        swa = swa_gqa_sinks(q_s.reshape(B, T, SWA_HEADS, SWA_DH),
                            k_s.reshape(B, T, SWA_KV_HEADS, SWA_DH),
                            v_s.reshape(B, T, SWA_KV_HEADS, SWA_DH),
                            sinks[l]).astype(dt)
        y_s = swa @ w_swa_out[l]
        merged = jax.nn.sigmoid(gate_r) * y_r + jax.nn.sigmoid(gate_s) * y_s
        x = x + rmsnorm(merged @ w_out[l], post_mix_norm[l])
        h = rmsnorm(x, pre_mlp_norm[l])
        u = jnp.square(jax.nn.relu(h @ w_up[l]))
        x = x + rmsnorm(u @ w_down[l], post_mlp_norm[l])
    return x


MIX_WIDTH = D_MODEL
POOL_WIDTH = MIX_WIDTH // 2
POOL_WINDOWS = (2, 4, 8, 16)
N_POOL_GROUPS = len(POOL_WINDOWS)
POOL_GROUP_WIDTH = POOL_WIDTH // N_POOL_GROUPS
ATTN_WIDTH = MIX_WIDTH - POOL_WIDTH
HEAD_DIM = 64
N_HEADS = ATTN_WIDTH // HEAD_DIM
IN_WIDTH = POOL_WIDTH + 3 * ATTN_WIDTH + N_HEADS
D_FF_2 = 4 * D_MODEL
BLOCK_Q = 128
LN_EPS = 1e-5
NEG_INF = -1e30
ALPHA = float((2.0 * DEPTH) ** 0.25)
BETA = float((8.0 * DEPTH) ** -0.25)


def layer_norm(x, g, b):
    xf = x.astype(jnp.float32)
    mu = jnp.mean(xf, axis=-1, keepdims=True)
    var = jnp.mean(jnp.square(xf - mu), axis=-1, keepdims=True)
    y = (xf - mu) * lax.rsqrt(var + LN_EPS)
    return (y * g.astype(jnp.float32) + b.astype(jnp.float32)).astype(x.dtype)

def pool_mixer(u, w, scale):
    B, S, _ = u.shape
    uf = u.astype(jnp.float32)
    c = jnp.cumsum(uf, axis=1)
    pos = jnp.arange(1, S + 1, dtype=jnp.float32)
    diffs = []
    for g, win in enumerate(POOL_WINDOWS):
        sl = slice(g * POOL_GROUP_WIDTH, (g + 1) * POOL_GROUP_WIDTH)
        cg = c[..., sl]
        shifted = jnp.pad(cg, ((0, 0), (win, 0), (0, 0)))[:, :S]
        count = jnp.minimum(pos, float(win))[None, :, None]
        diffs.append((cg - shifted) / count - uf[..., sl])
    d = jnp.concatenate(diffs, axis=-1).astype(u.dtype)
    d = d.reshape(B, S, N_POOL_GROUPS, POOL_GROUP_WIDTH)
    y = jnp.einsum('bsgc,gcd->bsgd', d, w).reshape(B, S, POOL_WIDTH)
    return y * scale

def forgetting_attention(q, k, v, f_logit):
    B, S, _ = q.shape
    to_heads = lambda t: t.reshape(B, S, N_HEADS, HEAD_DIM).transpose(0, 2, 1, 3)
    q, k, v = to_heads(q), to_heads(k), to_heads(v)
    log_f = jax.nn.log_sigmoid(f_logit.astype(jnp.float32)).transpose(0, 2, 1)
    cf = jnp.cumsum(log_f, axis=-1)
    scale = HEAD_DIM ** -0.5
    kpos = jnp.arange(S)
    n_blocks = S // BLOCK_Q

    def one_block(i):
        start = i * BLOCK_Q
        qb = lax.dynamic_slice_in_dim(q, start, BLOCK_Q, axis=2)
        cq = lax.dynamic_slice_in_dim(cf, start, BLOCK_Q, axis=2)
        qpos = start + jnp.arange(BLOCK_Q)
        s = jnp.einsum('bhqd,bhkd->bhqk', qb, k, preferred_element_type=jnp.float32) * scale
        s = s + cq[..., :, None] - cf[..., None, :]
        s = jnp.where(kpos[None, :] <= qpos[:, None], s, NEG_INF)
        p = jax.nn.softmax(s, axis=-1)
        return jnp.einsum('bhqk,bhkd->bhqd', p.astype(v.dtype), v)

    out = lax.map(one_block, jnp.arange(n_blocks))
    out = out.transpose(1, 0, 3, 2, 4).reshape(B, S, ATTN_WIDTH)
    return out

def hybrid_mixer(x, w_in, b_f, pool_w, pool_scale, w_out):
    h = x @ w_in
    o = 0
    u = h[..., o:o + POOL_WIDTH]; o += POOL_WIDTH
    q = h[..., o:o + ATTN_WIDTH]; o += ATTN_WIDTH
    k = h[..., o:o + ATTN_WIDTH]; o += ATTN_WIDTH
    v = h[..., o:o + ATTN_WIDTH]; o += ATTN_WIDTH
    f_logit = h[..., o:o + N_HEADS] + b_f
    pool_out = pool_mixer(u, pool_w, pool_scale)
    attn_out = forgetting_attention(q, k, v, f_logit)
    return jnp.concatenate([pool_out, attn_out], axis=-1) @ w_out

def second_inputs(seed: int = 0) -> dict:
    key = jax.random.key(seed)
    ks = jax.random.split(key, 12)
    f32 = jnp.float32
    x = jax.random.normal(ks[0], (BATCH, SEQ, D_MODEL), f32)
    w_in = jax.random.normal(ks[1], (DEPTH, D_MODEL, IN_WIDTH), f32) * D_MODEL ** -0.5
    col_scale = np.ones((IN_WIDTH,), np.float32)
    col_scale[:POOL_WIDTH] = BETA
    col_scale[POOL_WIDTH + 2 * ATTN_WIDTH:POOL_WIDTH + 3 * ATTN_WIDTH] = BETA
    w_in = w_in * jnp.asarray(col_scale)
    b_f = 3.0 + 0.5 * jax.random.normal(ks[2], (DEPTH, N_HEADS), f32)
    pool_w = jax.random.normal(ks[3], (DEPTH, N_POOL_GROUPS, POOL_GROUP_WIDTH, POOL_GROUP_WIDTH), f32) * POOL_GROUP_WIDTH ** -0.5
    pool_scale = 1.0 + 0.1 * jax.random.normal(ks[4], (DEPTH, POOL_WIDTH), f32)
    w_out = jax.random.normal(ks[5], (DEPTH, MIX_WIDTH, D_MODEL), f32) * (MIX_WIDTH ** -0.5 * BETA)
    ln1_g = 1.0 + 0.05 * jax.random.normal(ks[6], (DEPTH, D_MODEL), f32)
    ln1_b = 0.02 * jax.random.normal(ks[7], (DEPTH, D_MODEL), f32)
    w_mlp1 = jax.random.normal(ks[8], (DEPTH, D_MODEL, D_FF_2), f32) * D_MODEL ** -0.5
    w_mlp2 = jax.random.normal(ks[9], (DEPTH, D_FF_2, D_MODEL), f32) * (D_FF_2 ** -0.5 * BETA)
    ln2_g = 1.0 + 0.05 * jax.random.normal(ks[10], (DEPTH, D_MODEL), f32)
    ln2_b = 0.02 * jax.random.normal(ks[11], (DEPTH, D_MODEL), f32)
    return {"x": x, "w_in": w_in, "b_f": b_f, "pool_w": pool_w, "pool_scale": pool_scale,
            "w_out": w_out, "ln1_g": ln1_g, "ln1_b": ln1_b, "w_mlp1": w_mlp1,
            "w_mlp2": w_mlp2, "ln2_g": ln2_g, "ln2_b": ln2_b}

def second_block(x, w_in, b_f, pool_w, pool_scale, w_out, ln1_g, ln1_b, w_mlp1, w_mlp2, ln2_g, ln2_b):
    for l in range(DEPTH):
        mix = hybrid_mixer(x, w_in[l], b_f[l], pool_w[l], pool_scale[l], w_out[l])
        x = layer_norm(ALPHA * x + mix, ln1_g[l], ln1_b[l])
        hid = jnp.square(jax.nn.relu(x @ w_mlp1[l]))
        x = layer_norm(ALPHA * x + hid @ w_mlp2[l], ln2_g[l], ln2_b[l])
    return x


def setup_inputs(seed=0):
    out = dict(first_inputs(seed))
    for name, value in second_inputs(seed + 1).items():
        if name != "x":
            out[name + "_2"] = value
    return out


def reference(
    x, pre_mix_norm, w_in, w_ret_out, w_swa_out, w_out, sinks, post_mix_norm, pre_mlp_norm,
    w_up, w_down, post_mlp_norm, w_in_2, b_f_2, pool_w_2, pool_scale_2, w_out_2, ln1_g_2,
    ln1_b_2, w_mlp1_2, w_mlp2_2, ln2_g_2, ln2_b_2,
):
    x = first_block(
        x, pre_mix_norm, w_in, w_ret_out, w_swa_out, w_out, sinks, post_mix_norm, pre_mlp_norm,
        w_up, w_down, post_mlp_norm,
    )
    return second_block(
        x, w_in_2, b_f_2, pool_w_2, pool_scale_2, w_out_2, ln1_g_2, ln1_b_2, w_mlp1_2, w_mlp2_2,
        ln2_g_2, ln2_b_2,
    )


_drawn_inputs = setup_inputs


def setup_inputs(seed=0):
    import zlib

    import numpy as np

    out = dict(_drawn_inputs(seed))
    spreads = {}
    factors = {'post_mix_norm': 3.557,
     'pre_mlp_norm': 4.133,
     'post_mlp_norm': 4.521,
     'b_f_2': 4.328,
     'pool_scale_2': 3.191,
     'ln2_b_2': 2.667}
    for name, (base, spread) in spreads.items():
        noise = np.random.default_rng([zlib.crc32(name.encode()), seed]).standard_normal(out[name].shape)
        drawn = base * np.exp(spread * noise) if base else spread * noise
        out[name] = __import__('jax').numpy.asarray(drawn.astype(out[name].dtype))
    for name, factor in factors.items():
        out[name] = (out[name] * factor).astype(out[name].dtype)
    return out
```

```python
from contextlib import ExitStack

import numpy as np
import concourse.bass as bass
from concourse import mybir

F32 = mybir.dt.float32
F32R = mybir.dt.float32r
BF16 = mybir.dt.bfloat16
ACT = mybir.ActivationFunctionType
ALU = mybir.AluOpType

T = 1024
D = 1024
NT = 8
ALPHA = float(2.0 ** 0.25)
EPS = 1e-6
LN_EPS = 1e-5
NEG = -1e30
NPIECES = 218
SLOTS = 5
RAWS = 3
CW = 128 + 128 + 512 + 512 + 4 + 64


def constants():
    c = np.zeros((128, CW), np.float64)
    i = np.arange(128)
    c[:, 0:128] = np.eye(128)
    c[:, 128:256] = np.where(i[None, :] > i[:, None], NEG, 0.0)
    for h in range(4):
        lg = np.log(1.0 - 2.0 ** (-5.0 - h))
        diff = i[None, :] - i[:, None]
        c[:, 256 + 128 * h:384 + 128 * h] = np.where(diff >= 0, np.exp(lg * np.maximum(diff, 0)), 0.0) * 128 ** -0.5
        c[:, 768 + 128 * h:896 + 128 * h] = np.exp(lg * (i + 1.0))[None, :]
        c[:, 1280 + h] = np.exp(lg * (127.0 - i)) * 128 ** -0.5
    for g, win in enumerate((2, 4, 8, 16)):
        c[:, 1284 + 16 * g:1300 + 16 * g] = 1.0 / np.minimum(np.arange(16) + 1.0, win)
    b = np.zeros((128, 8, 256), np.float64)
    dist = (i[:, None] + 128) - np.arange(256)[None, :]
    for h in range(8):
        b[:, h, :] = np.where((dist >= 0) & (dist < 128), -(2.0 ** -(h + 1.0)) * dist, NEG)
    return c.astype(np.float32), b.reshape(128, 2048).astype(np.float32)


class Engine:

    def __init__(self, sem, e):
        self.sem, self.e, self.count, self.seen = sem, e, 0, {}

    def wait(self, *tokens):
        for t in tokens:
            if t is None:
                continue
            sem, value = t
            if self.seen.get(id(sem), 0) >= value:
                continue
            self.seen[id(sem)] = value
            if self.e is not None:
                self.e.wait_ge(sem, value)

    def do(self, f, *tokens):
        self.wait(*tokens)
        self.count += 1
        if self.e is not None:
            f(self.e).then_inc(self.sem, 1)
        return (self.sem, self.count)

    def run(self, f):
        if self.e is not None:
            f(self.e)

    def now(self):
        return (self.sem, self.count) if self.count else None


class Banks:
    def __init__(self, tensors):
        self.t, self.at, self.freed = tensors, 0, [None] * len(tensors)

    def take(self):
        b = self.at
        self.at = (self.at + 1) % len(self.t)
        return b, self.t[b], self.freed[b]

    def give(self, b, token):
        self.freed[b] = token


def interleave(main, side, ratio):
    live = [main, side]
    credit = 0.0
    while live:
        if main in live:
            credit += 1.0
            try:
                next(main)
            except StopIteration:
                live.remove(main)
        else:
            credit += 1e9
        while side in live and credit >= ratio:
            credit -= ratio
            try:
                next(side)
            except StopIteration:
                live.remove(side)
            if main not in live:
                credit = 1e9


def build(nc, wp, x_in, rows, small, cst, swab, poolw, wf, out, sg, cd):
    args = (wp, x_in, rows, small, cst, swab, poolw, wf, out, sg, cd)
    with ExitStack() as ctx:
        bank_t = [ctx.enter_context(nc.psum_tensor(f"bank{i}", [128, 512], F32)) for i in range(8)]
        block = ctx.enter_context(nc.Block())
        made, sems, said = {}, {}, []
        for reg, name in ((block.sync, "sp"), (block.scalar, "act"), (block.vector, "dve"), (block.gpsimd, "pool"),
                          (block.tensor, "pe")):
            @reg
            def _(e, name=name):
                said.append(program(nc, ctx, bank_t, made, sems, name, e, *args))
    assert all(d == said[0] for d in said)
    return said[0]


def program(nc, ctx, bank_t, made, sems, turn, engine, wp, x_in, rows, small, cst, swab, poolw, wf, out, sg, cd):
    base = (nc.sbuf_base + 31) // 32 * 32

    def at(name, kb, shape, dt=F32):
        if name not in made:
            made[name] = nc.alloc_sbuf_tensor_at(name, shape, dt, offset=base + int(kb * 1024))
        return made[name]

    def sem(name):
        if name not in sems:
            sems[name] = ctx.enter_context(nc.semaphore(name))
        return sems[name]

    banks = Banks(bank_t)
    pe, act, dve, pool, sp = (Engine(sem(f"s_{n}"), engine if n == turn else None) for n in ("pe", "act", "dve", "pool", "sp"))
    descs = []
    mark = {}

    XO, WO, RO, HO, CO, FO = 0, 32, 72, 84, 148, 149.375
    X = at("X", XO, [128, NT, D])
    whi = [at(f"whi{i}", WO + 4 * i, [128, 1024], F32R) for i in range(SLOTS)]
    wlo = [at(f"wlo{i}", WO + 20 + 4 * i, [128, 1024], F32R) for i in range(SLOTS)]
    raw = [at(f"raw{i}", RO + 4 * i, [128, 1024]) for i in range(RAWS)]
    ident = at("ident", CO, [128, 128])
    identb = at("identb", CO + 0.5, [128, 128], BF16)
    maskb = at("maskb", CO + 0.75, [128, 128], BF16)
    st = at("st", CO + 1, [128, 96])

    def H(name):
        return at(name + "hi", HO, [128, NT, T], F32R), at(name + "lo", HO + 32, [128, NT, T], F32R)

    def dma(dst, src, s, value, *tokens):
        sp.wait(*tokens)
        sp.run(lambda e: e.dma_start(dst, src).then_inc(s, 16))
        return (s, value)

    loads = {}

    def load(name, dst, src, *tokens):
        s = loads.setdefault(name, [sem("l_" + name), 0])
        s[1] += 16
        return dma(dst, src, s[0], s[1], *tokens)

    raw_sem = [sem(f"raw_{i}") for i in range(RAWS)]
    fetched, split_tok, slot_free = {}, {}, {}
    W = {"cur": 0, "split": 0}

    def fetch(n):
        if n >= NPIECES:
            return
        tokens = split_tok[n - RAWS] if n >= RAWS else ()
        fetched[n] = dma(raw[n % RAWS][:, :], wp[n], raw_sem[n % RAWS], 16 * (n // RAWS + 1), *tokens)

    def split(n):
        r, s = raw[n % RAWS], n % SLOTS
        a = act.do(lambda e: e.activation(whi[s][:, :], r[:, :], ACT.Copy), fetched[n], slot_free.get(n - SLOTS))
        b = dve.do(lambda e: e.tensor_tensor(out=wlo[s][:, :], in0=r[:, :], in1=whi[s][:, :].bitcast(F32),
                                             op=ALU.subtract), a)
        split_tok[n] = (a, b)
        fetch(n + RAWS)

    def ahead(limit):
        while W["split"] < min(limit, NPIECES):
            split(W["split"])
            W["split"] += 1

    def piece(*desc):
        n = W["cur"]
        W["cur"] += 1
        descs.append(desc)
        ahead(n + 1)
        pe.wait(*split_tok[n])
        return n

    def done(n, token):
        slot_free[n] = token
        ahead(n + SLOTS + 1)

    def hl(n):
        return whi[n % SLOTS], wlo[n % SLOTS]

    def mm3(out, sh, sl, mh, ml, first, last):
        pe.run(lambda e: e.matmul(out, sh, mh, start=first, stop=False))
        pe.run(lambda e: e.matmul(out, sh, ml, start=False, stop=False))
        f = lambda e: e.matmul(out, sl, mh, start=False, stop=last)
        if last:
            return pe.do(f)
        pe.run(f)

    def feature_major(name, col, hi, lo, evac):
        n = piece("F", name, col)
        wh, wl = hl(n)
        for half in range(2):
            b, P, free = banks.take()
            pe.wait(free)
            for k in range(8):
                tok = mm3(P[:, :], wh[:, 128 * k:128 * k + 128], wl[:, 128 * k:128 * k + 128],
                          hi[:, k, 512 * half:512 * half + 512], lo[:, k, 512 * half:512 * half + 512], k == 0, k == 7)
            banks.give(b, evac(half, P, tok))
            if half == 1:
                done(n, tok)
            yield

    def token_major(name, col, hi, lo, evac):
        ns = [piece("T", name, col, 0), piece("T", name, col, 4)]
        for t in range(NT):
            b, P, free = banks.take()
            pe.wait(free)
            for k in range(8):
                wh, wl = hl(ns[k // 4])
                c = 256 * (k % 4)
                tok = mm3(P[:, 0:256], hi[:, k, 128 * t:128 * t + 128], lo[:, k, 128 * t:128 * t + 128],
                          wh[:, c:c + 256], wl[:, c:c + 256], k == 0, k == 7)
            banks.give(b, evac(t, P, tok))
            if t % 4 == 3:
                if t == 7:
                    for n in ns:
                        done(n, tok)
                yield

    def rows_group(name, ks, stat, acc, first, after=None):
        mark["pre"] = pe.now()
        ns = [piece("D", name, k) for k in ks]
        for t in range(NT):
            for c in range(2):
                b, P, free = banks.take()
                pe.wait(free)
                for j, k in enumerate(ks):
                    wh, wl = hl(ns[j])
                    sh, sl = stat(k)
                    tok = mm3(P[:, :], sh[:, 128 * t:128 * t + 128], sl[:, 128 * t:128 * t + 128],
                              wh[:, 512 * c:512 * c + 512], wl[:, 512 * c:512 * c + 512], j == 0, j == len(ks) - 1)
                dst = acc[:, t, 512 * c:512 * c + 512]
                if first:
                    a = act.do(lambda e, dst=dst, P=P: e.activation(dst, P[:, :], ACT.Copy), tok)
                else:
                    a = dve.do(lambda e, dst=dst, P=P: e.tensor_tensor(out=dst, in0=P[:, :], in1=dst, op=ALU.add),
                               tok, act.now() if c == 0 and t == 0 else None, dve.now())
                banks.give(b, a)
            if t == 7:
                for n in ns:
                    done(n, tok)
            if after is not None:
                after(t, a)
            if t % 2:
                yield

    def run(gen):
        for _ in gen:
            pass

    def transpose_split(src, t, hi, lo, tokens, free=()):
        for q in range(2):
            b, P, f = banks.take()
            pe.wait(f, *tokens)
            for j in range(4):
                k = 4 * q + j
                g = lambda e, j=j, k=k, P=P: e.transpose(P[:, 128 * j:128 * j + 128], src[:, 128 * k:128 * k + 128], ident[:, :])
                if j == 3:
                    tok = pe.do(g)
                else:
                    pe.run(g)
            pv = P[:, :].rearrange("p (j c) -> p j c", j=4)
            oh = hi[:, 4 * q:4 * q + 4, 128 * t:128 * t + 128]
            ol = lo[:, 4 * q:4 * q + 4, 128 * t:128 * t + 128]
            a = act.do(lambda e, oh=oh, pv=pv: e.activation(oh, pv, ACT.Copy), tok, *free)
            d = dve.do(lambda e, oh=oh, ol=ol, pv=pv: e.tensor_tensor(out=ol, in0=pv, in1=oh.bitcast(F32), op=ALU.subtract), a)
            banks.give(b, d)
        return tok, (a, d)

    def rstd(src, dst, scale, eps, *tokens):
        a = dve.do(lambda e: e.tensor_scalar(dst, src, scale, eps, ALU.mult, ALU.add), *tokens)
        a = act.do(lambda e: e.activation(dst, dst, ACT.Sqrt), a)
        return dve.do(lambda e: e.reciprocal(dst, dst), a)

    fetch(0)
    xt = [load(f"x{t}", X[:, t, :], x_in[128 * t:128 * t + 128, :]) for t in range(2)]
    id_ok = load("id", ident[:, :], cst[:, 0:128])
    gb = at("gb0", FO, [128, 1024])
    gb_ok = load("row", gb[:, :], rows[0].partition_broadcast(128))
    fetch(1)
    fetch(2)
    xt += [load(f"x{t}", X[:, t, :], x_in[128 * t:128 * t + 128, :]) for t in range(2, NT)]
    junk = at("junk0", FO + 4, [128, 1024])
    ht = [at(f"ht0{i}", FO + 8 + 4 * i, [128, 1024]) for i in range(2)]
    hhi, hlo = H("h")
    read = [None, None]
    jt = None
    for t in range(NT):
        jt = act.do(lambda e, t=t: e.activation(junk[:, :], X[:, t, :], ACT.Square, accum_out=st[:, t:t + 1]), xt[t], jt)
        r = rstd(st[:, t:t + 1], st[:, 8 + t:9 + t], 1.0 / D, EPS, jt)
        s = dve.do(lambda e, t=t: e.scalar_tensor_tensor(ht[t % 2][:, :], X[:, t, :], st[:, 8 + t:9 + t], gb[:, :],
                                                         ALU.mult, ALU.mult), r, gb_ok, read[t % 2])
        read[t % 2], h_ok = transpose_split(ht[t % 2], t, hhi, hlo, (s, id_ok))
    pe.wait(*h_ok)
    x_free = s

    qs = at("qs", FO, [128, 4, T])
    ks = at("ks", FO + 16, [128, T])
    vs = at("vs", FO + 20, [128, NT, 128])
    sbias = at("sbias", FO + 24, [128, 8, 256])
    pt_ = [at(f"p{i}", FO + 32 + 8 * i, [128, 8, 256]) for i in range(2)]
    PT = [at(f"PT{i}", FO + 48 + 2 * i, [128, 512]) for i in range(4)]
    swa = at("swa", FO + 56, [128, 4, T])
    sig = [at(f"sig{i}", XO + 4 * i, [128, T]) for i in range(4)]
    vsT = at("vsT", XO + 16, [128, T])
    sb_ok = load("swab", sbias[:, :, :].rearrange("p h j -> p (h j)"), swab, read[0], read[1], pe.now(), dve.now())
    sink_ok = load("sink", st[:, 16:24], small["sinks"].partition_broadcast(128))

    def scaled_to(dst, scale, *tokens):
        def evac(half, P, tok):
            return act.do(lambda e: e.activation(dst[:, 512 * half:512 * half + 512], P[:, :], ACT.Copy, scale=scale), tok, *tokens)
        return evac

    for m in range(4):
        run(feature_major("q_s", m, hhi, hlo, scaled_to(qs[:, m, :], 0.125, pe.now(), dve.now())))
    run(feature_major("k_s", 0, hhi, hlo, scaled_to(ks, 1.0)))
    run(feature_major("v_s", 0, hhi, hlo, scaled_to(vsT, 1.0, x_free)))
    vs_in = act.now()
    for q in range(2):
        b, P, f = banks.take()
        pe.wait(f, vs_in)
        for j in range(4):
            t = 4 * q + j
            tok = pe.do(lambda e, j=j, t=t, P=P: e.transpose(P[:, 128 * j:128 * j + 128], vsT[:, 128 * t:128 * t + 128], ident[:, :]))
        vs_ok = dve.do(lambda e, q=q, P=P: e.tensor_copy(vs[:, 4 * q:4 * q + 4, :].rearrange("p a c -> p (a c)"), P[:, :]), tok)
        banks.give(b, vs_ok)

    sig_free = [None] * 4
    gate_ok = {}
    gcount = [0]

    def gate_evac(index):
        i = index % 4
        toks = []

        def evac(half, P, tok):
            v = sig[i][:, 512 * half:512 * half + 512]
            a = act.do(lambda e: e.activation(v, P[:, :], ACT.Tanh, scale=0.5), tok, sig_free[i], x_free)
            p = pool.do(lambda e: e.tensor_scalar(v, v, 0.5, 0.5, ALU.mult, ALU.add), a)
            toks.append(p)
            if half == 1:
                sig_free[i] = gate_ok[index] = load(f"sg{i}", sg[index], sig[i][:, :], *toks)
            return a
        return evac

    def gates(which):
        for index in which:
            yield from feature_major("gate_s" if index < 8 else "gate_r", index % 8, hhi, hlo, gate_evac(index))

    p_free = [None, None]
    PT_free = [None] * 4
    ptn = [0]

    def swa_scores(n):
        p = pt_[n % 2]
        j0 = 128 if n == 0 else 0
        last = None
        for mm in range(2):
            pair = [banks.take(), banks.take()]
            for m in range(2 * mm, 2 * mm + 2):
                for g in range(2):
                    b, P, f = pair[g]
                    pe.wait(f, qs_ok)
                    tok = pe.do(lambda e: e.matmul(
                        P[:, 256 * (m % 2) + j0:256 * (m % 2) + 256], qs[64 * g:64 * g + 64, m, 128 * n:128 * n + 128],
                        ks[64 * g:64 * g + 64, 128 * n - 128 + j0:128 * n + 128], start=True, stop=True))
            for g in range(2):
                b, P, f = pair[g]
                for m in range(2 * mm, 2 * mm + 2):
                    h = 4 * g + m
                    last = dve.do(lambda e: e.tensor_tensor_reduce(
                        out=p[:, h, j0:256], in0=P[:, 256 * (m % 2) + j0:256 * (m % 2) + 256], in1=sbias[:, h, j0:256], scale=1.0,
                        scalar=st[:, 16 + h:17 + h], op0=ALU.add, op1=ALU.max, accum_out=st[:, 24 + h:25 + h]),
                        tok, sb_ok, sink_ok, p_free[n % 2], swa_nm[0])
                banks.give(b, last)
        nm = dve.do(lambda e: e.tensor_scalar(st[:, 32:40], st[:, 24:32], -1.0, None, ALU.mult), last, act.now())
        sk = dve.do(lambda e: e.tensor_tensor(out=st[:, 40:48], in0=st[:, 16:24], in1=st[:, 24:32], op=ALU.subtract), last)
        swa_nm[0] = sk
        for h in range(8):
            ex = act.do(lambda e, h=h: e.activation(p[:, h, j0:256], p[:, h, j0:256], ACT.Exp, bias=st[:, 32 + h:33 + h],
                                                    accum_out=st[:, 48 + h:49 + h]), nm, swa_nm[1])
        es = act.do(lambda e: e.activation(st[:, 40:48], st[:, 40:48], ACT.Exp), sk)
        a = dve.do(lambda e: e.tensor_tensor(out=st[:, 48:56], in0=st[:, 48:56], in1=st[:, 40:48], op=ALU.add), ex, es)
        a = dve.do(lambda e: e.reciprocal(st[:, 48:56], st[:, 48:56]), a)
        for h in range(8):
            a2 = dve.do(lambda e, h=h: e.tensor_scalar(p[:, h, j0:256], p[:, h, j0:256], st[:, 48 + h:49 + h], None, ALU.mult), a)
        swa_nm[1] = a2
        return a2

    swa_nm = [None, None]
    qs_ok = act.now()

    def swa_values(n, ready):
        p = pt_[n % 2]
        jts = [1] if n == 0 else [0, 1]
        ob, O, of = banks.take()
        for g in range(2):
            for jt_ in jts:
                b, P, f = banks.take()
                pe.wait(f, ready)
                for r in range(4):
                    tok = pe.do(lambda e, r=r, P=P: e.transpose(P[:, 128 * r:128 * r + 128],
                                                                p[:, 4 * g + r, 128 * jt_:128 * jt_ + 128], ident[:, :]))
                i = ptn[0] % 4
                ptn[0] += 1
                a = act.do(lambda e, i=i, P=P: e.activation(PT[i][:, :], P[:, :], ACT.Copy), tok, PT_free[i])
                banks.give(b, a)
                pe.wait(a, of, vs_ok)
                PT_free[i] = pe.do(lambda e, i=i: e.matmul(O[64 * g:64 * g + 64, :], vs[:, n - 1 + jt_, 64 * g:64 * g + 64],
                                                           PT[i][:, :], start=jt_ == jts[0], stop=jt_ == 1))
        p_free[n % 2] = tok
        d = dve.do(lambda e: e.tensor_copy(swa[:, :, 128 * n:128 * n + 128], O[:, :].rearrange("p (r c) -> p r c", r=4)), PT_free[i])
        banks.give(ob, d)
        return d

    def swa_all():
        ready = swa_scores(0)
        yield
        for n in range(8):
            nxt = swa_scores(n + 1) if n < 7 else None
            yield
            swa_values(n, ready)
            ready = nxt
            yield

    interleave(gates(range(16)), swa_all(), 1.8)
    swa_ok = dve.now()
    swa_reads = (pe.now(), act.now(), dve.now())

    ret = at("ret", XO, [128, 8, T])
    rq = [at(f"rq{i}", FO + 4 * i, [128, T]) for i in range(2)]
    rk = [at(f"rk{i}", FO + 8 + 4 * i, [128, T]) for i in range(2)]
    rv = [at(f"rv{i}", FO + 16 + 8 * i, [128, NT, 256]) for i in range(2)]
    rg = at("rg", FO + 32, [128, 2, T])
    ro = at("ro", FO + 40, [128, NT, 256])
    dect = at("dect", FO + 48, [128, 1028])
    rs = [at(f"rs{i}", FO + 52.03125 + i, [128, 256]) for i in range(2)]
    ss = [at(f"ss{i}", FO + 54.03125 + 0.5 * i, [128, 128]) for i in range(2)]
    kd = at("kd", FO + 55.03125, [128, 128])
    rq2 = at("rq2", FO + 72, [128, 128])
    tb = at("tb", FO + 72.5, [128, 128])
    tab_ok = load("tab", dect[:, :], cst[:, 256:1284], *swa_reads)

    rfree = {"q": [None, None], "v": [None, None], "g": None, "o": None, "gs": None}
    rready = {}

    def ret_proj(h):
        i = h % 2
        run_ev = lambda dst, fr: scaled_to(dst, 1.0, fr, *swa_reads)
        yield from feature_major("q_r", h, hhi, hlo, run_ev(rq[i], rfree["q"][i]))
        yield from feature_major("k_r", h, hhi, hlo, run_ev(rk[i], rfree["q"][i]))

        def ev(t, P, tok):
            return act.do(lambda e: e.activation(rv[i][:, t, :], P[:, 0:256], ACT.Copy), tok, rfree["v"][i], *swa_reads)
        yield from token_major("v_r", 256 * h, hhi, hlo, ev)
        rready[h] = act.now()

    def ret_gate(h):
        for m in range(2):
            def ev(half, P, tok, m=m):
                v = rg[:, m, 512 * half:512 * half + 512]
                a = act.do(lambda e: e.activation(v, P[:, :], ACT.Tanh, scale=0.5), tok, rfree["g"], *swa_reads)
                a = pool.do(lambda e: e.tensor_scalar(v, v, 0.5, 0.5, ALU.mult, ALU.add), a)
                return dve.do(lambda e: e.tensor_tensor(out=v, in0=P[:, :], in1=v, op=ALU.mult), a)
            yield from feature_major("g_r", 2 * h + m, hhi, hlo, ev)
        rready["g"] = dve.now()

    def retention(h):
        i = h % 2
        gamma = 1.0 - 2.0 ** (-5.0 - h)
        decay = dect[:, 128 * h:128 * h + 128]
        qdec = dect[:, 512 + 128 * h:640 + 128 * h]
        kcol = dect[:, 1024 + h:1025 + h]
        qtmp = [rq2, tb]
        s_ok = rkv = None
        for n in range(8):
            c = slice(128 * n, 128 * n + 128)
            b, P, f = banks.take()
            pe.wait(f, rready[h])
            a = pe.do(lambda e: e.matmul(P[:, 0:128], rk[i][:, c], rq[i][:, c], start=True, stop=True))
            if n < 7:
                a = pe.do(lambda e: e.transpose(P[:, 128:256], rk[i][:, c], ident[:, :]))
            s1 = dve.do(lambda e: e.tensor_tensor(out=ss[n % 2][:, :], in0=P[:, 0:128], in1=decay, op=ALU.mult),
                        a, tab_ok, pe.now())
            if n > 0:
                q1 = dve.do(lambda e, n=n: e.tensor_tensor(out=qtmp[n % 2][:, :], in0=rq[i][:, c], in1=qdec, op=ALU.mult), s1)
            if n < 7:
                k1 = act.do(lambda e: e.activation(kd[:, :], P[:, 128:256], ACT.Copy, scale=kcol), a, s1, tab_ok, rkv)
                banks.give(b, k1)
            else:
                banks.give(b, s1)
            yield
            b, P, f = banks.take()
            pe.wait(f, s1)
            o = pe.do(lambda e, P=P: e.matmul(P[:, 0:256], ss[n % 2][:, :], rv[i][:, n, :], start=True, stop=n == 0))
            if n > 0:
                pe.wait(q1, s_ok)
                o = pe.do(lambda e, P=P: e.matmul(P[:, 0:256], qtmp[n % 2][:, :], rs[(n - 1) % 2][:, :], start=False, stop=True))
            if n < 7:
                b2, P2, f2 = banks.take()
                pe.wait(f2, k1)
                rkv = pe.do(lambda e, P2=P2: e.matmul(P2[:, 0:256], kd[:, :], rv[i][:, n, :], start=True, stop=True))
                if n == 0:
                    s_ok = dve.do(lambda e, P2=P2: e.tensor_copy(rs[0][:, :], P2[:, 0:256]), rkv)
                else:
                    s_ok = dve.do(lambda e, P2=P2: e.scalar_tensor_tensor(
                        rs[n % 2][:, :], rs[(n - 1) % 2][:, :], float(gamma ** 128), P2[:, 0:256], ALU.mult, ALU.add), rkv, s_ok)
                banks.give(b2, s_ok)
            a = act.do(lambda e, P=P: e.activation(ro[:, n, :], P[:, 0:256], ACT.Copy), o, rfree["o"])
            banks.give(b, a)
            bn = dve.do(lambda e: e.bn_stats(st[:, 24:30], ro[:, n, :]), a, dve.now())
            bn = dve.do(lambda e: e.bn_aggr(st[:, 32 + 2 * n:34 + 2 * n], st[:, 24:30]), bn)
            yield
        rfree["q"][i] = rfree["v"][i] = pe.now()
        mv = st[:, 32:48].rearrange("p (n two) -> p n two", two=2)
        r = rstd(mv[:, :, 1], st[:, 48:56], 1.0, EPS, bn)
        for n in range(8):
            d = dve.do(lambda e, n=n: e.tensor_scalar(ro[:, n, :], ro[:, n, :], st[:, 32 + 2 * n:33 + 2 * n],
                                                      st[:, 48 + n:49 + n], ALU.subtract, ALU.mult), r)
        yield
        for m in range(2):
            for q in range(2):
                b, P, f = banks.take()
                pe.wait(f, d)
                for j in range(4):
                    a = pe.do(lambda e, j=j, P=P: e.transpose(P[:, 128 * j:128 * j + 128],
                                                              ro[:, 4 * q + j, 128 * m:128 * m + 128], ident[:, :]))
                w = dve.do(lambda e, P=P: e.tensor_tensor(out=ret[:, 2 * h + m, 512 * q:512 * q + 512], in0=P[:, :],
                                                          in1=rg[:, m, 512 * q:512 * q + 512], op=ALU.mult),
                           a, rready["g"], *sig_free)
                banks.give(b, w)
            yield
        rfree["o"] = a
        rfree["g"] = w

    run(ret_proj(0))
    for h in range(4):
        def main(h=h):
            yield from ret_gate(h)
            if h < 3:
                yield from ret_proj(h + 1)
        interleave(main(), retention(h), 0.5)
    ret_ok = dve.now()

    h_dead = pe.now()
    rethi = at("rethi", HO, [128, 8, T], F32R)
    swahi = at("swahi", HO + 32, [128, 4, T], F32R)
    retlo = at("retlo", XO, [128, 8, T], F32R)
    swalo = at("swalo", FO + 56, [128, 4, T], F32R)
    Z = at("Z", FO, [128, 8, T])
    mlo = at("mlo", FO, [128, 8, T], F32R)
    gs = [at(f"gs{i}", FO + 32 + 4 * i, [128, T]) for i in range(4)]
    mp = [at("mp0", HO + 48, [128, 2, T], F32R), at("mp1", HO + 56, [128, 2, T], F32R),
          at("mp2", HO + 32, [128, 2, T], F32R), at("mp3", FO + 48, [128, 2, T], F32R)]
    gs_free = [None] * 4
    gl = {}
    F_free = (pe.now(), act.now(), dve.now())

    def fetch_gate(n):
        if n < 16:
            gl[n] = load(f"gl{n % 4}", gs[n % 4][:, :], sg[n], gate_ok[n], gs_free[n % 4], *F_free)

    for n in range(4):
        fetch_gate(n)
    sw_ok = {}
    for m in range(4):
        a = act.do(lambda e, m=m: e.activation(swahi[:, m, :], swa[:, m, :], ACT.Copy), h_dead, swa_ok)
        sw_ok[m] = dve.do(lambda e, m=m: e.tensor_tensor(out=swalo[:, m, :], in0=swa[:, m, :], in1=swahi[:, m, :].bitcast(F32),
                                                         op=ALU.subtract), a)
    rt_ok = {}

    def split_ret(m):
        a = act.do(lambda e, m=m: e.activation(rethi[:, m, :], ret[:, m, :], ACT.Copy), h_dead, ret_ok)
        rt_ok[m] = dve.do(lambda e, m=m: e.tensor_tensor(out=retlo[:, m, :], in0=ret[:, m, :], in1=rethi[:, m, :].bitcast(F32),
                                                         op=ALU.subtract), a)
    for m2 in range(4):
        n = piece("S", "w_swa_out", m2)
        wh, wl = hl(n)
        for mm in range(2):
            m = 2 * m2 + mm
            for half in range(2):
                c = slice(512 * half, 512 * half + 512)
                b, P, f = banks.take()
                pe.wait(f)
                for k in range(4):
                    pe.wait(sw_ok[k])
                    w0 = 512 * mm + 128 * k
                    tok = mm3(P[:, :], wh[:, w0:w0 + 128], wl[:, w0:w0 + 128], swahi[:, k, c], swalo[:, k, c], k == 0, k == 3)
                z = dve.do(lambda e, P=P, c=c, m=m: e.tensor_tensor(out=Z[:, m, c], in0=P[:, :], in1=gs[m % 4][:, c], op=ALU.mult),
                           tok, gl[m], *F_free)
                banks.give(b, z)
            gs_free[m % 4] = z
            fetch_gate(m + 4)
            split_ret(m)
        done(n, tok)
    swa_dead = pe.now()
    m_ok = {}
    tmpz = gs
    for m in range(8):
        n = piece("F", "w_ret_out", m)
        wh, wl = hl(n)
        for half in range(2):
            c = slice(512 * half, 512 * half + 512)
            b, P, f = banks.take()
            pe.wait(f)
            for k in range(8):
                pe.wait(rt_ok[k])
                tok = mm3(P[:, :], wh[:, 128 * k:128 * k + 128], wl[:, 128 * k:128 * k + 128], rethi[:, k, c], retlo[:, k, c],
                          k == 0, k == 7)
            g = gs[m % 4]
            z = dve.do(lambda e, P=P, c=c, g=g: e.tensor_tensor(out=g[:, c], in0=P[:, :], in1=g[:, c], op=ALU.mult), tok, gl[8 + m])
            banks.give(b, z)
            z = pool.do(lambda e, c=c, m=m, g=g: e.tensor_tensor(out=Z[:, m, c], in0=Z[:, m, c], in1=g[:, c], op=ALU.add), z)
            hi_ = mp[m // 2][:, m % 2, c]
            a = act.do(lambda e, hi_=hi_, c=c, m=m: e.activation(hi_, Z[:, m, c], ACT.Copy), z, swa_dead)
            m_ok[m] = dve.do(lambda e, hi_=hi_, c=c, m=m: e.tensor_tensor(out=mlo[:, m, c], in0=Z[:, m, c], in1=hi_.bitcast(F32),
                                                                          op=ALU.subtract), a)
        done(n, tok)
        gs_free[m % 4] = z
        fetch_gate(8 + m + 4)
    ret_dead = pe.now()

    acc = at("accX", XO, [128, NT, D])
    xs = [at(f"xs{i}", FO + 32 + 4 * i, [128, D]) for i in range(4)]
    g1 = at("g1", FO + 56, [128, D])
    g2 = at("g2", FO + 60, [128, D])
    hj = at("hj", FO + 64, [128, D])
    hs = at("hs", FO + 68, [128, D])
    row_ok = load("row", g1[:, :], rows[1].partition_broadcast(128), swa_dead, ret_dead, pool.now(), dve.now())
    row_ok = load("row", g2[:, :], rows[2].partition_broadcast(128))
    xs_free = [(pool.now(), dve.now())] * 4
    xl = {}

    def fetch_x(t):
        if t < NT:
            xl[t] = load(f"xl{t % 4}", xs[t % 4][:, :], x_in[128 * t:128 * t + 128, :], *xs_free[t % 4])

    for t in range(4):
        fetch_x(t)
    hhi2, hlo2 = H("h2")
    st_free = {"j": None, "h": None}

    def mix_after(t, tok):
        a = act.do(lambda e: e.activation(hj[:, :], acc[:, t, :], ACT.Square, accum_out=st[:, 0:1]), tok, st_free["j"], swa_dead, dve.now())
        r = rstd(st[:, 0:1], st[:, 1:2], 1.0 / D, EPS, a)
        d = dve.do(lambda e: e.scalar_tensor_tensor(acc[:, t, :], acc[:, t, :], st[:, 1:2], g1[:, :], ALU.mult, ALU.mult), r, row_ok)
        d = pool.do(lambda e: e.tensor_tensor(out=acc[:, t, :], in0=acc[:, t, :], in1=xs[t % 4][:, :], op=ALU.add), d, xl[t])
        xs_free[t % 4] = (d,)
        fetch_x(t + 4)
        a = act.do(lambda e: e.activation(hj[:, :], acc[:, t, :], ACT.Square, accum_out=st[:, 2:3]), d)
        st_free["j"] = a
        r = rstd(st[:, 2:3], st[:, 3:4], 1.0 / D, EPS, a)
        d = dve.do(lambda e: e.scalar_tensor_tensor(hs[:, :], acc[:, t, :], st[:, 3:4], g2[:, :], ALU.mult, ALU.mult), r, st_free["h"])
        st_free["h"], st_free["w"] = transpose_split(hs, t, hhi2, hlo2, (d,), (x_dead[0],))

    x_dead = [None]
    for g in range(4):
        if g == 3:
            x_dead[0] = pe.now()
        run(rows_group("w_out", [2 * g, 2 * g + 1], lambda k: (mp[k // 2][:, k % 2, :], mlo[:, k, :]), acc, g == 0,
                       mix_after if g == 3 else None))

    def mlp(up, down, hi, lo, acc, first_copy, after, free, tag):
        uh = [at(f"uh{tag}{i}", FO + 8 * i, [128, 2, T], F32R) for i in range(2)]
        ul = [at(f"ul{tag}{i}", FO + 16 + 8 * i, [128, 2, T], F32R) for i in range(2)]
        rr = [at(f"rr{tag}{i}", FO + RR + 2 * i, [128, 512]) for i in range(2)]
        uu = [at(f"uu{tag}{i}", FO + RR + 4 + 2 * i, [128, 512]) for i in range(2)]
        u_ok, u_free, count = {}, {}, [0]
        lastd = [None, None]

        def up_group(G):
            for m in range(2):
                def evac(half, P, tok, m=m):
                    i = count[0] % 2
                    count[0] += 1
                    c = slice(512 * half, 512 * half + 512)
                    a = act.do(lambda e: e.activation(rr[i][:, :], P[:, :], ACT.Relu), tok, lastd[i], *free)
                    p = pool.do(lambda e: e.tensor_tensor(out=uu[i][:, :], in0=rr[i][:, :], in1=rr[i][:, :], op=ALU.mult), a, lastd[i])
                    b = act.do(lambda e: e.activation(uh[G % 2][:, m, c], rr[i][:, :], ACT.Square), a, u_free.get(G - 2))
                    lastd[i] = dve.do(lambda e: e.tensor_tensor(out=ul[G % 2][:, m, c], in0=uu[i][:, :],
                                                                in1=uh[G % 2][:, m, c].bitcast(F32), op=ALU.subtract), p, b)
                    return a
                yield from feature_major(up, 2 * G + m, hi, lo, evac)
            u_ok[G] = dve.now()

        def down_group(G):
            pe.wait(u_ok[G])
            yield from rows_group(down, [2 * G, 2 * G + 1], lambda k: (uh[G % 2][:, k % 2, :], ul[G % 2][:, k % 2, :]), acc,
                                  first_copy and G == 0, after if G == 15 else None)
            u_free[G] = pe.now()

        run(up_group(0))
        for G in range(16):
            if G < 15:
                run(up_group(G + 1))
            run(down_group(G))

    RR = 64
    pe.wait(*st_free["w"])
    acc2 = at("acc2", FO + 32, [128, NT, D])
    ya = at("ya", FO, [128, D])
    yj = at("yj", FO + 4, [128, D])
    g3 = at("g3", FO + 16, [128, D])
    yhi, ylo = H("y")
    y_st = {"j": None, "w": None, "x": None}

    def mlp1_after(t, tok):
        if t == 0:
            y_st["row"] = load("row", g3[:, :], rows[3].partition_broadcast(128), mark["pre"])
            y_st["h"] = mark["pre"]
        a = act.do(lambda e: e.activation(yj[:, :], acc2[:, t, :], ACT.Square, accum_out=st[:, 0:1]), tok, y_st["j"], y_st["h"], dve.now())
        y_st["j"] = a
        r = rstd(st[:, 0:1], st[:, 1:2], 1.0 / D, EPS, a)
        d = dve.do(lambda e: e.scalar_tensor_tensor(acc2[:, t, :], acc2[:, t, :], st[:, 1:2], g3[:, :], ALU.mult, ALU.mult), r, y_st["row"])
        d = pool.do(lambda e: e.tensor_tensor(out=acc[:, t, :], in0=acc[:, t, :], in1=acc2[:, t, :], op=ALU.add), d)
        y_st["r"], y_st["w"] = transpose_split(acc[:, t, :], t, yhi, ylo, (d,), (y_st["h"],))
        y_st["x"] = act.do(lambda e: e.activation(acc[:, t, :], acc[:, t, :], ACT.Copy, scale=ALPHA), y_st["r"], y_st["x"])

    free1 = (pe.now(), act.now(), dve.now(), pool.now())
    mlp("w_up", "w_down", hhi2, hlo2, acc2, True, mlp1_after, free1, "a")
    pe.wait(*y_st["w"])

    q2 = at("q2", FO, [128, 4, T])
    k2 = at("k2", FO + 16, [128, 4, T])
    v2 = at("v2", FO + 32, [128, NT, 512])
    u2 = at("u2", FO + 48, [128, 4, T])
    cc = at("cc", FO + 64, [8, T])
    ce = at("ce", FO + 68, [8, T])
    wfr = at("wfr", FO + 72, [128, 64])
    wfh = at("wfh", FO + 72.25, [128, 64], F32R)
    wfl = at("wfl", FO + 72.5, [128, 64], F32R)
    freeF = (pe.now(), act.now(), dve.now(), pool.now())
    wf_ok = load("wf", wfr[:, :], wf, *freeF)
    bf_ok = load("bf", st[0:8, 94:95], small["b_f"])
    ps_ok = load("ps", st[:, 88:92], small["pool_scale"])
    rm = at("rmask", FO + 48, [128, 128])
    mk_ok = load("mask", rm[:, :], cst[:, 128:256], *freeF)
    a = dve.do(lambda e: e.tensor_copy(maskb[:, :], rm[:, :]), mk_ok)
    mask_ok = dve.do(lambda e: e.tensor_copy(identb[:, :], ident[:, :]), a)
    a = act.do(lambda e: e.activation(wfh[:, :], wfr[:, :], ACT.Copy), wf_ok)
    wfs = dve.do(lambda e: e.tensor_tensor(out=wfl[:, :], in0=wfr[:, :], in1=wfh[:, :].bitcast(F32), op=ALU.subtract), a)

    for half in range(2):
        c = slice(512 * half, 512 * half + 512)
        b, P, f = banks.take()
        pe.wait(f, wfs)
        for k in range(8):
            tok = mm3(P[0:8, :], wfh[:, 8 * k:8 * k + 8], wfl[:, 8 * k:8 * k + 8], yhi[:, k, c], ylo[:, k, c], k == 0, k == 7)
        a = act.do(lambda e, P=P, c=c: e.activation(cc[:, c], P[0:8, :], ACT.Identity, bias=st[0:8, 94:95]), tok, bf_ok, *freeF)
        banks.give(b, a)
    a1 = act.do(lambda e: e.activation(ce[:, :], cc[:, :], ACT.Abs), a)
    a2 = act.do(lambda e: e.activation(ce[:, :], ce[:, :], ACT.Exp, scale=-1.0), a1)
    a2 = act.do(lambda e: e.activation(ce[:, :], ce[:, :], ACT.Ln, bias=1.0), a2)
    d = dve.do(lambda e: e.tensor_scalar(cc[:, :], cc[:, :], 0.0, None, ALU.min), a1)
    d = dve.do(lambda e: e.tensor_tensor(out=ce[:, :], in0=cc[:, :], in1=ce[:, :], op=ALU.subtract), d, a2)
    one = dve.do(lambda e: e.memset(cc[:, :], 1.0), d)
    d = dve.do(lambda e: e.tensor_tensor_scan(cc[:, :], cc[:, :], ce[:, :], 0.0, ALU.mult, ALU.add), one)
    n_ = dve.do(lambda e: e.tensor_scalar(ce[:, :], cc[:, :], -1.0, None, ALU.mult), d)
    c_st = load("cst_", cd, ce[:, :], n_)
    cT = at("cT", FO + 72.75, [128, 64])

    run(feature_major("u_2", 0, yhi, ylo, scaled_to(u2[:, 0, :], 1.0, *freeF)))
    b, P, f = banks.take()
    pe.wait(f, d)
    for t in range(NT):
        tok = pe.do(lambda e, t=t, P=P: e.transpose(P[:, 8 * t:8 * t + 8], cc[:, 128 * t:128 * t + 128], ident[0:8, 0:8]))
    cT_ok = dve.do(lambda e, P=P: e.tensor_copy(cT[:, :], P[:, 0:64]), tok)
    banks.give(b, cT_ok)
    for m in range(1, 4):
        run(feature_major("u_2", m, yhi, ylo, scaled_to(u2[:, m, :], 1.0, *freeF)))
    u_in = act.now()
    for vh in range(2):
        def ev(t, P, tok, vh=vh):
            return act.do(lambda e: e.activation(v2[:, t, 256 * vh:256 * vh + 256], P[:, 0:256], ACT.Copy), tok, *freeF)
        run(token_major("v_2", 256 * vh, yhi, ylo, ev))
    for m in range(4):
        run(feature_major("q_2", m, yhi, ylo, scaled_to(q2[:, m, :], 0.125, *freeF)))
        run(feature_major("k_2", m, yhi, ylo, scaled_to(k2[:, m, :], 1.0, *freeF)))
    qkv_ok = act.now()
    y_dead = pe.now()

    chi = [at(f"chi{k}", HO + 4 * k, [128, T], F32R) for k in range(6)] + \
          [at("chi6", FO + 16, [128, T], F32R), at("chi7", FO + 24, [128, T], F32R)]
    clo = [at(f"clo{k}", HO + 32 + 4 * k, [128, T], F32R) for k in range(6)] + \
          [at("clo6", FO + 20, [128, T], F32R), at("clo7", FO + 8, [128, T], F32R)]
    pA = at("pA", HO + 24, [128, T])
    pB = at("pB", HO + 28, [128, T])
    pw = at("pw", HO + 20, [128, 4, 128])
    pr = at("pr", HO + 22, [128, 64])
    pw_ok = load("pw", pw[:, :, :], poolw, y_dead)
    pr_ok = load("pr", pr[:, :], cst[:, 1284:1348], y_dead)
    pool_read = None
    cat_ok = {}

    def pool_mixer():
        nonlocal pool_read
        for g, win in enumerate((2, 4, 8, 16)):
            src, width = u2[:, g, :], 1
            bufs = [pA, pB]
            tok = y_dead
            i = 0
            while width < win:
                dst = bufs[i % 2]
                a = pool.do(lambda e, dst=dst, src=src, w=width: e.tensor_tensor(out=dst[:, w:], in0=src[:, w:], in1=src[:, :T - w], op=ALU.add),
                            tok, u_in, pool_read)
                tok = pool.do(lambda e, dst=dst, src=src, w=width: e.tensor_copy(dst[:, 0:w], src[:, 0:w]), a)
                src = dst
                width *= 2
                i += 1
            a = dve.do(lambda e, src=src, g=g: e.tensor_tensor(out=src[:, 0:16], in0=src[:, 0:16], in1=pr[:, 16 * g:16 * g + 16], op=ALU.mult), tok, pr_ok)
            a = dve.do(lambda e, src=src, g=g: e.tensor_tensor(out=src[:, 0:16], in0=src[:, 0:16], in1=u2[:, g, 0:16], op=ALU.subtract), a)
            a = dve.do(lambda e, src=src, g=g, win=win: e.scalar_tensor_tensor(src[:, 16:], src[:, 16:], 1.0 / win, u2[:, g, 16:],
                                                                               ALU.mult, ALU.subtract), a)
            for half in range(2):
                c = slice(512 * half, 512 * half + 512)
                b, P, f = banks.take()
                pe.wait(f, a, pw_ok)
                tok = pe.do(lambda e, P=P, src=src, c=c, g=g: e.matmul(P[:, :], pw[:, g, :], src[:, c], start=True, stop=True))
                s = st[:, 88 + g:89 + g]
                h_ = act.do(lambda e, P=P, c=c, g=g, s=s: e.activation(chi[g][:, c], P[:, :], ACT.Copy, scale=s), tok, ps_ok, y_dead)
                l_ = dve.do(lambda e, P=P, c=c, g=g, s=s: e.scalar_tensor_tensor(clo[g][:, c], P[:, :], s, chi[g][:, c].bitcast(F32),
                                                                                 ALU.mult, ALU.subtract), h_)
                banks.give(b, l_)
            pool_read = tok
            cat_ok[g] = l_
            yield

    nb = [at(f"nb{i}", FO + 64 + 4 * i, [128, T]) for i in range(2)]
    sx = [at(f"sx{i}", FO + 48 + 4 * i, [128, T]) for i in range(3)]
    P2 = [at(f"P2{i}", FO + 60 + 2 * i, [128, 512]) for i in range(2)]
    ao = [at("ao0", HO + 56, [128, NT, 128]), at("ao1", HO + 60, [128, NT, 128]),
          at("ao2", FO, [128, NT, 128]), at("ao3", FO + 4, [128, NT, 128])]
    run(pool_mixer())
    s_free = [None] * 3
    P2_free = [None] * 2
    nb_ok, nb_free = {}, [None, None]
    scratch_ok = (pe.now(), act.now(), dve.now(), pool.now())

    def fetch_nb(h):
        if h < 8:
            nb_ok[h] = load(f"nb{h % 2}", nb[h % 2][:, :], cd[h].partition_broadcast(128), c_st, nb_free[h % 2], cT_ok, *scratch_ok)

    fetch_nb(0)
    fetch_nb(1)
    pcount = [0]
    items = [(h, i) for h in range(8) for i in range(8)]

    def scores(idx):
        h, i = items[idx]
        s = sx[idx % 3]
        g = slice(64 * (h % 2), 64 * (h % 2) + 64)
        nk = 128 * (i + 1)
        mcol = 4 * (idx % 3)
        prev = NEG
        for c0 in range(0, nk, 512):
            w = min(512, nk - c0)
            diag = c0 + w == nk
            b, P, f = banks.take()
            pe.wait(f, qkv_ok, mask_ok)
            mmf = lambda e, P=P, c0=c0, w=w, diag=diag: e.matmul(P[:, 0:w], q2[g, h // 2, 128 * i:128 * i + 128], k2[g, h // 2, c0:c0 + w],
                                                                start=True, stop=not diag)
            if diag:
                pe.run(mmf)
                tok = pe.do(lambda e, P=P, w=w: e.matmul(P[:, w - 128:w], identb[:, :], maskb[:, :], start=False, stop=True))
            else:
                tok = pe.do(mmf)
            mo = st[:, 24 + mcol + c0 // 512:25 + mcol + c0 // 512]
            last = dve.do(lambda e, P=P, c0=c0, w=w, prev=prev, mo=mo: e.tensor_tensor_reduce(
                out=s[:, c0:c0 + w], in0=P[:, 0:w], in1=nb[h % 2][:, c0:c0 + w], scale=1.0, scalar=prev, op0=ALU.add,
                op1=ALU.max, accum_out=mo), tok, nb_ok[h], s_free[idx % 3], dve.now(), *scratch_ok)
            banks.give(b, last)
            prev = mo
        if i == 7:
            nb_free[h % 2] = last
            fetch_nb(h + 2)
        cq = cT[:, 8 * i + h:8 * i + h + 1]
        nm = st[:, 26 + mcol:27 + mcol]
        ls = st[:, 27 + mcol:28 + mcol]
        d = dve.do(lambda e: e.scalar_tensor_tensor(nm, prev, cq, cq, ALU.add, ALU.subtract, reverse1=True), last, cT_ok)
        a = act.do(lambda e: e.activation(s[:, 0:nk], s[:, 0:nk], ACT.Exp, bias=nm, accum_out=ls), d)
        d = dve.do(lambda e: e.reciprocal(ls, ls), a)
        return a, d

    def transposed(idx, ready):
        h, i = items[idx]
        s = sx[idx % 3]
        out_ = []
        for q in range(0, i + 1, 4):
            n = min(4, i + 1 - q)
            b, P, f = banks.take()
            pe.wait(f, ready)
            for j in range(n):
                tok = pe.do(lambda e, j=j, P=P, q=q: e.transpose(P[:, 128 * j:128 * j + 128], s[:, 128 * (q + j):128 * (q + j) + 128], ident[:, :]))
            p = pcount[0] % 2
            pcount[0] += 1
            eng = act if p else dve
            if eng is act:
                a = act.do(lambda e, P=P, p=p, n=n: e.activation(P2[p][:, 0:128 * n], P[:, 0:128 * n], ACT.Copy), tok, P2_free[p])
            else:
                a = dve.do(lambda e, P=P, p=p, n=n: e.tensor_copy(P2[p][:, 0:128 * n], P[:, 0:128 * n]), tok, P2_free[p])
            banks.give(b, a)
            out_.append((q, n, p, a))
        s_free[idx % 3] = tok
        return out_

    def values(idx, parts, rl):
        h, i = items[idx]
        b, P, f = banks.take()
        pe.wait(f)
        for q, n, p, a in parts:
            pe.wait(a)
            for j in range(n):
                k = q + j
                tok = pe.do(lambda e, k=k, j=j, p=p, P=P: e.matmul(P[:, 0:64], P2[p][:, 128 * j:128 * j + 128],
                                                                   v2[:, k, 64 * h:64 * h + 64], start=k == 0, stop=k == i))
            P2_free[p] = tok
        ls = st[:, 27 + 4 * (idx % 3):28 + 4 * (idx % 3)]
        o = ao[h // 2][:, i, 64 * (h % 2):64 * (h % 2) + 64]
        d = dve.do(lambda e, P=P: e.tensor_scalar(o, P[:, 0:64], ls, None, ALU.mult), tok, rl, q_dead.get(h // 2))
        banks.give(b, d)
        return d

    q_dead = {}

    def pair_out(t, tok):
        for q in range(2):
            b, P, f = banks.take()
            pe.wait(f, tok)
            for j in range(4):
                a = pe.do(lambda e, j=j, P=P, q=q: e.transpose(P[:, 128 * j:128 * j + 128], ao[t][:, 4 * q + j, :], ident[:, :]))
            c = slice(512 * q, 512 * q + 512)
            h_ = act.do(lambda e, P=P, c=c: e.activation(chi[4 + t][:, c], P[:, :], ACT.Copy), a, *scratch_ok)
            l_ = dve.do(lambda e, P=P, c=c: e.tensor_tensor(out=clo[4 + t][:, c], in0=P[:, :], in1=chi[4 + t][:, c].bitcast(F32),
                                                            op=ALU.subtract), h_)
            banks.give(b, l_)
        cat_ok[4 + t] = l_

    ready = scores(0)
    nxt = scores(1)
    for idx in range(64):
        later = scores(idx + 2) if idx + 2 < 64 else None
        parts = transposed(idx, ready[0])
        tok = values(idx, parts, ready[1])
        ready, nxt = nxt, later
        h, i = items[idx]
        if i == 7 and h % 2:
            q_dead[h // 2 + 2] = pe.now()
            pair_out(h // 2, tok)

    h2hi, h2lo = H("z")
    lg = at("lg", FO + 48, [128, D])
    lb = at("lb", FO + 52, [128, D])
    lx = [at(f"lx{i}", FO + 56 + 4 * i, [128, D]) for i in range(2)]
    a_dead = (pe.now(), act.now(), dve.now())
    row_ok = load("row", lg[:, :], rows[4].partition_broadcast(128), *a_dead)
    row_ok = load("row", lb[:, :], rows[5].partition_broadcast(128))
    ln = {"r": [None, None], "w": None, "x": None}

    def layer_norm(t, tok, dst, gain, bias, row):
        d = tok
        for c in range(2):
            d = dve.do(lambda e, c=c: e.bn_stats(st[:, 24 + 6 * c:30 + 6 * c], acc[:, t, 512 * c:512 * c + 512]), d, dve.now())
        d = dve.do(lambda e: e.bn_aggr(st[:, 36:38], st[:, 24:36]), d)
        r = rstd(st[:, 37:38], st[:, 38:39], 1.0, LN_EPS, d)
        d = dve.do(lambda e: e.tensor_scalar(dst, acc[:, t, :], st[:, 36:37], st[:, 38:39], ALU.subtract, ALU.mult), r)
        d = pool.do(lambda e: e.tensor_tensor(out=dst, in0=dst, in1=gain[:, :], op=ALU.mult), d, row)
        return pool.do(lambda e: e.tensor_tensor(out=dst, in0=dst, in1=bias[:, :], op=ALU.add), d)

    def ln1_after(t, tok):
        x_ = lx[t % 2]
        dve.wait(ln["r"][t % 2], ln["x"])
        d = layer_norm(t, tok, x_[:, :], lg, lb, row_ok)
        r, ln["w"] = transpose_split(x_, t, h2hi, h2lo, (d,), (mark["pre"],))
        ln["r"][t % 2] = r
        ln["x"] = act.do(lambda e: e.activation(acc[:, t, :], x_[:, :], ACT.Copy, scale=ALPHA), d)

    for g in range(4):
        pe.wait(cat_ok[2 * g], cat_ok[2 * g + 1])
        run(rows_group("w_out_2", [2 * g, 2 * g + 1], lambda k: (chi[k], clo[k]), acc, False, ln1_after if g == 3 else None))
    pe.wait(*ln["w"])

    fg = at("fg", FO + 32, [128, D])
    fb = at("fb", FO + 36, [128, D])
    frow = load("row", fg[:, :], rows[6].partition_broadcast(128), *a_dead)
    frow = load("row", fb[:, :], rows[7].partition_broadcast(128))
    outs = []

    def ln2_after(t, tok):
        d = layer_norm(t, tok, acc[:, t, :], fg, fb, frow)
        outs.append(load("out", out[128 * t:128 * t + 128, :], acc[:, t, :], d))

    free2 = (pe.now(), act.now(), dve.now(), pool.now())
    mlp("w_mlp1", "w_mlp2", h2hi, h2lo, acc, False, ln2_after, free2, "b")
    sp.wait(outs[-1])
    assert W["cur"] == NPIECES, W["cur"]

    return descs


def pack(inputs, descs):
    cuts = {}
    edge = np.cumsum([0, 512, 512, 1024, 1024, 512, 128, 128, 1024, 1024])
    w_in = inputs["w_in"][0]
    for name, a, b in zip(("q_r", "k_r", "v_r", "g_r", "q_s", "k_s", "v_s", "gate_r", "gate_s"), edge[:-1], edge[1:]):
        cuts[name] = w_in[:, a:b]
    heads = [h for m in range(4) for h in (m, 4 + m)]
    cuts["q_s"] = cuts["q_s"].reshape(1024, 8, 64)[:, heads].reshape(1024, 512)
    cuts["w_swa_out"] = inputs["w_swa_out"][0].reshape(8, 64, 1024)[heads].reshape(512, 1024)
    w2 = inputs["w_in_2"][0]
    for i, name in enumerate(("u_2", "q_2", "k_2", "v_2")):
        cuts[name] = w2[:, 512 * i:512 * i + 512]
    for name, key in (("w_ret_out",) * 2, ("w_out",) * 2, ("w_up",) * 2, ("w_down",) * 2, ("w_out_2",) * 2,
                      ("w_mlp1", "w_mlp1_2"), ("w_mlp2", "w_mlp2_2")):
        cuts[name] = inputs[key][0]
    wp = np.empty((len(descs), 128, 1024), np.float32)
    for n, d in enumerate(descs):
        w = cuts[d[1]]
        if d[0] == "F":
            wp[n].reshape(128, 8, 128)[:] = w[:, 128 * d[2]:128 * d[2] + 128].reshape(8, 128, 128).transpose(1, 0, 2)
        elif d[0] == "T":
            wp[n].reshape(128, 4, 256)[:] = w[128 * d[3]:128 * d[3] + 512, d[2]:d[2] + 256].reshape(4, 128, 256).transpose(1, 0, 2)
        elif d[0] == "D":
            wp[n] = w[128 * d[2]:128 * d[2] + 128]
        else:
            wp[n].reshape(128, 2, 4, 128)[:] = w[:, 256 * d[2]:256 * d[2] + 256].reshape(4, 128, 2, 128).transpose(1, 2, 0, 3)
    return wp


def kernel(**inputs):
    import concourse.bacc as _bacc
    from concourse.bass_utils import run_bass_kernel_spmd as _run

    inputs = {k: np.asarray(v) for k, v in inputs.items()}
    nc = _bacc.Bacc("TRN2", target_bir_lowering=False, num_devices=1, dynamic_dma_scratch_size=1024)
    cst, swab = constants()
    arrays = {
        "x_d": np.ascontiguousarray(inputs["x"][0]),
        "rows_d": np.concatenate([inputs[n] for n in ("pre_mix_norm", "post_mix_norm", "pre_mlp_norm", "post_mlp_norm",
                                                      "ln1_g_2", "ln1_b_2", "ln2_g_2", "ln2_b_2")]),
        "cst_d": cst,
        "swab_d": swab,
        "sinks_d": np.ascontiguousarray(inputs["sinks"][0]),
        "bf_d": np.ascontiguousarray(inputs["b_f_2"][0].reshape(8, 1)),
        "ps_d": np.ascontiguousarray(inputs["pool_scale_2"][0].reshape(4, 128).T),
        "pw_d": np.ascontiguousarray(inputs["pool_w_2"][0].transpose(1, 0, 2)),
        "wf_d": np.ascontiguousarray(inputs["w_in_2"][0][:, 2048:].reshape(8, 128, 8).transpose(1, 0, 2).reshape(128, 64)),
    }
    I = {n: nc.dram_tensor(n, a.shape, F32, kind="ExternalInput").ap() for n, a in arrays.items()}
    I["wp_d"] = nc.dram_tensor("wp_d", (NPIECES, 128, 1024), F32, kind="ExternalInput").ap()
    out = nc.dram_tensor("out_d", (T, D), F32, kind="ExternalOutput").ap()
    sg = nc.dram_tensor("sg_d", (16, 128, T), F32, kind="Internal").ap()
    cd = nc.dram_tensor("cd_d", (8, T), F32, kind="Internal").ap()
    descs = build(nc, I["wp_d"], I["x_d"], I["rows_d"], {"sinks": I["sinks_d"], "b_f": I["bf_d"], "pool_scale": I["ps_d"]},
                  I["cst_d"], I["swab_d"], I["pw_d"], I["wf_d"], out, sg, cd)
    arrays["wp_d"] = pack(inputs, descs)
    r = _run(nc, [arrays], core_ids=[0])
    return r.results[0]["out_d"].reshape(1, T, D)
```

```python
from contextlib import ExitStack

import numpy as np
import concourse.bass as bass
from concourse import mybir

F32 = mybir.dt.float32
F32R = mybir.dt.float32r
BF16 = mybir.dt.bfloat16
ACT = mybir.ActivationFunctionType
ALU = mybir.AluOpType

T = 1024
D = 1024
NT = 8
ALPHA = float(2.0 ** 0.25)
EPS = 1e-6
LN_EPS = 1e-5
NEG = -1e30
NPIECES = 218
SLOTS = 5
RAWS = 3
CW = 128 + 128 + 512 + 512 + 4 + 64


def constants():
    c = np.zeros((128, CW), np.float64)
    i = np.arange(128)
    c[:, 0:128] = np.eye(128)
    c[:, 128:256] = np.where(i[None, :] > i[:, None], NEG, 0.0)
    for h in range(4):
        lg = np.log(1.0 - 2.0 ** (-5.0 - h))
        diff = i[None, :] - i[:, None]
        c[:, 256 + 128 * h:384 + 128 * h] = np.where(diff >= 0, np.exp(lg * np.maximum(diff, 0)), 0.0) * 128 ** -0.5
        c[:, 768 + 128 * h:896 + 128 * h] = np.exp(lg * (i + 1.0))[None, :]
        c[:, 1280 + h] = np.exp(lg * (127.0 - i)) * 128 ** -0.5
    for g, win in enumerate((2, 4, 8, 16)):
        c[:, 1284 + 16 * g:1300 + 16 * g] = 1.0 / np.minimum(np.arange(16) + 1.0, win)
    b = np.zeros((128, 8, 256), np.float64)
    dist = (i[:, None] + 128) - np.arange(256)[None, :]
    for h in range(8):
        b[:, h, :] = np.where((dist >= 0) & (dist < 128), -(2.0 ** -(h + 1.0)) * dist, NEG)
    return c.astype(np.float32), b.reshape(128, 2048).astype(np.float32)


class Engine:

    def __init__(self, sem, e):
        self.sem, self.e, self.count, self.seen = sem, e, 0, {}

    def wait(self, *tokens):
        for t in tokens:
            if t is None:
                continue
            sem, value = t
            if self.seen.get(id(sem), 0) >= value:
                continue
            self.seen[id(sem)] = value
            if self.e is not None:
                self.e.wait_ge(sem, value)

    def do(self, f, *tokens):
        self.wait(*tokens)
        self.count += 1
        if self.e is not None:
            f(self.e).then_inc(self.sem, 1)
        return (self.sem, self.count)

    def run(self, f):
        if self.e is not None:
            f(self.e)

    def now(self):
        return (self.sem, self.count) if self.count else None


class Banks:
    def __init__(self, tensors):
        self.t, self.at, self.freed = tensors, 0, [None] * len(tensors)

    def take(self):
        b = self.at
        self.at = (self.at + 1) % len(self.t)
        return b, self.t[b], self.freed[b]

    def give(self, b, token):
        self.freed[b] = token


class Pipeline:

    def __init__(self, n, *stages):
        self.n, self.stages, self.step = n, stages, 0

    def push(self, *_):
        for lag in reversed(range(len(self.stages))):
            t = self.step - lag
            if 0 <= t < self.n:
                self.stages[lag](t)
        self.step += 1
        if self.step == self.n:
            for _ in range(len(self.stages) - 1):
                self.push()


def interleave(main, side, ratio):
    live = [main, side]
    credit = 0.0
    while live:
        if main in live:
            credit += 1.0
            try:
                next(main)
            except StopIteration:
                live.remove(main)
        else:
            credit += 1e9
        while side in live and credit >= ratio:
            credit -= ratio
            try:
                next(side)
            except StopIteration:
                live.remove(side)
            if main not in live:
                credit = 1e9


def build(nc, wp, x_in, rows, small, cst, swab, poolw, wf, out, sg, cd, yd):
    args = (wp, x_in, rows, small, cst, swab, poolw, wf, out, sg, cd, yd)
    with ExitStack() as ctx:
        bank_t = [ctx.enter_context(nc.psum_tensor(f"bank{i}", [128, 512], F32)) for i in range(8)]
        block = ctx.enter_context(nc.Block())
        made, sems, said = {}, {}, []
        for reg, name in ((block.sync, "sp"), (block.scalar, "act"), (block.vector, "dve"), (block.gpsimd, "pool"),
                          (block.tensor, "pe")):
            @reg
            def _(e, name=name):
                said.append(program(nc, ctx, bank_t, made, sems, name, e, *args))
    assert all(d == said[0] for d in said)
    return said[0]


def program(nc, ctx, bank_t, made, sems, turn, engine, wp, x_in, rows, small, cst, swab, poolw, wf, out, sg, cd, yd):
    base = (nc.sbuf_base + 31) // 32 * 32

    def at(name, kb, shape, dt=F32):
        if name not in made:
            made[name] = nc.alloc_sbuf_tensor_at(name, shape, dt, offset=base + int(kb * 1024))
        return made[name]

    def sem(name):
        if name not in sems:
            sems[name] = ctx.enter_context(nc.semaphore(name))
        return sems[name]

    banks = Banks(bank_t)
    pe, act, dve, pool, sp = (Engine(sem(f"s_{n}"), engine if n == turn else None) for n in ("pe", "act", "dve", "pool", "sp"))
    descs = []
    mark = {}

    XO, WO, RO, HO, CO, FO = 0, 32, 72, 84, 148, 149.625
    X = at("X", XO, [128, NT, D])
    whi = [at(f"whi{i}", WO + 4 * i, [128, 1024], F32R) for i in range(SLOTS)]
    wlo = [at(f"wlo{i}", WO + 20 + 4 * i, [128, 1024], F32R) for i in range(SLOTS)]
    raw = [at(f"raw{i}", RO + 4 * i, [128, 1024]) for i in range(RAWS)]
    ident = at("ident", CO, [128, 128])
    identb = at("identb", CO + 0.5, [128, 128], BF16)
    maskb = at("maskb", CO + 0.75, [128, 128], BF16)
    st = at("st", CO + 1, [128, 160])

    def H(name):
        return at(name + "hi", HO, [128, NT, T], F32R), at(name + "lo", HO + 32, [128, NT, T], F32R)

    def dma(dst, src, s, value, *tokens):
        sp.wait(*tokens)
        sp.run(lambda e: e.dma_start(dst, src).then_inc(s, 16))
        return (s, value)

    loads = {}

    def load(name, dst, src, *tokens):
        s = loads.setdefault(name, [sem("l_" + name), 0])
        s[1] += 16
        return dma(dst, src, s[0], s[1], *tokens)

    raw_sem = [sem(f"raw_{i}") for i in range(RAWS)]
    fetched, split_tok, slot_free = {}, {}, {}
    W = {"cur": 0, "split": 0}

    def fetch(n):
        if n >= NPIECES:
            return
        tokens = split_tok[n - RAWS] if n >= RAWS else ()
        fetched[n] = dma(raw[n % RAWS][:, :], wp[n], raw_sem[n % RAWS], 16 * (n // RAWS + 1), *tokens)

    def split(n):
        r, s = raw[n % RAWS], n % SLOTS
        a = act.do(lambda e: e.activation(whi[s][:, :], r[:, :], ACT.Copy), fetched[n], slot_free.get(n - SLOTS))
        b = dve.do(lambda e: e.tensor_tensor(out=wlo[s][:, :], in0=r[:, :], in1=whi[s][:, :].bitcast(F32),
                                             op=ALU.subtract), a)
        split_tok[n] = (a, b)
        fetch(n + RAWS)

    def ahead(limit):
        while W["split"] < min(limit, NPIECES):
            split(W["split"])
            W["split"] += 1

    def piece(*desc):
        n = W["cur"]
        W["cur"] += 1
        descs.append(desc)
        ahead(n + 1)
        pe.wait(*split_tok[n])
        return n

    def done(n, token):
        slot_free[n] = token
        ahead(n + SLOTS + 1)

    def hl(n):
        return whi[n % SLOTS], wlo[n % SLOTS]

    def mm3(out, sh, sl, mh, ml, first, last):
        pe.run(lambda e: e.matmul(out, sh, mh, start=first, stop=False))
        pe.run(lambda e: e.matmul(out, sh, ml, start=False, stop=False))
        f = lambda e: e.matmul(out, sl, mh, start=False, stop=last)
        if last:
            return pe.do(f)
        pe.run(f)

    def half_product(n, half, hi, lo, evac, *ready):
        wh, wl = hl(n)
        b, P, free = banks.take()
        pe.wait(free, *ready)
        for k in range(8):
            tok = mm3(P[:, :], wh[:, 128 * k:128 * k + 128], wl[:, 128 * k:128 * k + 128],
                      hi[:, k, 512 * half:512 * half + 512], lo[:, k, 512 * half:512 * half + 512], k == 0, k == 7)
            if k == 3:
                yield
        banks.give(b, evac(half, P, tok))
        if half == 1:
            done(n, tok)
        yield

    def feature_major(name, col, hi, lo, evac):
        n = piece("F", name, col)
        for half in range(2):
            yield from half_product(n, half, hi, lo, evac)

    def feature_major_start(name, cols, hi, lo, evacs, ready):
        ns = []
        for half in range(2):
            for c, evac in zip(cols, evacs):
                if half == 0:
                    ns.append(piece("F", name, c))
                run(half_product(ns[cols.index(c)], half, hi, lo, evac, *ready[4 * half + 3]))

    def token_major(name, col, hi, lo, evac):
        ns = [piece("T", name, col, 0), piece("T", name, col, 4)]
        for t in range(NT):
            b, P, free = banks.take()
            pe.wait(free)
            for k in range(8):
                wh, wl = hl(ns[k // 4])
                c = 256 * (k % 4)
                tok = mm3(P[:, 0:256], hi[:, k, 128 * t:128 * t + 128], lo[:, k, 128 * t:128 * t + 128],
                          wh[:, c:c + 256], wl[:, c:c + 256], k == 0, k == 7)
            banks.give(b, evac(t, P, tok))
            if t % 4 == 3:
                if t == 7:
                    for n in ns:
                        done(n, tok)
                yield

    def rows_group(name, ks, stat, acc, first, after=None, seed=None):
        mark["pre"] = pe.now()
        ns = [piece("D", name, k) for k in ks]
        for t in range(NT):
            for c in range(2):
                b, P, free = banks.take()
                pe.wait(free)
                for j, k in enumerate(ks):
                    wh, wl = hl(ns[j])
                    sh, sl = stat(k)
                    tok = mm3(P[:, :], sh[:, 128 * t:128 * t + 128], sl[:, 128 * t:128 * t + 128],
                              wh[:, 512 * c:512 * c + 512], wl[:, 512 * c:512 * c + 512], j == 0, j == len(ks) - 1)
                dst = acc[:, t, 512 * c:512 * c + 512]
                if seed is not None:
                    add, ok = seed(t)
                    a = dve.do(lambda e: e.tensor_tensor(out=dst, in0=P[:, :], in1=add[:, 512 * c:512 * c + 512], op=ALU.add),
                               tok, ok, *first)
                elif first:
                    a = act.do(lambda e, dst=dst, P=P: e.activation(dst, P[:, :], ACT.Copy), tok)
                else:
                    a = dve.do(lambda e, dst=dst, P=P: e.tensor_tensor(out=dst, in0=P[:, :], in1=dst, op=ALU.add),
                               tok, act.now() if c == 0 and t == 0 else None, dve.now())
                banks.give(b, a)
            if t == 7:
                for n in ns:
                    done(n, tok)
            if after is not None:
                after(t, a)
            if t % 2:
                yield

    def run(gen):
        for _ in gen:
            pass

    def transpose_split(src, t, hi, lo, tokens, free=()):
        for q in range(2):
            b, P, f = banks.take()
            pe.wait(f, *tokens)
            for j in range(4):
                k = 4 * q + j
                g = lambda e, j=j, k=k, P=P: e.transpose(P[:, 128 * j:128 * j + 128], src[:, 128 * k:128 * k + 128], ident[:, :])
                if j == 3:
                    tok = pe.do(g)
                else:
                    pe.run(g)
            pv = P[:, :].rearrange("p (j c) -> p j c", j=4)
            oh = hi[:, 4 * q:4 * q + 4, 128 * t:128 * t + 128]
            ol = lo[:, 4 * q:4 * q + 4, 128 * t:128 * t + 128]
            a = act.do(lambda e, oh=oh, pv=pv: e.activation(oh, pv, ACT.Copy), tok, *free)
            d = dve.do(lambda e, oh=oh, ol=ol, pv=pv: e.tensor_tensor(out=ol, in0=pv, in1=oh.bitcast(F32), op=ALU.subtract), a)
            banks.give(b, d)
        return tok, (a, d)

    def rstd(src, dst, scale, eps, *tokens):
        a = dve.do(lambda e: e.tensor_scalar(dst, src, scale, eps, ALU.mult, ALU.add), *tokens)
        a = act.do(lambda e: e.activation(dst, dst, ACT.Sqrt), a)
        return dve.do(lambda e: e.reciprocal(dst, dst), a)

    fetch(0)
    xt = [load(f"x{t}", X[:, t, :], x_in[128 * t:128 * t + 128, :]) for t in range(2)]
    id_ok = load("id", ident[:, :], cst[:, 0:128])
    gb = at("gb0", FO, [128, 1024])
    gb_ok = load("row", gb[:, :], rows[0].partition_broadcast(128))
    fetch(1)
    fetch(2)
    xt += [load(f"x{t}", X[:, t, :], x_in[128 * t:128 * t + 128, :]) for t in range(2, NT)]
    junk = at("junk0", FO + 4, [128, 1024])
    ht = [at(f"ht0{i}", FO + 8 + 4 * i, [128, 1024]) for i in range(2)]
    hhi, hlo = H("h")
    read = [None, None]
    rows_ok = {}
    sq_ok = {}

    def s_square(t):
        sq_ok[t] = act.do(lambda e: e.activation(junk[:, :], X[:, t, :], ACT.Square, accum_out=st[:, t:t + 1]), xt[t], sq_ok.get(t - 1))

    def s_scale(t):
        r = rstd(st[:, t:t + 1], st[:, 8 + t:9 + t], 1.0 / D, EPS, sq_ok[t])
        sq_ok[t] = dve.do(lambda e: e.scalar_tensor_tensor(ht[t % 2][:, :], X[:, t, :], st[:, 8 + t:9 + t], gb[:, :],
                                                           ALU.mult, ALU.mult), r, gb_ok, read[t % 2])

    def s_transpose(t):
        read[t % 2], rows_ok[t] = transpose_split(ht[t % 2], t, hhi, hlo, (sq_ok[t], id_ok))

    start = Pipeline(NT, s_square, s_scale, s_transpose)
    for t in range(NT):
        start.push()
    x_free = sq_ok[7]

    qs = at("qs", FO, [128, 4, T])
    ks = at("ks", FO + 16, [128, T])
    vs = at("vs", FO + 20, [128, NT, 128])
    sbias = at("sbias", FO + 24, [128, 8, 256])
    pt_ = [at(f"p{i}", FO + 32 + 8 * i, [128, 8, 256]) for i in range(2)]
    PT = [at(f"PT{i}", FO + 48 + 2 * i, [128, 512]) for i in range(4)]
    swa = at("swa", FO + 56, [128, 4, T])
    sig = [at(f"sig{i}", XO + 4 * i, [128, T]) for i in range(4)]
    vsT = at("vsT", XO + 16, [128, T])
    sb_ok = load("swab", sbias[:, :, :].rearrange("p h j -> p (h j)"), swab, read[0], read[1], pe.now(), dve.now())
    sink_ok = load("sink", st[:, 16:24], small["sinks"].partition_broadcast(128))

    def scaled_to(dst, scale, *tokens):
        def evac(half, P, tok):
            return act.do(lambda e: e.activation(dst[:, 512 * half:512 * half + 512], P[:, :], ACT.Copy, scale=scale), tok, *tokens)
        return evac

    feature_major_start("q_s", [0, 1, 2, 3], hhi, hlo,
                        [scaled_to(qs[:, m, :], 0.125, pe.now(), dve.now()) for m in range(4)], rows_ok)
    run(feature_major("k_s", 0, hhi, hlo, scaled_to(ks, 1.0)))
    run(feature_major("v_s", 0, hhi, hlo, scaled_to(vsT, 1.0, x_free)))
    vs_in = act.now()
    for q in range(2):
        b, P, f = banks.take()
        pe.wait(f, vs_in)
        for j in range(4):
            t = 4 * q + j
            tok = pe.do(lambda e, j=j, t=t, P=P: e.transpose(P[:, 128 * j:128 * j + 128], vsT[:, 128 * t:128 * t + 128], ident[:, :]))
        vs_ok = dve.do(lambda e, q=q, P=P: e.tensor_copy(vs[:, 4 * q:4 * q + 4, :].rearrange("p a c -> p (a c)"), P[:, :]), tok)
        banks.give(b, vs_ok)

    sig_free = [None] * 4
    gate_ok = {}
    gcount = [0]

    def gate_evac(index):
        i = index % 4
        toks = []

        def evac(half, P, tok):
            v = sig[i][:, 512 * half:512 * half + 512]
            a = act.do(lambda e: e.activation(v, P[:, :], ACT.Tanh, scale=0.5), tok, sig_free[i], x_free)
            p = pool.do(lambda e: e.tensor_scalar(v, v, 0.5, 0.5, ALU.mult, ALU.add), a)
            toks.append(p)
            if half == 1:
                sig_free[i] = gate_ok[index] = load(f"sg{i}", sg[index], sig[i][:, :], *toks)
            return a
        return evac

    def gates(which):
        for index in which:
            yield from feature_major("gate_s" if index < 8 else "gate_r", index % 8, hhi, hlo, gate_evac(index))

    p_free = [None, None]
    PT_free = [None] * 4
    ptn = [0]

    def swa_scores(n):
        p = pt_[n % 2]
        j0 = 128 if n == 0 else 0
        last = None
        for mm in range(2):
            pair = [banks.take(), banks.take()]
            for m in range(2 * mm, 2 * mm + 2):
                for g in range(2):
                    b, P, f = pair[g]
                    pe.wait(f, qs_ok)
                    tok = pe.do(lambda e: e.matmul(
                        P[:, 256 * (m % 2) + j0:256 * (m % 2) + 256], qs[64 * g:64 * g + 64, m, 128 * n:128 * n + 128],
                        ks[64 * g:64 * g + 64, 128 * n - 128 + j0:128 * n + 128], start=True, stop=True))
            for g in range(2):
                b, P, f = pair[g]
                for m in range(2 * mm, 2 * mm + 2):
                    h = 4 * g + m
                    last = dve.do(lambda e: e.tensor_tensor_reduce(
                        out=p[:, h, j0:256], in0=P[:, 256 * (m % 2) + j0:256 * (m % 2) + 256], in1=sbias[:, h, j0:256], scale=1.0,
                        scalar=st[:, 16 + h:17 + h], op0=ALU.add, op1=ALU.max, accum_out=st[:, 24 + h:25 + h]),
                        tok, sb_ok, sink_ok, p_free[n % 2], swa_nm[0])
                banks.give(b, last)
        nm = dve.do(lambda e: e.tensor_scalar(st[:, 32:40], st[:, 24:32], -1.0, None, ALU.mult), last, act.now())
        sk = dve.do(lambda e: e.tensor_tensor(out=st[:, 40:48], in0=st[:, 16:24], in1=st[:, 24:32], op=ALU.subtract), last)
        swa_nm[0] = sk
        for h in range(8):
            ex = act.do(lambda e, h=h: e.activation(p[:, h, j0:256], p[:, h, j0:256], ACT.Exp, bias=st[:, 32 + h:33 + h],
                                                    accum_out=st[:, 48 + h:49 + h]), nm, swa_nm[1])
        es = act.do(lambda e: e.activation(st[:, 40:48], st[:, 40:48], ACT.Exp), sk)
        a = dve.do(lambda e: e.tensor_tensor(out=st[:, 48:56], in0=st[:, 48:56], in1=st[:, 40:48], op=ALU.add), ex, es)
        a = dve.do(lambda e: e.reciprocal(st[:, 48:56], st[:, 48:56]), a)
        for h in range(8):
            a2 = dve.do(lambda e, h=h: e.tensor_scalar(p[:, h, j0:256], p[:, h, j0:256], st[:, 48 + h:49 + h], None, ALU.mult), a)
        swa_nm[1] = a2
        return a2

    swa_nm = [None, None]
    qs_ok = act.now()

    def swa_values(n, ready):
        p = pt_[n % 2]
        jts = [1] if n == 0 else [0, 1]
        ob, O, of = banks.take()
        for g in range(2):
            for jt_ in jts:
                b, P, f = banks.take()
                pe.wait(f, ready)
                for r in range(4):
                    tok = pe.do(lambda e, r=r, P=P: e.transpose(P[:, 128 * r:128 * r + 128],
                                                                p[:, 4 * g + r, 128 * jt_:128 * jt_ + 128], ident[:, :]))
                i = ptn[0] % 4
                ptn[0] += 1
                a = act.do(lambda e, i=i, P=P: e.activation(PT[i][:, :], P[:, :], ACT.Copy), tok, PT_free[i])
                banks.give(b, a)
                pe.wait(a, of, vs_ok)
                PT_free[i] = pe.do(lambda e, i=i: e.matmul(O[64 * g:64 * g + 64, :], vs[:, n - 1 + jt_, 64 * g:64 * g + 64],
                                                           PT[i][:, :], start=jt_ == jts[0], stop=jt_ == 1))
        p_free[n % 2] = tok
        d = dve.do(lambda e: e.tensor_copy(swa[:, :, 128 * n:128 * n + 128], O[:, :].rearrange("p (r c) -> p r c", r=4)), PT_free[i])
        banks.give(ob, d)
        return d

    def swa_all():
        ready = swa_scores(0)
        yield
        for n in range(8):
            nxt = swa_scores(n + 1) if n < 7 else None
            yield
            swa_values(n, ready)
            ready = nxt
            yield

    interleave(gates(range(16)), swa_all(), 1.8)
    swa_ok = dve.now()
    swa_reads = (pe.now(), act.now(), dve.now())

    ret = at("ret", XO, [128, 8, T])
    rq = [at(f"rq{i}", FO + 4 * i, [128, T]) for i in range(2)]
    rk = [at(f"rk{i}", FO + 8 + 4 * i, [128, T]) for i in range(2)]
    rv = [at(f"rv{i}", FO + 16 + 8 * i, [128, NT, 256]) for i in range(2)]
    rg = at("rg", FO + 32, [128, 2, T])
    ro = at("ro", FO + 40, [128, NT, 256])
    dect = at("dect", FO + 48, [128, 1028])
    rs = [at(f"rs{i}", FO + 52.03125 + i, [128, 256]) for i in range(2)]
    ss = [at(f"ss{i}", FO + 54.03125 + 0.5 * i, [128, 128]) for i in range(2)]
    kd = at("kd", FO + 55.03125, [128, 128])
    rq2 = at("rq2", FO + 72, [128, 128])
    tb = at("tb", FO + 72.5, [128, 128])
    tab_ok = load("tab", dect[:, :], cst[:, 256:1284], *swa_reads)

    rfree = {"q": [None, None], "v": [None, None], "g": None, "o": None, "gs": None}
    rready = {}

    def ret_proj(h):
        i = h % 2
        run_ev = lambda dst, fr: scaled_to(dst, 1.0, fr, *swa_reads)
        yield from feature_major("q_r", h, hhi, hlo, run_ev(rq[i], rfree["q"][i]))
        yield from feature_major("k_r", h, hhi, hlo, run_ev(rk[i], rfree["q"][i]))

        def ev(t, P, tok):
            return act.do(lambda e: e.activation(rv[i][:, t, :], P[:, 0:256], ACT.Copy), tok, rfree["v"][i], *swa_reads)
        yield from token_major("v_r", 256 * h, hhi, hlo, ev)
        rready[h] = act.now()

    def ret_gate(h):
        for m in range(2):
            def ev(half, P, tok, m=m):
                v = rg[:, m, 512 * half:512 * half + 512]
                a = act.do(lambda e: e.activation(v, P[:, :], ACT.Tanh, scale=0.5), tok, rfree["g"], *swa_reads)
                a = pool.do(lambda e: e.tensor_scalar(v, v, 0.5, 0.5, ALU.mult, ALU.add), a)
                return dve.do(lambda e: e.tensor_tensor(out=v, in0=P[:, :], in1=v, op=ALU.mult), a)
            yield from feature_major("g_r", 2 * h + m, hhi, hlo, ev)
        rready["g"] = dve.now()

    def retention(h):
        i = h % 2
        gamma = 1.0 - 2.0 ** (-5.0 - h)
        decay = dect[:, 128 * h:128 * h + 128]
        qdec = dect[:, 512 + 128 * h:640 + 128 * h]
        kcol = dect[:, 1024 + h:1025 + h]
        qtmp = [rq2, tb]
        s_ok = rkv = None
        for n in range(8):
            c = slice(128 * n, 128 * n + 128)
            b, P, f = banks.take()
            pe.wait(f, rready[h])
            a = pe.do(lambda e: e.matmul(P[:, 0:128], rk[i][:, c], rq[i][:, c], start=True, stop=True))
            if n < 7:
                a = pe.do(lambda e: e.transpose(P[:, 128:256], rk[i][:, c], ident[:, :]))
            s1 = dve.do(lambda e: e.tensor_tensor(out=ss[n % 2][:, :], in0=P[:, 0:128], in1=decay, op=ALU.mult),
                        a, tab_ok, pe.now())
            if n > 0:
                q1 = dve.do(lambda e, n=n: e.tensor_tensor(out=qtmp[n % 2][:, :], in0=rq[i][:, c], in1=qdec, op=ALU.mult), s1)
            if n < 7:
                k1 = act.do(lambda e: e.activation(kd[:, :], P[:, 128:256], ACT.Copy, scale=kcol), a, s1, tab_ok, rkv)
                banks.give(b, k1)
            else:
                banks.give(b, s1)
            yield
            b, P, f = banks.take()
            pe.wait(f, s1)
            o = pe.do(lambda e, P=P: e.matmul(P[:, 0:256], ss[n % 2][:, :], rv[i][:, n, :], start=True, stop=n == 0))
            if n > 0:
                pe.wait(q1, s_ok)
                o = pe.do(lambda e, P=P: e.matmul(P[:, 0:256], qtmp[n % 2][:, :], rs[(n - 1) % 2][:, :], start=False, stop=True))
            if n < 7:
                b2, P2, f2 = banks.take()
                pe.wait(f2, k1)
                rkv = pe.do(lambda e, P2=P2: e.matmul(P2[:, 0:256], kd[:, :], rv[i][:, n, :], start=True, stop=True))
                if n == 0:
                    s_ok = dve.do(lambda e, P2=P2: e.tensor_copy(rs[0][:, :], P2[:, 0:256]), rkv)
                else:
                    s_ok = dve.do(lambda e, P2=P2: e.scalar_tensor_tensor(
                        rs[n % 2][:, :], rs[(n - 1) % 2][:, :], float(gamma ** 128), P2[:, 0:256], ALU.mult, ALU.add), rkv, s_ok)
                banks.give(b2, s_ok)
            a = act.do(lambda e, P=P: e.activation(ro[:, n, :], P[:, 0:256], ACT.Copy), o, rfree["o"])
            banks.give(b, a)
            bn = dve.do(lambda e: e.bn_stats(st[:, 24:30], ro[:, n, :]), a, dve.now())
            bn = dve.do(lambda e: e.bn_aggr(st[:, 32 + 2 * n:34 + 2 * n], st[:, 24:30]), bn)
            yield
        rfree["q"][i] = rfree["v"][i] = pe.now()
        mv = st[:, 32:48].rearrange("p (n two) -> p n two", two=2)
        r = rstd(mv[:, :, 1], st[:, 48:56], 1.0, EPS, bn)
        for n in range(8):
            d = dve.do(lambda e, n=n: e.tensor_scalar(ro[:, n, :], ro[:, n, :], st[:, 32 + 2 * n:33 + 2 * n],
                                                      st[:, 48 + n:49 + n], ALU.subtract, ALU.mult), r)
        yield
        for m in range(2):
            for q in range(2):
                b, P, f = banks.take()
                pe.wait(f, d)
                for j in range(4):
                    a = pe.do(lambda e, j=j, P=P: e.transpose(P[:, 128 * j:128 * j + 128],
                                                              ro[:, 4 * q + j, 128 * m:128 * m + 128], ident[:, :]))
                w = dve.do(lambda e, P=P: e.tensor_tensor(out=ret[:, 2 * h + m, 512 * q:512 * q + 512], in0=P[:, :],
                                                          in1=rg[:, m, 512 * q:512 * q + 512], op=ALU.mult),
                           a, rready["g"], *sig_free)
                banks.give(b, w)
            yield
        rfree["o"] = a
        rfree["g"] = w

    run(ret_proj(0))
    for h in range(4):
        def main(h=h):
            yield from ret_gate(h)
            if h < 3:
                yield from ret_proj(h + 1)
        interleave(main(), retention(h), 0.5)
    ret_ok = dve.now()

    h_dead = pe.now()
    rethi = at("rethi", HO, [128, 8, T], F32R)
    swahi = at("swahi", HO + 32, [128, 4, T], F32R)
    retlo = at("retlo", XO, [128, 8, T], F32R)
    swalo = at("swalo", FO + 56, [128, 4, T], F32R)
    Z = at("Z", FO, [128, 8, T])
    mlo = at("mlo", FO, [128, 8, T], F32R)
    gs = [at(f"gs{i}", FO + 32 + 4 * i, [128, T]) for i in range(4)]
    mp = [at("mp0", HO + 48, [128, 2, T], F32R), at("mp1", HO + 56, [128, 2, T], F32R),
          at("mp2", HO + 32, [128, 2, T], F32R), at("mp3", FO + 48, [128, 2, T], F32R)]
    gs_free = [None] * 4
    gl = {}
    F_free = (pe.now(), act.now(), dve.now())

    def fetch_gate(n):
        if n < 16:
            gl[n] = load(f"gl{n % 4}", gs[n % 4][:, :], sg[n], gate_ok[n], gs_free[n % 4], *F_free)

    for n in range(4):
        fetch_gate(n)
    sw_ok = {}
    for m in range(4):
        a = act.do(lambda e, m=m: e.activation(swahi[:, m, :], swa[:, m, :], ACT.Copy), h_dead, swa_ok)
        sw_ok[m] = dve.do(lambda e, m=m: e.tensor_tensor(out=swalo[:, m, :], in0=swa[:, m, :], in1=swahi[:, m, :].bitcast(F32),
                                                         op=ALU.subtract), a)
    rt_ok = {}

    def split_ret(m):
        a = act.do(lambda e, m=m: e.activation(rethi[:, m, :], ret[:, m, :], ACT.Copy), h_dead, ret_ok)
        rt_ok[m] = dve.do(lambda e, m=m: e.tensor_tensor(out=retlo[:, m, :], in0=ret[:, m, :], in1=rethi[:, m, :].bitcast(F32),
                                                         op=ALU.subtract), a)
    for m2 in range(4):
        n = piece("S", "w_swa_out", m2)
        wh, wl = hl(n)
        for mm in range(2):
            m = 2 * m2 + mm
            for half in range(2):
                c = slice(512 * half, 512 * half + 512)
                b, P, f = banks.take()
                pe.wait(f)
                for k in range(4):
                    pe.wait(sw_ok[k])
                    w0 = 512 * mm + 128 * k
                    tok = mm3(P[:, :], wh[:, w0:w0 + 128], wl[:, w0:w0 + 128], swahi[:, k, c], swalo[:, k, c], k == 0, k == 3)
                z = dve.do(lambda e, P=P, c=c, m=m: e.tensor_tensor(out=Z[:, m, c], in0=P[:, :], in1=gs[m % 4][:, c], op=ALU.mult),
                           tok, gl[m], *F_free)
                banks.give(b, z)
            gs_free[m % 4] = z
            fetch_gate(m + 4)
            split_ret(m)
        done(n, tok)
    swa_dead = pe.now()
    m_ok = {}
    tmpz = gs
    for m in range(8):
        n = piece("F", "w_ret_out", m)
        wh, wl = hl(n)
        for half in range(2):
            c = slice(512 * half, 512 * half + 512)
            b, P, f = banks.take()
            pe.wait(f)
            for k in range(8):
                pe.wait(rt_ok[k])
                tok = mm3(P[:, :], wh[:, 128 * k:128 * k + 128], wl[:, 128 * k:128 * k + 128], rethi[:, k, c], retlo[:, k, c],
                          k == 0, k == 7)
            g = gs[m % 4]
            z = dve.do(lambda e, P=P, c=c, g=g: e.tensor_tensor(out=g[:, c], in0=P[:, :], in1=g[:, c], op=ALU.mult), tok, gl[8 + m])
            banks.give(b, z)
            z = pool.do(lambda e, c=c, m=m, g=g: e.tensor_tensor(out=Z[:, m, c], in0=Z[:, m, c], in1=g[:, c], op=ALU.add), z)
            hi_ = mp[m // 2][:, m % 2, c]
            a = act.do(lambda e, hi_=hi_, c=c, m=m: e.activation(hi_, Z[:, m, c], ACT.Copy), z, swa_dead)
            m_ok[m] = dve.do(lambda e, hi_=hi_, c=c, m=m: e.tensor_tensor(out=mlo[:, m, c], in0=Z[:, m, c], in1=hi_.bitcast(F32),
                                                                          op=ALU.subtract), a)
        done(n, tok)
        gs_free[m % 4] = z
        fetch_gate(8 + m + 4)
    ret_dead = pe.now()

    acc = at("accX", XO, [128, NT, D])
    xs = [at(f"xs{i}", FO + 32 + 4 * i, [128, D]) for i in range(3)]
    g1 = at("g1", FO + 56, [128, D])
    g2 = at("g2", FO + 60, [128, D])
    hj = at("hj", FO + 44, [128, D])
    hs = [at("hs0", FO + 64, [128, D]), at("hs1", FO + 68, [128, D])]
    row_ok = load("row", g1[:, :], rows[1].partition_broadcast(128), swa_dead, ret_dead, pool.now(), dve.now())
    row_ok = load("row", g2[:, :], rows[2].partition_broadcast(128))
    xs_free = [(pool.now(), dve.now())] * 3
    xl = {}

    def fetch_x(t):
        if t < NT:
            xl[t] = load(f"xl{t % 3}", xs[t % 3][:, :], x_in[128 * t:128 * t + 128, :], *xs_free[t % 3])

    for t in range(3):
        fetch_x(t)
    hhi2, hlo2 = H("h2")
    accd, r1, r2, h2_ok, hs_free, mg = {}, {}, {}, {}, [None, None], {}
    z_dead = (act.now(), dve.now(), pool.now())

    def m_square(t):
        r1[t] = act.do(lambda e: e.activation(hj[:, :], acc[:, t, :], ACT.Square, accum_out=st[:, 4 * t:4 * t + 1]),
                       accd[t], mg.get("j"), *z_dead)
        mg["j"] = r1[t]

    def m_residual(t):
        r = rstd(st[:, 4 * t:4 * t + 1], st[:, 4 * t + 1:4 * t + 2], 1.0 / D, EPS, r1[t])
        d = dve.do(lambda e: e.scalar_tensor_tensor(acc[:, t, :], acc[:, t, :], st[:, 4 * t + 1:4 * t + 2], g1[:, :],
                                                    ALU.mult, ALU.mult), r, row_ok)
        r1[t] = pool.do(lambda e: e.tensor_tensor(out=acc[:, t, :], in0=acc[:, t, :], in1=xs[t % 3][:, :], op=ALU.add), d, xl[t])
        xs_free[t % 3] = (r1[t],)
        fetch_x(t + 3)

    def m_square2(t):
        r2[t] = act.do(lambda e: e.activation(hj[:, :], acc[:, t, :], ACT.Square, accum_out=st[:, 4 * t + 2:4 * t + 3]), r1[t], mg["j"])
        mg["j"] = r2[t]

    def m_scale(t):
        r = rstd(st[:, 4 * t + 2:4 * t + 3], st[:, 4 * t + 3:4 * t + 4], 1.0 / D, EPS, r2[t])
        r2[t] = dve.do(lambda e: e.scalar_tensor_tensor(hs[t % 2][:, :], acc[:, t, :], st[:, 4 * t + 3:4 * t + 4], g2[:, :],
                                                        ALU.mult, ALU.mult), r, hs_free[t % 2])

    def m_transpose(t):
        hs_free[t % 2], h2_ok[t] = transpose_split(hs[t % 2], t, hhi2, hlo2, (r2[t],), (mg["x"],))

    mix = Pipeline(NT, m_square, m_residual, m_square2, m_scale, m_transpose)

    def mix_after(t, tok):
        accd[t] = tok
        mix.push()

    for g in range(4):
        if g == 3:
            mg["x"] = pe.now()
        run(rows_group("w_out", [2 * g, 2 * g + 1], lambda k: (mp[k // 2][:, k % 2, :], mlo[:, k, :]), acc, g == 0,
                       mix_after if g == 3 else None))

    def mlp(up, down, hi, lo, ready, acc, first_copy, after, free, tag):
        uh = [at(f"uh{tag}{i}", FO + 8 * i, [128, 2, T], F32R) for i in range(2)]
        ul = [at(f"ul{tag}{i}", FO + 16 + 8 * i, [128, 2, T], F32R) for i in range(2)]
        rr = [at(f"rr{tag}{i}", FO + RR + 2 * i, [128, 512]) for i in range(2)]
        uu = [at(f"uu{tag}{i}", FO + RR + 4 + 2 * i, [128, 512]) for i in range(2)]
        u_ok, u_free, count = {}, {}, [0]
        lastd = [None, None]

        def up_evac(G, m):
            def evac(half, P, tok):
                i = count[0] % 2
                count[0] += 1
                c = slice(512 * half, 512 * half + 512)
                a = act.do(lambda e: e.activation(rr[i][:, :], P[:, :], ACT.Relu), tok, lastd[i], *free)
                p = pool.do(lambda e: e.tensor_tensor(out=uu[i][:, :], in0=rr[i][:, :], in1=rr[i][:, :], op=ALU.mult), a, lastd[i])
                b = act.do(lambda e: e.activation(uh[G % 2][:, m, c], rr[i][:, :], ACT.Square), a, u_free.get(G - 2))
                lastd[i] = dve.do(lambda e: e.tensor_tensor(out=ul[G % 2][:, m, c], in0=uu[i][:, :],
                                                            in1=uh[G % 2][:, m, c].bitcast(F32), op=ALU.subtract), p, b)
                return a
            return evac

        def up_group(G):
            for m in range(2):
                yield from feature_major(up, 2 * G + m, hi, lo, up_evac(G, m))
            u_ok[G] = dve.now()

        def down_group(G):
            pe.wait(u_ok[G])
            yield from rows_group(down, [2 * G, 2 * G + 1], lambda k: (uh[G % 2][:, k % 2, :], ul[G % 2][:, k % 2, :]), acc,
                                  first_copy and G == 0, after if G == 15 else None)
            u_free[G] = pe.now()

        feature_major_start(up, [0, 1, 2, 3], hi, lo, [up_evac(0, 0), up_evac(0, 1), up_evac(1, 0), up_evac(1, 1)], ready)
        u_ok[0] = u_ok[1] = dve.now()
        for G in range(16):
            if 0 < G < 15:
                run(up_group(G + 1))
            run(down_group(G))

    RR = 64
    acc2 = at("acc2", FO + 32, [128, NT, D])
    yj = at("yj", FO + 4, [128, D])
    g3 = at("g3", FO, [128, D])
    yhi, ylo = H("y")
    ys, y_ok, yd_ok = {}, {}, {}

    def y_square(t):
        if t == 0:
            ys["dead"] = mark["pre"]
            ys["row"] = load("row", g3[:, :], rows[3].partition_broadcast(128), ys["dead"])
        ys["j"] = ys[t] = act.do(lambda e: e.activation(yj[:, :], acc2[:, t, :], ACT.Square, accum_out=st[:, 4 * t:4 * t + 1]),
                                 accd[t], ys["dead"], ys.get("j"))

    def y_residual(t):
        r = rstd(st[:, 4 * t:4 * t + 1], st[:, 4 * t + 1:4 * t + 2], 1.0 / D, EPS, ys[t])
        d = dve.do(lambda e: e.scalar_tensor_tensor(acc2[:, t, :], acc2[:, t, :], st[:, 4 * t + 1:4 * t + 2], g3[:, :],
                                                    ALU.mult, ALU.mult), r, ys["row"])
        ys[t] = pool.do(lambda e: e.tensor_tensor(out=acc[:, t, :], in0=acc[:, t, :], in1=acc2[:, t, :], op=ALU.add), d)

    def y_transpose(t):
        r, y_ok[t] = transpose_split(acc[:, t, :], t, yhi, ylo, (ys[t],), (ys["dead"],))
        a = act.do(lambda e: e.activation(acc[:, t, :], acc[:, t, :], ACT.Copy, scale=ALPHA), r)
        yd_ok[t] = load("yd", yd[t], acc[:, t, :], a)

    mlp1_norm = Pipeline(NT, y_square, y_residual, y_transpose)

    def mlp1_after(t, tok):
        accd[t] = tok
        mlp1_norm.push()

    free1 = (pe.now(), act.now(), dve.now(), pool.now())
    mlp("w_up", "w_down", hhi2, hlo2, h2_ok, acc2, True, mlp1_after, free1, "a")

    q2 = at("q2", FO, [128, 4, T])
    k2 = at("k2", FO + 16, [128, 4, T])
    vhi = at("vhi", FO + 32, [128, NT, 512], F32R)
    vlo = at("vlo", FO + 48, [128, NT, 512], F32R)
    u2 = at("u2", FO + 32, [128, 4, T])
    pA = at("pA", FO + 48, [128, T])
    pB = at("pB", FO + 52, [128, T])
    pr = at("pr", FO + 58, [128, 64])
    pd = at("pd", XO, [128, 4, T])
    cc = at("cc", FO + 64, [8, T])
    ce = at("ce", FO + 68, [8, T])
    wfr = at("wfr", FO + 72, [128, 64])
    wfh = at("wfh", FO + 72.25, [128, 64], F32R)
    wfl = at("wfl", FO + 72.5, [128, 64], F32R)
    cT = at("cT", FO + 72.75, [128, 64])
    rm = at("rmask", FO + 59, [128, 128])
    pw = at("pw", XO + 16, [128, 4, 128])
    freeF = (pe.now(), act.now(), dve.now(), pool.now())
    wf_ok = load("wf", wfr[:, :], wf, *freeF)
    bf_ok = load("bf", st[0:8, 159:160], small["b_f"])
    ps_ok = load("ps", st[:, 152:156], small["pool_scale"])
    mk_ok = load("mask", rm[:, :], cst[:, 128:256])
    pr_ok = load("pr", pr[:, :], cst[:, 1284:1348])
    pw_ok = load("pw", pw[:, :, :], poolw, yd_ok[7])
    feature_major_start("u_2", [0, 1, 2, 3], yhi, ylo, [scaled_to(u2[:, m, :], 1.0, *freeF) for m in range(4)], y_ok)
    u_in = act.now()
    a = dve.do(lambda e: e.tensor_copy(maskb[:, :], rm[:, :]), mk_ok)
    mask_ok = dve.do(lambda e: e.tensor_copy(identb[:, :], ident[:, :]), a)
    a = act.do(lambda e: e.activation(wfh[:, :], wfr[:, :], ACT.Copy), wf_ok)
    wfs = dve.do(lambda e: e.tensor_tensor(out=wfl[:, :], in0=wfr[:, :], in1=wfh[:, :].bitcast(F32), op=ALU.subtract), a)

    for half in range(2):
        c = slice(512 * half, 512 * half + 512)
        b, P, f = banks.take()
        pe.wait(f, wfs)
        for k in range(8):
            tok = mm3(P[0:8, :], wfh[:, 8 * k:8 * k + 8], wfl[:, 8 * k:8 * k + 8], yhi[:, k, c], ylo[:, k, c], k == 0, k == 7)
        a = act.do(lambda e: e.activation(cc[:, c], P[0:8, :], ACT.Identity, bias=st[0:8, 159:160]), tok, bf_ok, *freeF)
        banks.give(b, a)
    a1 = act.do(lambda e: e.activation(ce[:, :], cc[:, :], ACT.Abs), a)
    a2 = act.do(lambda e: e.activation(ce[:, :], ce[:, :], ACT.Exp, scale=-1.0), a1)
    a2 = act.do(lambda e: e.activation(ce[:, :], ce[:, :], ACT.Ln, bias=1.0), a2)
    d = dve.do(lambda e: e.tensor_scalar(cc[:, :], cc[:, :], 0.0, None, ALU.min), a1)
    d = dve.do(lambda e: e.tensor_tensor(out=ce[:, :], in0=cc[:, :], in1=ce[:, :], op=ALU.subtract), d, a2)
    d = dve.do(lambda e: e.memset(cc[:, :], 1.0), d)
    c_sum = dve.do(lambda e: e.tensor_tensor_scan(cc[:, :], cc[:, :], ce[:, :], 0.0, ALU.mult, ALU.add), d)
    d = dve.do(lambda e: e.tensor_scalar(ce[:, :], cc[:, :], -1.0, None, ALU.mult), c_sum)
    c_st = load("cst_", cd, ce[:, :], d)

    def pool_differences():
        tok = None
        for g, win in enumerate((2, 4, 8, 16)):
            src, width, i = u2[:, g, :], 1, 0
            while width < win:
                dst = (pA, pB)[i % 2]
                a = dve.do(lambda e: e.tensor_tensor(out=dst[:, width:], in0=src[:, width:], in1=src[:, :T - width], op=ALU.add),
                           tok, u_in)
                tok = dve.do(lambda e: e.tensor_copy(dst[:, 0:width], src[:, 0:width]), tok)
                tok = (tok[0], max(tok[1], a[1]))
                src, width, i = dst, 2 * width, i + 1
                yield
            a = dve.do(lambda e: e.tensor_tensor(out=src[:, 0:16], in0=src[:, 0:16], in1=pr[:, 16 * g:16 * g + 16], op=ALU.mult), tok, pr_ok)
            a = dve.do(lambda e: e.tensor_tensor(out=pd[:, g, 0:16], in0=src[:, 0:16], in1=u2[:, g, 0:16], op=ALU.subtract), a, yd_ok[7])
            tok = dve.do(lambda e: e.scalar_tensor_tensor(pd[:, g, 16:], src[:, 16:], 1.0 / win, u2[:, g, 16:], ALU.mult, ALU.subtract))
            yield

    def qk_products():
        for m in range(4):
            yield from feature_major("q_2", m, yhi, ylo, scaled_to(q2[:, m, :], 0.125, *freeF))
            if m == 0:
                b, P, f = banks.take()
                pe.wait(f, c_sum)
                for t in range(NT):
                    tok = pe.do(lambda e: e.transpose(P[:, 8 * t:8 * t + 8], cc[:, 128 * t:128 * t + 128], ident[0:8, 0:8]))
                banks.give(b, dve.do(lambda e: e.tensor_copy(cT[:, :], P[:, 0:64]), tok))
                qk_["cT"] = dve.now()
            yield from feature_major("k_2", m, yhi, ylo, scaled_to(k2[:, m, :], 1.0, *freeF))

    qk_ = {}
    interleave(qk_products(), pool_differences(), 1.5)
    cT_ok = qk_["cT"]
    qk_ok, pd_ok = act.now(), dve.now()

    QS = [at(f"QS{i}", XO + 4 * i, [128, T], F32R) for i in range(2)]
    KH = [at(f"KH{i}", XO + 8 + 4 * i, [128, T], F32R) for i in range(2)]
    KL = [at(f"KL{i}", XO + 16 + 4 * i, [128, T], F32R) for i in range(2)]
    nb = [at(f"nb{i}", XO + 24 + 4 * i, [128, T]) for i in range(2)]
    for vh in range(2):
        def ev(t, P, tok):
            hi_, lo_ = vhi[:, t, 256 * vh:256 * vh + 256], vlo[:, t, 256 * vh:256 * vh + 256]
            a = act.do(lambda e: e.activation(hi_, P[:, 0:256], ACT.Copy), tok, pd_ok, mask_ok)
            return dve.do(lambda e: e.tensor_tensor(out=lo_, in0=P[:, 0:256], in1=hi_.bitcast(F32), op=ALU.subtract), a)
        run(token_major("v_2", 256 * vh, yhi, ylo, ev))
    v_ok = dve.now()
    y_dead = pe.now()

    chi = [at(f"chi{k}", HO + 4 * k, [128, T], F32R) for k in range(4)] + \
          [at("chi4", HO + 32, [128, T], F32R), at("chi5", HO + 40, [128, T], F32R),
           at("chi6", FO + 4, [128, T], F32R), at("chi7", FO + 8, [128, T], F32R)]
    clo = [at(f"clo{k}", HO + 16 + 4 * k, [128, T], F32R) for k in range(4)] + \
          [at("clo4", HO + 36, [128, T], F32R), at("clo5", HO + 44, [128, T], F32R),
           at("clo6", FO + 20, [128, T], F32R), at("clo7", FO + 24, [128, T], F32R)]
    cat_ok = {}
    for g in range(4):
        for half in range(2):
            c = slice(512 * half, 512 * half + 512)
            b, P, f = banks.take()
            pe.wait(f, pd_ok, pw_ok)
            tok = pe.do(lambda e: e.matmul(P[:, :], pw[:, g, :], pd[:, g, c], start=True, stop=True))
            s = st[:, 152 + g:153 + g]
            h_ = act.do(lambda e: e.activation(chi[g][:, c], P[:, :], ACT.Copy, scale=s), tok, ps_ok, y_dead)
            l_ = dve.do(lambda e: e.scalar_tensor_tensor(clo[g][:, c], P[:, :], s, chi[g][:, c].bitcast(F32),
                                                         ALU.mult, ALU.subtract), h_)
            banks.give(b, l_)
        cat_ok[g] = l_
    pd_dead = pe.now()

    sx = [[at(f"sx{i}{j}", HO + 48 + 8 * i + 4 * j, [128, T]) for j in range(2)] for i in range(2)] + \
         [[at("sx20", FO, [128, T]), at("sx21", FO + 16, [128, T])]]
    PH = [at(f"PH{i}", FO + 64 + 2 * i, [128, 512], F32R) for i in range(2)]
    PL = [at(f"PL{i}", FO + 68 + 2 * i, [128, 512], F32R) for i in range(2)]
    s_free, p_free2, fa = [None] * 3, [(pd_dead, c_st, cT_ok)] * 2, {"n": 0}
    items = [(t, i) for t in range(4) for i in range(8)]
    nb_ok, stack_ok = {}, {}

    def fetch_nb(t, *tokens):
        for j in range(2):
            nb_ok[2 * t + j] = load(f"nb{j}", nb[j][:, :], cd[2 * t + j].partition_broadcast(128), c_st, *tokens)

    def stack(t, *tokens):
        for j in range(2):
            own, other = slice(64 * j, 64 * j + 64), slice(64 - 64 * j, 128 - 64 * j)
            q, k = q2[own, t, :], k2[own, t, :]
            a = act.do(lambda e: e.activation(QS[j][own, :], q, ACT.Copy), qk_ok, *tokens)
            b_ = act.do(lambda e: e.activation(KH[j][own, :], k, ACT.Copy))
            act.do(lambda e: e.activation(KH[j][other, :], k, ACT.Copy))
            dve.do(lambda e: e.tensor_tensor(out=QS[j][other, :], in0=q, in1=QS[j][own, :].bitcast(F32), op=ALU.subtract), a)
            dve.do(lambda e: e.tensor_tensor(out=KL[j][own, :], in0=k, in1=KH[j][own, :].bitcast(F32), op=ALU.subtract), b_)
            dve.do(lambda e: e.tensor_tensor(out=KL[j][other, :], in0=k, in1=KH[j][own, :].bitcast(F32), op=ALU.subtract))
            stack_ok[2 * t + j] = (act.now(), dve.now())

    def scores(idx):
        t, i = items[idx]
        nk = 128 * (i + 1)
        for c0 in range(0, nk, 512):
            for j in range(2):
                w = min(512, nk - c0)
                diag = c0 + w == nk
                b, P, f = banks.take()
                pe.wait(f, *stack_ok[2 * t + j])
                pe.run(lambda e: e.matmul(P[:, 0:w], QS[j][:, 128 * i:128 * i + 128], KH[j][:, c0:c0 + w], start=True, stop=False))
                g = lambda e: e.matmul(P[:, 0:w], QS[j][:, 128 * i:128 * i + 128], KL[j][:, c0:c0 + w], start=False, stop=not diag)
                if diag:
                    pe.wait(mask_ok)
                    pe.run(g)
                    tok = pe.do(lambda e: e.matmul(P[:, w - 128:w], identb[:, :], maskb[:, :], start=False, stop=True))
                else:
                    tok = pe.do(g)
                scored.append((idx, j, c0, w, b, P, tok))
        if i == 7 and t < 3:
            fa["stack"] = (t + 1, pe.now())

    def maxima(idx):
        t, i = items[idx]
        nk = 128 * (i + 1)
        prev = {0: NEG, 1: NEG}
        mine = [x for x in scored if x[0] == idx]
        scored.clear()
        for _, j, c0, w, b, P, tok in mine:
            s = sx[idx % 3][j]
            col = 8 * (idx % 3) + 4 * j
            mo = st[:, col + c0 // 512:col + c0 // 512 + 1]
            fa["max"] = dve.do(lambda e: e.tensor_tensor_reduce(
                out=s[:, c0:c0 + w], in0=P[:, 0:w], in1=nb[j][:, c0:c0 + w], scale=1.0, scalar=prev[j], op0=ALU.add,
                op1=ALU.max, accum_out=mo), tok, nb_ok[2 * t + j], s_free[idx % 3], chunk_ok.get((idx, j)), y_dead, *stack_ok[1])
            chunk_ok[idx, j] = fa["max"]
            banks.give(b, fa["max"])
            prev[j] = mo
            yield
        for j in range(2):
            cq = cT[:, 8 * i + 2 * t + j:8 * i + 2 * t + j + 1]
            nm = st[:, 8 * (idx % 3) + 4 * j + 2:8 * (idx % 3) + 4 * j + 3]
            shift_ok[idx] = dve.do(lambda e: e.scalar_tensor_tensor(nm, prev[j], cq, cq, ALU.add, ALU.subtract, reverse1=True),
                                   fa["max"], cT_ok)
        if "stack" in fa:
            t2, used = fa.pop("stack")
            fetch_nb(t2, fa["max"])
            stack(t2, used)

    def exponents(idx):
        t, i = items[idx]
        nk = 128 * (i + 1)
        for j in range(2):
            s = sx[idx % 3][j]
            col = 8 * (idx % 3) + 4 * j
            exp_ok[idx, j] = act.do(lambda e: e.activation(s[:, 0:nk], s[:, 0:nk], ACT.Exp, bias=st[:, col + 2:col + 3],
                                                           accum_out=st[:, col + 3:col + 4]), shift_ok[idx])

    def normalise(idx):
        t, i = items[idx]
        nk = 128 * (i + 1)
        out_ = []
        for j in range(2):
            s = sx[idx % 3][j]
            ls = st[:, 8 * (idx % 3) + 4 * j + 3:8 * (idx % 3) + 4 * j + 4]
            r = dve.do(lambda e: e.reciprocal(ls, ls), exp_ok[idx, j])
            on = pool if j else dve
            out_.append(on.do(lambda e: e.tensor_scalar(s[:, 0:nk], s[:, 0:nk], ls, None, ALU.mult), r))
        return out_

    scored, shift_ok, exp_ok, chunk_ok = [], {}, {}, {}

    def transposed(idx, q, ready):
        t, i = items[idx]
        b, P, f = banks.take()
        pe.wait(f, *ready)
        ks_ = range(2 * q, min(2 * q + 2, i + 1))
        for k in ks_:
            for j in range(2):
                c = 256 * (k - 2 * q) + 128 * j
                tok = pe.do(lambda e: e.transpose(P[:, c:c + 128], sx[idx % 3][j][:, 128 * k:128 * k + 128], ident[:, :]))
        s_free[idx % 3] = tok
        p = fa["n"] % 2
        fa["n"] += 1
        w = 256 * len(ks_)
        a = act.do(lambda e: e.activation(PH[p][:, 0:w], P[:, 0:w], ACT.Copy), tok, *p_free2[p])
        d = dve.do(lambda e: e.tensor_tensor(out=PL[p][:, 0:w], in0=P[:, 0:w], in1=PH[p][:, 0:w].bitcast(F32), op=ALU.subtract), a)
        banks.give(b, d)
        return ks_, p, (a, d)

    def weighted(idx, O, part):
        t, i = items[idx]
        ks_, p, ok = part
        pe.wait(*ok)
        for k in ks_:
            c = 256 * (k - ks_[0])
            v = slice(128 * t, 128 * t + 128)
            args = [(vhi, PH, k == 0, False), (vhi, PL, False, False), (vlo, PH, False, k == i)]
            for V, Q, first, last in args:
                tok = pe.do(lambda e: e.matmul(O[:, 0:256], V[:, k, v], Q[p][:, c:c + 256], start=first, stop=last))
        p_free2[p] = (tok,)
        return tok

    fetch_nb(0, yd_ok[7])
    stack(0, pd_dead)
    pe.wait(v_ok)
    scores(0)
    run(maxima(0))
    exponents(0)
    scores(1)
    run(maxima(1))
    ready = normalise(0)
    for idx in range(32):
        t, i = items[idx]
        if idx < 31:
            exponents(idx + 1)
        mx = iter(())
        if idx < 30:
            scores(idx + 2)
            mx = maxima(idx + 2)
        ob, O, of = banks.take()
        n = (i + 2) // 2
        part = transposed(idx, 0, ready)
        pe.wait(of)
        for q in range(n):
            nxt = transposed(idx, q + 1, ready) if q + 1 < n else None
            next(mx, None)
            if q == 0 and idx < 31:
                later = normalise(idx + 1)
            tok = weighted(idx, O, part)
            part = nxt
        run(mx)
        for j in range(2):
            r = slice(64 * j, 64 * j + 64)
            hi_, lo_ = chi[4 + t][r, 128 * i:128 * i + 128], clo[4 + t][r, 128 * i:128 * i + 128]
            src = O[r, 128 * j:128 * j + 128]
            a = act.do(lambda e: e.activation(hi_, src, ACT.Copy), tok, y_dead, *stack_ok[2 * t + 1])
            last = dve.do(lambda e: e.tensor_tensor(out=lo_, in0=src, in1=hi_.bitcast(F32), op=ALU.subtract), a)
        banks.give(ob, last)
        cat_ok[4 + t] = last
        ready = later

    zhi, zlo = H("z")
    lg = at("lg", FO + 32, [128, D])
    lb = at("lb", FO + 36, [128, D])
    lx = [at(f"lx{i}", FO + 40 + 4 * i, [128, D]) for i in range(3)]
    yr = [at(f"yr{i}", FO + 52 + 4 * i, [128, D]) for i in range(3)]
    a_dead = (pe.now(), act.now(), dve.now())
    yr_free, yr_ok = [a_dead] * 3, {}

    def fetch_y(t):
        if t < NT:
            yr_ok[t] = load(f"yr{t % 3}", yr[t % 3][:, :], yd[t], yd_ok[7], *yr_free[t % 3])

    def seed(t):
        if t not in seeded:
            seeded.add(t)
            if t > 0:
                yr_free[(t - 1) % 3] = (dve.now(),)
                fetch_y(t + 2)
        return yr[t % 3], yr_ok[t]

    seeded = set()
    for t in range(3):
        fetch_y(t)
    row_ok = load("row", lg[:, :], rows[4].partition_broadcast(128), *a_dead)
    row_ok = load("row", lb[:, :], rows[5].partition_broadcast(128))
    lns, z_ok, lx_free, z2_ok = {}, {}, [(), (), ()], {}

    def l_stats(t):
        d = accd[t]
        for c in range(2):
            d = dve.do(lambda e: e.bn_stats(st[:, 12 * t + 6 * c:12 * t + 6 * c + 6], acc[:, t, 512 * c:512 * c + 512]), d, dve.now())
        d = dve.do(lambda e: e.bn_aggr(st[:, 96 + 4 * t:98 + 4 * t], st[:, 12 * t:12 * t + 12]), d)
        v = st[:, 97 + 4 * t:98 + 4 * t]
        d = dve.do(lambda e: e.tensor_scalar(v, v, 1.0, LN_EPS, ALU.mult, ALU.add), d)
        lns[t] = act.do(lambda e: e.activation(v, v, ACT.Sqrt), d)

    def l_scale(t, dst, gain, row, *tokens):
        m, v = st[:, 96 + 4 * t:97 + 4 * t], st[:, 97 + 4 * t:98 + 4 * t]
        r = dve.do(lambda e: e.reciprocal(v, v), lns[t])
        d = dve.do(lambda e: e.tensor_scalar(dst, acc[:, t, :], m, v, ALU.subtract, ALU.mult), r, *tokens)
        lns[t] = pool.do(lambda e: e.tensor_tensor(out=dst, in0=dst, in1=gain[:, :], op=ALU.mult), d, row)

    def l_bias(t, dst, bias, row):
        lns[t] = dve.do(lambda e: e.tensor_tensor(out=dst, in0=dst, in1=bias[:, :], op=ALU.add), lns[t], row)

    def l_transpose(t):
        r, z_ok[t] = transpose_split(lx[t % 3], t, zhi, zlo, (lns[t],), (lnx[0],))
        z2_ok[t] = act.do(lambda e: e.activation(acc[:, t, :], lx[t % 3][:, :], ACT.Copy, scale=ALPHA), lns[t])
        lx_free[t % 3] = (r, z2_ok[t])

    lnx = [None]
    ln1 = Pipeline(NT, l_stats, lambda t: l_scale(t, lx[t % 3][:, :], lg, row_ok, *lx_free[t % 3]),
                   lambda t: l_bias(t, lx[t % 3][:, :], lb, row_ok), l_transpose)

    def ln1_after(t, tok):
        accd[t] = tok
        ln1.push()

    for g in range(4):
        pe.wait(cat_ok[2 * g], cat_ok[2 * g + 1])
        lnx[0] = pe.now()
        run(rows_group("w_out_2", [2 * g, 2 * g + 1], lambda k: (chi[k], clo[k]), acc, a_dead, ln1_after if g == 3 else None,
                       seed if g == 0 else None) if g == 0 else
            rows_group("w_out_2", [2 * g, 2 * g + 1], lambda k: (chi[k], clo[k]), acc, False, ln1_after if g == 3 else None))

    fg = at("fg", FO + 32, [128, D])
    fb = at("fb", FO + 36, [128, D])
    frow = load("row", fg[:, :], rows[6].partition_broadcast(128), dve.now(), pool.now(), act.now(), pe.now())
    frow = load("row", fb[:, :], rows[7].partition_broadcast(128))
    outs = []

    def o_out(t):
        outs.append(load("out", out[128 * t:128 * t + 128, :], acc[:, t, :], lns[t]))

    ln2 = Pipeline(NT, l_stats, lambda t: l_scale(t, acc[:, t, :], fg, frow), lambda t: l_bias(t, acc[:, t, :], fb, frow), o_out)

    def ln2_after(t, tok):
        accd[t] = tok
        ln2.push()

    free2 = (pe.now(), act.now(), dve.now(), pool.now())
    mlp("w_mlp1", "w_mlp2", zhi, zlo, z_ok, acc, False, ln2_after, free2, "b")
    sp.wait(outs[-1])
    assert W["cur"] == NPIECES, W["cur"]

    return descs


def pack(inputs, descs):
    cuts = {}
    edge = np.cumsum([0, 512, 512, 1024, 1024, 512, 128, 128, 1024, 1024])
    w_in = inputs["w_in"][0]
    for name, a, b in zip(("q_r", "k_r", "v_r", "g_r", "q_s", "k_s", "v_s", "gate_r", "gate_s"), edge[:-1], edge[1:]):
        cuts[name] = w_in[:, a:b]
    heads = [h for m in range(4) for h in (m, 4 + m)]
    cuts["q_s"] = cuts["q_s"].reshape(1024, 8, 64)[:, heads].reshape(1024, 512)
    cuts["w_swa_out"] = inputs["w_swa_out"][0].reshape(8, 64, 1024)[heads].reshape(512, 1024)
    w2 = inputs["w_in_2"][0]
    for i, name in enumerate(("u_2", "q_2", "k_2", "v_2")):
        cuts[name] = w2[:, 512 * i:512 * i + 512]
    for name, key in (("w_ret_out",) * 2, ("w_out",) * 2, ("w_up",) * 2, ("w_down",) * 2, ("w_out_2",) * 2,
                      ("w_mlp1", "w_mlp1_2"), ("w_mlp2", "w_mlp2_2")):
        cuts[name] = inputs[key][0]
    wp = np.empty((len(descs), 128, 1024), np.float32)
    for n, d in enumerate(descs):
        w = cuts[d[1]]
        if d[0] == "F":
            wp[n].reshape(128, 8, 128)[:] = w[:, 128 * d[2]:128 * d[2] + 128].reshape(8, 128, 128).transpose(1, 0, 2)
        elif d[0] == "T":
            wp[n].reshape(128, 4, 256)[:] = w[128 * d[3]:128 * d[3] + 512, d[2]:d[2] + 256].reshape(4, 128, 256).transpose(1, 0, 2)
        elif d[0] == "D":
            wp[n] = w[128 * d[2]:128 * d[2] + 128]
        else:
            wp[n].reshape(128, 2, 4, 128)[:] = w[:, 256 * d[2]:256 * d[2] + 256].reshape(4, 128, 2, 128).transpose(1, 2, 0, 3)
    return wp


def kernel(**inputs):
    import concourse.bacc as _bacc
    from concourse.bass_utils import run_bass_kernel_spmd as _run

    inputs = {k: np.asarray(v) for k, v in inputs.items()}
    nc = _bacc.Bacc("TRN2", target_bir_lowering=False, num_devices=1, dynamic_dma_scratch_size=1024)
    cst, swab = constants()
    arrays = {
        "x_d": np.ascontiguousarray(inputs["x"][0]),
        "rows_d": np.concatenate([inputs[n] for n in ("pre_mix_norm", "post_mix_norm", "pre_mlp_norm", "post_mlp_norm",
                                                      "ln1_g_2", "ln1_b_2", "ln2_g_2", "ln2_b_2")]),
        "cst_d": cst,
        "swab_d": swab,
        "sinks_d": np.ascontiguousarray(inputs["sinks"][0]),
        "bf_d": np.ascontiguousarray(inputs["b_f_2"][0].reshape(8, 1)),
        "ps_d": np.ascontiguousarray(inputs["pool_scale_2"][0].reshape(4, 128).T),
        "pw_d": np.ascontiguousarray(inputs["pool_w_2"][0].transpose(1, 0, 2)),
        "wf_d": np.ascontiguousarray(inputs["w_in_2"][0][:, 2048:].reshape(8, 128, 8).transpose(1, 0, 2).reshape(128, 64)),
    }
    I = {n: nc.dram_tensor(n, a.shape, F32, kind="ExternalInput").ap() for n, a in arrays.items()}
    I["wp_d"] = nc.dram_tensor("wp_d", (NPIECES, 128, 1024), F32, kind="ExternalInput").ap()
    out = nc.dram_tensor("out_d", (T, D), F32, kind="ExternalOutput").ap()
    sg = nc.dram_tensor("sg_d", (16, 128, T), F32, kind="Internal").ap()
    cd = nc.dram_tensor("cd_d", (8, T), F32, kind="Internal").ap()
    yd = nc.dram_tensor("yd_d", (NT, 128, D), F32, kind="Internal").ap()
    descs = build(nc, I["wp_d"], I["x_d"], I["rows_d"], {"sinks": I["sinks_d"], "b_f": I["bf_d"], "pool_scale": I["ps_d"]},
                  I["cst_d"], I["swab_d"], I["pw_d"], I["wf_d"], out, sg, cd, yd)
    arrays["wp_d"] = pack(inputs, descs)
    r = _run(nc, [arrays], core_ids=[0])
    return r.results[0]["out_d"].reshape(1, T, D)
```

```python
from contextlib import ExitStack

import numpy as np
import concourse.bass as bass
from concourse import mybir

F32 = mybir.dt.float32
F32R = mybir.dt.float32r
BF16 = mybir.dt.bfloat16
ACT = mybir.ActivationFunctionType
ALU = mybir.AluOpType

T = 1024
D = 1024
NT = 8
ALPHA = float(2.0 ** 0.25)
EPS = 1e-6
LN_EPS = 1e-5
NEG = -1e30
NPIECES = 218
SLOTS = 5
RAWS = 3
CW = 128 + 128 + 512 + 512 + 4 + 64 + 256


def constants():
    c = np.zeros((128, CW), np.float64)
    i = np.arange(128)
    c[:, 0:128] = np.eye(128)
    c[:, 128:256] = np.where(i[None, :] > i[:, None], NEG, 0.0)
    for h in range(4):
        lg = np.log(1.0 - 2.0 ** (-5.0 - h))
        diff = i[None, :] - i[:, None]
        c[:, 256 + 128 * h:384 + 128 * h] = np.where(diff >= 0, np.exp(lg * np.maximum(diff, 0)), 0.0) * 128 ** -0.5
        c[:, 768 + 128 * h:896 + 128 * h] = np.exp(lg * (i + 1.0))[None, :]
        c[:, 1280 + h] = np.exp(lg * (127.0 - i)) * 128 ** -0.5
    for g, win in enumerate((2, 4, 8, 16)):
        c[:, 1284 + 16 * g:1300 + 16 * g] = 1.0 / np.minimum(np.arange(16) + 1.0, win)
    for j in range(2):
        for p in (0, 32):
            c[p + 2 * j:p + 2 * j + 2, 1348 + 128 * j:1476 + 128 * j] = 1.0
    b = np.zeros((128, 8, 256), np.float64)
    dist = (i[:, None] + 128) - np.arange(256)[None, :]
    for h in range(8):
        b[:, h, :] = np.where((dist >= 0) & (dist < 128), -(2.0 ** -(h + 1.0)) * dist, NEG)
    return c.astype(np.float32), b.reshape(128, 2048).astype(np.float32)


class Engine:

    def __init__(self, sem, e):
        self.sem, self.e, self.count, self.seen = sem, e, 0, {}

    def wait(self, *tokens):
        for t in tokens:
            if t is None:
                continue
            sem, value = t
            if self.seen.get(id(sem), 0) >= value:
                continue
            self.seen[id(sem)] = value
            if self.e is not None:
                self.e.wait_ge(sem, value)

    def do(self, f, *tokens):
        self.wait(*tokens)
        self.count += 1
        if self.e is not None:
            f(self.e).then_inc(self.sem, 1)
        return (self.sem, self.count)

    def run(self, f):
        if self.e is not None:
            f(self.e)

    def now(self):
        return (self.sem, self.count) if self.count else None


class Banks:
    def __init__(self, tensors):
        self.t, self.freed = tensors, [None] * len(tensors)
        self.turn(range(len(tensors)))

    def turn(self, order):
        self.order, self.at = list(order), 0

    def take(self):
        b = self.order[self.at]
        self.at = (self.at + 1) % len(self.order)
        return b, self.t[b], self.freed[b]

    def give(self, b, token):
        self.freed[b] = token


class Pipeline:

    def __init__(self, n, *stages):
        self.n, self.stages, self.step = n, stages, 0

    def push(self):
        for lag in reversed(range(len(self.stages))):
            t = self.step - lag
            if 0 <= t < self.n:
                self.stages[lag](t)
        self.step += 1

    def rest(self):
        for _ in range(len(self.stages) - 1):
            self.push()
            yield


def interleave(main, side, ratio):
    live = [main, side]
    credit = 0.0
    while live:
        if main in live:
            credit += 1.0
            try:
                next(main)
            except StopIteration:
                live.remove(main)
        else:
            credit += 1e9
        while side in live and credit >= ratio:
            credit -= ratio
            try:
                next(side)
            except StopIteration:
                live.remove(side)
            if main not in live:
                credit = 1e9


def build(nc, wp, x_in, rows, small, cst, swab, poolw, wf, out, sg, cd, yd):
    args = (wp, x_in, rows, small, cst, swab, poolw, wf, out, sg, cd, yd)
    with ExitStack() as ctx:
        bank_t = [ctx.enter_context(nc.psum_tensor(f"bank{i}", [128, 512], F32)) for i in range(8)]
        block = ctx.enter_context(nc.Block())
        made, sems, said = {}, {}, []
        for reg, name in ((block.sync, "sp"), (block.scalar, "act"), (block.vector, "dve"), (block.gpsimd, "pool"),
                          (block.tensor, "pe")):
            @reg
            def _(e, name=name):
                said.append(program(nc, ctx, bank_t, made, sems, name, e, *args))
    assert all(d == said[0] for d in said)
    return said[0]


def program(nc, ctx, bank_t, made, sems, turn, engine, wp, x_in, rows, small, cst, swab, poolw, wf, out, sg, cd, yd):
    base = (nc.sbuf_base + 31) // 32 * 32

    def at(name, kb, shape, dt=F32):
        if name not in made:
            made[name] = nc.alloc_sbuf_tensor_at(name, shape, dt, offset=base + int(kb * 1024))
        return made[name]

    def sem(name):
        if name not in sems:
            sems[name] = ctx.enter_context(nc.semaphore(name))
        return sems[name]

    banks = Banks(bank_t)
    pe, act, dve, pool, sp = (Engine(sem(f"s_{n}"), engine if n == turn else None) for n in ("pe", "act", "dve", "pool", "sp"))
    descs = []
    mark = {}

    XO, WO, RO, HO, CO, FO = 0, 32, 72, 84, 148, 149.625
    X = at("X", XO, [128, NT, D])
    whi = [at(f"whi{i}", WO + 4 * i, [128, 1024], F32R) for i in range(SLOTS)]
    wlo = [at(f"wlo{i}", WO + 20 + 4 * i, [128, 1024], F32R) for i in range(SLOTS)]
    raw = [at(f"raw{i}", RO + 4 * i, [128, 1024]) for i in range(RAWS)]
    ident = at("ident", CO, [128, 128])
    identb = at("identb", CO + 0.5, [128, 128], BF16)
    maskb = at("maskb", CO + 0.75, [128, 128], BF16)
    st = at("st", CO + 1, [128, 160])

    def H(name):
        return at(name + "hi", HO, [128, NT, T], F32R), at(name + "lo", HO + 32, [128, NT, T], F32R)

    def dma(dst, src, s, value, *tokens):
        sp.wait(*tokens)
        sp.run(lambda e: e.dma_start(dst, src).then_inc(s, 16))
        return (s, value)

    loads = {}

    def load(name, dst, src, *tokens):
        s = loads.setdefault(name, [sem("l_" + name), 0])
        s[1] += 16
        return dma(dst, src, s[0], s[1], *tokens)

    raw_sem = [sem(f"raw_{i}") for i in range(RAWS)]
    fetched, split_tok, slot_free = {}, {}, {}
    W = {"cur": 0, "split": 0, "limit": NPIECES, "late": []}

    def fetch(n, *tokens):
        if n >= W["limit"]:
            W["late"] += [n] if n < NPIECES else []
            return
        tokens += split_tok[n - RAWS] if n >= RAWS else ()
        fetched[n] = dma(raw[n % RAWS][:, :], wp[n], raw_sem[n % RAWS], 16 * (n // RAWS + 1), *tokens)

    def split(n):
        r, s = raw[n % RAWS], n % SLOTS
        a = act.do(lambda e: e.activation(whi[s][:, :], r[:, :], ACT.Copy), fetched[n], slot_free.get(n - SLOTS))
        b = dve.do(lambda e: e.tensor_tensor(out=wlo[s][:, :], in0=r[:, :], in1=whi[s][:, :].bitcast(F32),
                                             op=ALU.subtract), a)
        split_tok[n] = (a, b)
        fetch(n + RAWS)

    def ahead(limit):
        while W["split"] < min(limit, NPIECES):
            split(W["split"])
            W["split"] += 1

    def piece(*desc):
        n = W["cur"]
        W["cur"] += 1
        descs.append(desc)
        ahead(n + 1)
        pe.wait(*split_tok[n])
        return n

    def done(n, token, depth=SLOTS):
        slot_free[n] = token
        ahead(min(n + SLOTS + 1, W["cur"] + depth))

    def hl(n):
        return whi[n % SLOTS], wlo[n % SLOTS]

    def mm3(out, sh, sl, mh, ml, first, last):
        pe.run(lambda e: e.matmul(out, sh, mh, start=first, stop=False))
        pe.run(lambda e: e.matmul(out, sh, ml, start=False, stop=False))
        f = lambda e: e.matmul(out, sl, mh, start=False, stop=last)
        if last:
            return pe.do(f)
        pe.run(f)

    def half_product(n, half, hi, lo, evac, *ready):
        wh, wl = hl(n)
        b, P, free = banks.take()
        pe.wait(free, *ready)
        for k in range(8):
            tok = mm3(P[:, :], wh[:, 128 * k:128 * k + 128], wl[:, 128 * k:128 * k + 128],
                      hi[:, k, 512 * half:512 * half + 512], lo[:, k, 512 * half:512 * half + 512], k == 0, k == 7)
            if k == 3:
                yield
        banks.give(b, evac(half, P, tok))
        if half == 1:
            done(n, tok)
        yield

    def feature_major(name, col, hi, lo, evac):
        n = piece("F", name, col)
        for half in range(2):
            yield from half_product(n, half, hi, lo, evac)

    def feature_major_start(name, cols, hi, lo, evacs, ready, rest=iter(())):
        ns = []
        for half in range(2):
            for c, evac in zip(cols, evacs):
                if half == 0:
                    ns.append(piece("F", name, c))
                    ahead(W["cur"] + 1)
                run(half_product(ns[cols.index(c)], half, hi, lo, evac, *ready[4 * half + 3]))
                next(rest, None)
            run(rest)

    def token_major(name, col, hi, lo, evac):
        ns = [piece("T", name, col, 0), piece("T", name, col, 4)]
        for t in range(NT):
            b, P, free = banks.take()
            pe.wait(free)
            for k in range(8):
                wh, wl = hl(ns[k // 4])
                c = 256 * (k % 4)
                tok = mm3(P[:, 0:256], hi[:, k, 128 * t:128 * t + 128], lo[:, k, 128 * t:128 * t + 128],
                          wh[:, c:c + 256], wl[:, c:c + 256], k == 0, k == 7)
            banks.give(b, evac(t, P, tok))
            if t == 7:
                for n in ns:
                    done(n, tok)
            yield

    def rows_group(name, ks, stat, acc, first, after=None, seed=None):
        mark["pre"] = pe.now()
        ns = [piece("D", name, k) for k in ks]
        for t in range(NT):
            for c in range(2):
                b, P, free = banks.take()
                pe.wait(free)
                for j, k in enumerate(ks):
                    wh, wl = hl(ns[j])
                    sh, sl = stat(k)
                    tok = mm3(P[:, :], sh[:, 128 * t:128 * t + 128], sl[:, 128 * t:128 * t + 128],
                              wh[:, 512 * c:512 * c + 512], wl[:, 512 * c:512 * c + 512], j == 0, j == len(ks) - 1)
                dst = acc[:, t, 512 * c:512 * c + 512]
                if seed is not None:
                    add, ok = seed(t)
                    a = dve.do(lambda e: e.tensor_tensor(out=dst, in0=P[:, :], in1=add[:, 512 * c:512 * c + 512], op=ALU.add),
                               tok, ok, *first)
                elif first:
                    a = act.do(lambda e, dst=dst, P=P: e.activation(dst, P[:, :], ACT.Copy), tok, *first)
                else:
                    a = dve.do(lambda e, dst=dst, P=P: e.tensor_tensor(out=dst, in0=P[:, :], in1=dst, op=ALU.add),
                               tok, act.now() if c == 0 and t == 0 else None, dve.now())
                banks.give(b, a)
            if t == 7:
                for n in ns:
                    done(n, tok, 2 if after else SLOTS)
            if after is not None:
                after(t, a)
            if t % 2:
                yield

    def run(gen):
        for _ in gen:
            pass

    def transpose_split(src, t, hi, lo, tokens, free=()):
        for q in range(2):
            b, P, f = banks.take()
            pe.wait(f, *tokens)
            for j in range(4):
                k = 4 * q + j
                g = lambda e, j=j, k=k, P=P: e.transpose(P[:, 128 * j:128 * j + 128], src[:, 128 * k:128 * k + 128], ident[:, :])
                if j == 3:
                    tok = pe.do(g)
                else:
                    pe.run(g)
            pv = P[:, :].rearrange("p (j c) -> p j c", j=4)
            oh = hi[:, 4 * q:4 * q + 4, 128 * t:128 * t + 128]
            ol = lo[:, 4 * q:4 * q + 4, 128 * t:128 * t + 128]
            a = act.do(lambda e, oh=oh, pv=pv: e.activation(oh, pv, ACT.Copy), tok, *free)
            d = dve.do(lambda e, oh=oh, ol=ol, pv=pv: e.tensor_tensor(out=ol, in0=pv, in1=oh.bitcast(F32), op=ALU.subtract), a)
            banks.give(b, d)
        return tok, (a, d)

    def rstd(src, dst, scale, eps, *tokens):
        a = dve.do(lambda e: e.tensor_scalar(dst, src, scale, eps, ALU.mult, ALU.add), *tokens)
        a = act.do(lambda e: e.activation(dst, dst, ACT.Sqrt), a)
        return dve.do(lambda e: e.reciprocal(dst, dst), a)

    xt = [load(f"x{t}", X[:, t, :], x_in[128 * t:128 * t + 128, :]) for t in range(4)]
    gb = at("gb0", FO + 56, [128, 1024])
    gb_ok = load("row", gb[:, :], rows[0].partition_broadcast(128))
    id_ok = load("id", ident[:, :], cst[:, 0:128])
    fetch(0)
    fetch(1)
    xt += [load(f"x{t}", X[:, t, :], x_in[128 * t:128 * t + 128, :]) for t in range(4, NT)]
    fetch(2)
    junk = at("junk0", FO + 60, [128, 1024])
    ht = [at(f"ht0{i}", FO + 64 + 4 * i, [128, 1024]) for i in range(2)]
    hhi, hlo = H("h")
    read = [None, None]
    rows_ok, sq_ok = {}, {}

    def s_squares(group):
        for t in group:
            sq_ok[t] = act.do(lambda e: e.activation(junk[:, :], X[:, t, :], ACT.Square, accum_out=st[:, t:t + 1]), xt[t], sq_ok.get(t - 1))

    def s_rstd(group):
        c = slice(group[0], group[-1] + 1)
        r = rstd(st[:, c], st[:, 8 + group[0]:9 + group[-1]], 1.0 / D, EPS, sq_ok[group[-1]])
        for t in group:
            sq_ok[t] = r

    def s_scale(t):
        sq_ok[t] = dve.do(lambda e: e.scalar_tensor_tensor(ht[t % 2][:, :], X[:, t, :], st[:, 8 + t:9 + t], gb[:, :],
                                                           ALU.mult, ALU.mult), sq_ok[t], gb_ok, read[t % 2])

    def s_transpose(t):
        read[t % 2], rows_ok[t] = transpose_split(ht[t % 2], t, hhi, hlo, (sq_ok[t], id_ok))

    def s_rest():
        for _ in range(3):
            start.push()
            yield
        yield from start.rest()

    start = Pipeline(NT, s_scale, s_transpose)
    s_squares([0, 1])
    s_rstd([0, 1])
    start.push()
    s_squares([2, 3])
    s_rstd([2, 3])
    start.push()
    start.push()
    s_squares([4, 5, 6, 7])
    s_rstd([4, 5, 6, 7])
    start.push()
    start.push()

    qs = at("qs", FO, [128, 4, T])
    ks = at("ks", FO + 16, [128, T])
    vs = at("vs", FO + 20, [128, NT, 128])
    sbias = at("sbias", FO + 24, [128, 8, 256])
    pt_ = [at(f"p{i}", FO + 32 + 8 * i, [128, 8, 256]) for i in range(2)]
    PT = [at(f"PT{i}", FO + 48 + 2 * i, [128, 512]) for i in range(4)]
    swa = at("swa", FO + 56, [128, 4, T])
    sig = [at(f"sig{i}", XO + 4 * i, [128, T]) for i in range(4)]
    vsT = at("vsT", XO + 16, [128, T])
    sb_ok = load("swab", sbias[:, :, :].rearrange("p h j -> p (h j)"), swab)
    sink_ok = load("sink", st[:, 16:24], small["sinks"].partition_broadcast(128))

    def scaled_to(dst, scale, *tokens):
        def evac(half, P, tok):
            return act.do(lambda e: e.activation(dst[:, 512 * half:512 * half + 512], P[:, :], ACT.Copy, scale=scale), tok, *tokens)
        return evac

    feature_major_start("q_s", [0, 1, 2, 3], hhi, hlo,
                        [scaled_to(qs[:, m, :], 0.125) for m in range(4)], rows_ok, s_rest())
    x_free = sq_ok[7]
    start_dead = (pe.now(), act.now())
    run(feature_major("k_s", 0, hhi, hlo, scaled_to(ks, 1.0)))
    run(feature_major("v_s", 0, hhi, hlo, scaled_to(vsT, 1.0, x_free)))
    vs_in = act.now()
    for q in range(2):
        b, P, f = banks.take()
        pe.wait(f, vs_in)
        for j in range(4):
            t = 4 * q + j
            tok = pe.do(lambda e, j=j, t=t, P=P: e.transpose(P[:, 128 * j:128 * j + 128], vsT[:, 128 * t:128 * t + 128], ident[:, :]))
        vs_ok = dve.do(lambda e, q=q, P=P: e.tensor_copy(vs[:, 4 * q:4 * q + 4, :].rearrange("p a c -> p (a c)"), P[:, :]), tok)
        banks.give(b, vs_ok)

    stages = {"gates": (sig, x_free)}
    sig_free = [None] * 4
    gate_ok = {}

    def gate_evac(index):
        i = index % 4
        toks = []

        def evac(half, P, tok):
            stage, ready = stages["gates"]
            v = stage[i][:, 512 * half:512 * half + 512]
            a = act.do(lambda e: e.activation(v, P[:, :], ACT.Tanh, scale=0.5), tok, sig_free[i], ready)
            p = pool.do(lambda e: e.tensor_scalar(v, v, 0.5, 0.5, ALU.mult, ALU.add), a)
            toks.append(p)
            if half == 1:
                sig_free[i] = gate_ok[index] = load(f"sg{i}", sg[index], stage[i][:, :], *toks)
            return a
        return evac

    def gates(which):
        for index in which:
            yield from feature_major("gate_s" if index < 8 else "gate_r", index % 8, hhi, hlo, gate_evac(index))

    p_free = [None, None]
    PT_free = [None] * 4
    ptn = [0]

    def swa_scores(n):
        p = pt_[n % 2]
        j0 = 128 if n == 0 else 0
        last = None
        for mm in range(2):
            pair = [banks.take(), banks.take()]
            for m in range(2 * mm, 2 * mm + 2):
                for g in range(2):
                    b, P, f = pair[g]
                    pe.wait(f, qs_ok)
                    tok = pe.do(lambda e: e.matmul(
                        P[:, 256 * (m % 2) + j0:256 * (m % 2) + 256], qs[64 * g:64 * g + 64, m, 128 * n:128 * n + 128],
                        ks[64 * g:64 * g + 64, 128 * n - 128 + j0:128 * n + 128], start=True, stop=True))
            for g in range(2):
                b, P, f = pair[g]
                for m in range(2 * mm, 2 * mm + 2):
                    h = 4 * g + m
                    last = dve.do(lambda e: e.tensor_tensor_reduce(
                        out=p[:, h, j0:256], in0=P[:, 256 * (m % 2) + j0:256 * (m % 2) + 256], in1=sbias[:, h, j0:256], scale=1.0,
                        scalar=st[:, 16 + h:17 + h], op0=ALU.add, op1=ALU.max, accum_out=st[:, 24 + h:25 + h]),
                        tok, sb_ok, sink_ok, p_free[n % 2], swa_nm[0])
                banks.give(b, last)
            yield
        nm = dve.do(lambda e: e.tensor_scalar(st[:, 32:40], st[:, 24:32], -1.0, None, ALU.mult), last, act.now())
        sk = dve.do(lambda e: e.tensor_tensor(out=st[:, 40:48], in0=st[:, 16:24], in1=st[:, 24:32], op=ALU.subtract), last)
        swa_nm[0] = sk
        for h in range(8):
            ex = act.do(lambda e, h=h: e.activation(p[:, h, j0:256], p[:, h, j0:256], ACT.Exp, bias=st[:, 32 + h:33 + h],
                                                    accum_out=st[:, 48 + h:49 + h]), nm, swa_nm[1])
        es = act.do(lambda e: e.activation(st[:, 40:48], st[:, 40:48], ACT.Exp), sk)
        a = dve.do(lambda e: e.tensor_tensor(out=st[:, 48:56], in0=st[:, 48:56], in1=st[:, 40:48], op=ALU.add), ex, es)
        a = dve.do(lambda e: e.reciprocal(st[:, 48:56], st[:, 48:56]), a)
        for h in range(8):
            a2 = dve.do(lambda e, h=h: e.tensor_scalar(p[:, h, j0:256], p[:, h, j0:256], st[:, 48 + h:49 + h], None, ALU.mult), a)
        swa_nm[1] = swa_ready[n] = a2

    swa_nm = [None, None]
    qs_ok = act.now()

    def swa_values(n):
        p = pt_[n % 2]
        O = banks.t[7]
        jts = [1] if n == 0 else [0, 1]
        waiting = []

        def product():
            g, jt_, i, a = waiting.pop()
            pe.wait(a, banks.freed[7], vs_ok)
            PT_free[i] = pe.do(lambda e: e.matmul(O[64 * g:64 * g + 64, :], vs[:, n - 1 + jt_, 64 * g:64 * g + 64],
                                                  PT[i][:, :], start=jt_ == jts[0], stop=jt_ == 1))

        for g in range(2):
            for jt_ in jts:
                b, P, f = banks.take()
                pe.wait(f, swa_ready[n])
                for r in range(4):
                    tok = pe.do(lambda e: e.transpose(P[:, 128 * r:128 * r + 128], p[:, 4 * g + r, 128 * jt_:128 * jt_ + 128],
                                                      ident[:, :]))
                i = ptn[0] % 4
                ptn[0] += 1
                a = act.do(lambda e: e.activation(PT[i][:, :], P[:, :], ACT.Copy), tok, PT_free[i])
                banks.give(b, a)
                if waiting:
                    product()
                waiting.append((g, jt_, i, a))
                yield
        p_free[n % 2] = tok
        product()
        d = dve.do(lambda e: e.tensor_copy(swa[:, :, 128 * n:128 * n + 128], O[:, :].rearrange("p (r c) -> p r c", r=4)), pe.now(), *start_dead)
        banks.give(7, d)
        yield

    def swa_all():
        yield from swa_scores(0)
        for n in range(8):
            if n < 7:
                yield from swa_scores(n + 1)
            yield from swa_values(n)

    swa_ready = {}
    banks.turn(range(7))
    interleave(gates(range(13)), swa_all(), 1.1)
    banks.turn(range(8))
    swa_ok = dve.now()
    swa_reads = (pe.now(), act.now(), dve.now())

    ret = at("ret", XO, [128, 8, T])
    rq = [at(f"rq{i}", FO + 4 * i, [128, T]) for i in range(2)]
    rk = [at(f"rk{i}", FO + 8 + 4 * i, [128, T]) for i in range(2)]
    rv = [at(f"rv{i}", FO + 16 + 8 * i, [128, NT, 256]) for i in range(2)]
    rg = at("rg", FO + 32, [128, 2, T])
    ro = at("ro", FO + 40, [128, NT, 256])
    dect = at("dect", FO + 48, [128, 1028])
    rs = [at(f"rs{i}", FO + 52.03125 + i, [128, 256]) for i in range(2)]
    ss = [at(f"ss{i}", FO + 54.03125 + 0.5 * i, [128, 128]) for i in range(2)]
    kd = at("kd", FO + 55.03125, [128, 128])
    rq2 = at("rq2", FO + 72, [128, 128])
    tb = at("tb", FO + 72.5, [128, 128])
    tab_ok = load("tab", dect[:, :], cst[:, 256:1284], *swa_reads)

    rfree = {"q": [None, None], "v": [None, None], "g": None, "o": None, "gs": None}
    rready = {}

    def ret_proj(h):
        i = h % 2
        run_ev = lambda dst, fr: scaled_to(dst, 1.0, fr, *swa_reads)
        yield from feature_major("q_r", h, hhi, hlo, run_ev(rq[i], rfree["q"][i]))
        yield from feature_major("k_r", h, hhi, hlo, run_ev(rk[i], rfree["q"][i]))

        def ev(t, P, tok):
            return act.do(lambda e: e.activation(rv[i][:, t, :], P[:, 0:256], ACT.Copy), tok, rfree["v"][i], *swa_reads)
        yield from token_major("v_r", 256 * h, hhi, hlo, ev)
        rready[h] = act.now()

    def ret_gate(h):
        for m in range(2):
            def ev(half, P, tok, m=m):
                v = rg[:, m, 512 * half:512 * half + 512]
                a = act.do(lambda e: e.activation(v, P[:, :], ACT.Tanh, scale=0.5), tok, rfree["g"], *swa_reads)
                a = pool.do(lambda e: e.tensor_scalar(v, v, 0.5, 0.5, ALU.mult, ALU.add), a)
                return dve.do(lambda e: e.tensor_tensor(out=v, in0=P[:, :], in1=v, op=ALU.mult), a)
            yield from feature_major("g_r", 2 * h + m, hhi, hlo, ev)
        rready["g"] = dve.now()

    def retention(h):
        i = h % 2
        gamma = 1.0 - 2.0 ** (-5.0 - h)
        decay = dect[:, 128 * h:128 * h + 128]
        qdec = dect[:, 512 + 128 * h:640 + 128 * h]
        kcol = dect[:, 1024 + h:1025 + h]
        qtmp = [rq2, tb]
        s_ok = rkv = None
        for n in range(8):
            c = slice(128 * n, 128 * n + 128)
            b, P, f = banks.take()
            pe.wait(f, rready[h])
            a = pe.do(lambda e: e.matmul(P[:, 0:128], rk[i][:, c], rq[i][:, c], start=True, stop=True))
            if n < 7:
                a = pe.do(lambda e: e.transpose(P[:, 128:256], rk[i][:, c], ident[:, :]))
            s1 = dve.do(lambda e: e.tensor_tensor(out=ss[n % 2][:, :], in0=P[:, 0:128], in1=decay, op=ALU.mult),
                        a, tab_ok, pe.now())
            if n > 0:
                q1 = dve.do(lambda e, n=n: e.tensor_tensor(out=qtmp[n % 2][:, :], in0=rq[i][:, c], in1=qdec, op=ALU.mult), s1)
            if n < 7:
                k1 = act.do(lambda e: e.activation(kd[:, :], P[:, 128:256], ACT.Copy, scale=kcol), a, s1, tab_ok, rkv)
                banks.give(b, k1)
            else:
                banks.give(b, s1)
            yield
            b, P, f = banks.take()
            pe.wait(f, s1)
            o = pe.do(lambda e, P=P: e.matmul(P[:, 0:256], ss[n % 2][:, :], rv[i][:, n, :], start=True, stop=n == 0))
            if n > 0:
                pe.wait(q1, s_ok)
                o = pe.do(lambda e, P=P: e.matmul(P[:, 0:256], qtmp[n % 2][:, :], rs[(n - 1) % 2][:, :], start=False, stop=True))
            if n < 7:
                b2, P2, f2 = banks.take()
                pe.wait(f2, k1)
                rkv = pe.do(lambda e, P2=P2: e.matmul(P2[:, 0:256], kd[:, :], rv[i][:, n, :], start=True, stop=True))
                if n == 0:
                    s_ok = dve.do(lambda e, P2=P2: e.tensor_copy(rs[0][:, :], P2[:, 0:256]), rkv)
                else:
                    s_ok = dve.do(lambda e, P2=P2: e.scalar_tensor_tensor(
                        rs[n % 2][:, :], rs[(n - 1) % 2][:, :], float(gamma ** 128), P2[:, 0:256], ALU.mult, ALU.add), rkv, s_ok)
                banks.give(b2, s_ok)
            a = act.do(lambda e, P=P: e.activation(ro[:, n, :], P[:, 0:256], ACT.Copy), o, rfree["o"])
            banks.give(b, a)
            bn = dve.do(lambda e: e.bn_stats(st[:, 24:30], ro[:, n, :]), a, dve.now())
            bn = dve.do(lambda e: e.bn_aggr(st[:, 32 + 2 * n:34 + 2 * n], st[:, 24:30]), bn)
            yield
        rfree["q"][i] = rfree["v"][i] = pe.now()
        mv = st[:, 32:48].rearrange("p (n two) -> p n two", two=2)
        r = rstd(mv[:, :, 1], st[:, 48:56], 1.0, EPS, bn)
        for n in range(8):
            d = dve.do(lambda e, n=n: e.tensor_scalar(ro[:, n, :], ro[:, n, :], st[:, 32 + 2 * n:33 + 2 * n],
                                                      st[:, 48 + n:49 + n], ALU.subtract, ALU.mult), r)
        yield
        yield
        for m in range(2):
            for q in range(2):
                b, P, f = banks.take()
                pe.wait(f, d)
                for j in range(4):
                    a = pe.do(lambda e, j=j, P=P: e.transpose(P[:, 128 * j:128 * j + 128],
                                                              ro[:, 4 * q + j, 128 * m:128 * m + 128], ident[:, :]))
                w = dve.do(lambda e, P=P: e.tensor_tensor(out=ret[:, 2 * h + m, 512 * q:512 * q + 512], in0=P[:, :],
                                                          in1=rg[:, m, 512 * q:512 * q + 512], op=ALU.mult),
                           a, rready["g"], *sig_free)
                banks.give(b, w)
            yield
        rfree["o"] = a
        rfree["g"] = w

    run(ret_proj(0))
    for h in range(4):
        def main(h=h):
            yield from ret_gate(h)
            if h < 3:
                yield from ret_proj(h + 1)
            else:
                stages["gates"] = ([at("lsig0", FO, [128, T]), at("lsig1", FO + 8, [128, T]), at("lsig2", FO + 16, [128, T]),
                                    at("lsig3", FO + 20, [128, T])], rfree["v"][0])
                yield from gates(range(13, 16))
        interleave(main(), retention(h), 1.2 if h < 3 else 1.0)
    ret_ok = retention_end = dve.now()

    h_dead = pe.now()
    rethi = at("rethi", HO, [128, 8, T], F32R)
    swahi = at("swahi", HO + 32, [128, 4, T], F32R)
    retlo = at("retlo", XO, [128, 8, T], F32R)
    swalo = at("swalo", FO + 56, [128, 4, T], F32R)
    Z = at("Z", FO, [128, 8, T])
    mlo = at("mlo", FO, [128, 8, T], F32R)
    gs = [at(f"gs{i}", FO + 32 + 4 * i, [128, T]) for i in range(4)]
    mp = [at("mp0", HO + 48, [128, 2, T], F32R), at("mp1", HO + 56, [128, 2, T], F32R),
          at("mp2", HO + 32, [128, 2, T], F32R), at("mp3", FO + 48, [128, 2, T], F32R)]
    gs_free = [None] * 4
    gl = {}
    F_free = (pe.now(), act.now(), dve.now(), gate_ok[13], gate_ok[14], gate_ok[15])

    def fetch_gate(n):
        if n < 16:
            gl[n] = load(f"gl{n % 4}", gs[n % 4][:, :], sg[n], gate_ok[n], gs_free[n % 4], *F_free)

    for n in range(4):
        fetch_gate(n)
    sw_ok = {}
    for m in range(4):
        a = act.do(lambda e, m=m: e.activation(swahi[:, m, :], swa[:, m, :], ACT.Copy), h_dead, swa_ok)
        sw_ok[m] = dve.do(lambda e, m=m: e.tensor_tensor(out=swalo[:, m, :], in0=swa[:, m, :], in1=swahi[:, m, :].bitcast(F32),
                                                         op=ALU.subtract), a)
    rt_ok = {}

    def split_ret(m):
        a = act.do(lambda e, m=m: e.activation(rethi[:, m, :], ret[:, m, :], ACT.Copy), h_dead, ret_ok)
        rt_ok[m] = dve.do(lambda e, m=m: e.tensor_tensor(out=retlo[:, m, :], in0=ret[:, m, :], in1=rethi[:, m, :].bitcast(F32),
                                                         op=ALU.subtract), a)
    for m2 in range(4):
        n = piece("S", "w_swa_out", m2)
        wh, wl = hl(n)
        for mm in range(2):
            m = 2 * m2 + mm
            for half in range(2):
                c = slice(512 * half, 512 * half + 512)
                b, P, f = banks.take()
                pe.wait(f)
                for k in range(4):
                    pe.wait(sw_ok[k])
                    w0 = 512 * mm + 128 * k
                    tok = mm3(P[:, :], wh[:, w0:w0 + 128], wl[:, w0:w0 + 128], swahi[:, k, c], swalo[:, k, c], k == 0, k == 3)
                z = dve.do(lambda e, P=P, c=c, m=m: e.tensor_tensor(out=Z[:, m, c], in0=P[:, :], in1=gs[m % 4][:, c], op=ALU.mult),
                           tok, gl[m], *F_free)
                banks.give(b, z)
            gs_free[m % 4] = z
            fetch_gate(m + 4)
            split_ret(m)
        done(n, tok)
    swa_dead = pe.now()
    m_ok = {}
    for m in range(8):
        n = piece("F", "w_ret_out", m)
        wh, wl = hl(n)
        for half in range(2):
            c = slice(512 * half, 512 * half + 512)
            b, P, f = banks.take()
            pe.wait(f)
            for k in range(8):
                pe.wait(rt_ok[k])
                tok = mm3(P[:, :], wh[:, 128 * k:128 * k + 128], wl[:, 128 * k:128 * k + 128], rethi[:, k, c], retlo[:, k, c],
                          k == 0, k == 7)
            g = gs[m % 4]
            z = dve.do(lambda e, P=P, c=c, g=g: e.tensor_tensor(out=g[:, c], in0=P[:, :], in1=g[:, c], op=ALU.mult), tok, gl[8 + m])
            banks.give(b, z)
            z = pool.do(lambda e, c=c, m=m, g=g: e.tensor_tensor(out=Z[:, m, c], in0=Z[:, m, c], in1=g[:, c], op=ALU.add), z)
            hi_ = mp[m // 2][:, m % 2, c]
            a = act.do(lambda e, hi_=hi_, c=c, m=m: e.activation(hi_, Z[:, m, c], ACT.Copy), z, swa_dead)
            m_ok[m] = dve.do(lambda e, hi_=hi_, c=c, m=m: e.tensor_tensor(out=mlo[:, m, c], in0=Z[:, m, c], in1=hi_.bitcast(F32),
                                                                          op=ALU.subtract), a)
        done(n, tok)
        gs_free[m % 4] = z
        fetch_gate(8 + m + 4)
    ret_dead = pe.now()

    acc = at("accX", XO, [128, NT, D])
    xs = [at(f"xs{i}", FO + 32 + 4 * i, [128, D]) for i in range(3)]
    g1 = at("g1", FO + 56, [128, D])
    g2 = at("g2", FO + 60, [128, D])
    hj = at("hj", FO + 44, [128, D])
    hs = [at("hs0", FO + 64, [128, D]), at("hs1", FO + 68, [128, D])]
    row_ok = load("row", g1[:, :], rows[1].partition_broadcast(128), swa_dead, ret_dead, pool.now(), dve.now())
    row_ok = load("row", g2[:, :], rows[2].partition_broadcast(128))
    xs_free = [(pool.now(), dve.now())] * 3
    xl = {}

    def fetch_x(t):
        if t < NT:
            xl[t] = load(f"xl{t % 3}", xs[t % 3][:, :], x_in[128 * t:128 * t + 128, :], *xs_free[t % 3])

    for t in range(3):
        fetch_x(t)
    hhi2, hlo2 = H("h2")
    accd, r1, r2, h2_ok, hs_free, mg = {}, {}, {}, {}, [None, None], {}
    z_dead = (act.now(), dve.now(), pool.now())

    def m_square(t):
        r1[t] = act.do(lambda e: e.activation(hj[:, :], acc[:, t, :], ACT.Square, accum_out=st[:, 4 * t:4 * t + 1]),
                       accd[t], mg.get("j"), *z_dead)
        mg["j"] = r1[t]

    def m_residual(t):
        r = rstd(st[:, 4 * t:4 * t + 1], st[:, 4 * t + 1:4 * t + 2], 1.0 / D, EPS, r1[t])
        d = dve.do(lambda e: e.scalar_tensor_tensor(acc[:, t, :], acc[:, t, :], st[:, 4 * t + 1:4 * t + 2], g1[:, :],
                                                    ALU.mult, ALU.mult), r, row_ok)
        r1[t] = pool.do(lambda e: e.tensor_tensor(out=acc[:, t, :], in0=acc[:, t, :], in1=xs[t % 3][:, :], op=ALU.add), d, xl[t])
        xs_free[t % 3] = (r1[t],)
        fetch_x(t + 3)

    def m_square2(t):
        r2[t] = act.do(lambda e: e.activation(hj[:, :], acc[:, t, :], ACT.Square, accum_out=st[:, 4 * t + 2:4 * t + 3]), r1[t], mg["j"])
        mg["j"] = r2[t]

    def m_scale(t):
        r = rstd(st[:, 4 * t + 2:4 * t + 3], st[:, 4 * t + 3:4 * t + 4], 1.0 / D, EPS, r2[t])
        r2[t] = dve.do(lambda e: e.scalar_tensor_tensor(hs[t % 2][:, :], acc[:, t, :], st[:, 4 * t + 3:4 * t + 4], g2[:, :],
                                                        ALU.mult, ALU.mult), r, hs_free[t % 2])

    def m_transpose(t):
        hs_free[t % 2], h2_ok[t] = transpose_split(hs[t % 2], t, hhi2, hlo2, (r2[t],), (mg["x"], mg["m5"]))

    mix = Pipeline(NT, m_square, m_residual, m_square2, m_scale, m_transpose)

    def mix_after(t, tok):
        accd[t] = tok
        mix.push()

    mp5 = at("mp5", FO, [128, T], F32R)
    for g, ks_ in enumerate(([0, 1], [2, 3, 4], [5, 6, 7])):
        if g == 1:
            m5 = pool.do(lambda e: e.tensor_copy(mp5[:, :], mp[2][:, 1, :].bitcast(F32)), m_ok[5], pe.now())
        if g == 2:
            mg["x"] = pe.now()
            mg["m5"] = m5
            pe.wait(m5)
        run(rows_group("w_out", ks_, lambda k: (mp5[:, :] if k == 5 else mp[k // 2][:, k % 2, :], mlo[:, k, :]), acc,
                       (None,) if g == 0 else (), mix_after if g == 2 else None))

    mix_end = pe.now()

    def mlp(up, down, hi, lo, ready, acc, first_copy, after, free, tag, at_first, rest):
        uh = [at(f"uh{tag}{i}", FO + 8 * i, [128, 2, T], F32R) for i in range(2)]
        ul = [at(f"ul{tag}{i}", FO + 16 + 8 * i, [128, 2, T], F32R) for i in range(2)]
        sets = [[[at(f"{n}{tag}{s}{i}", FO + kb + o + 2 * i, [128, 512]) for i in range(2)] for n, o in (("rr", 0), ("uu", 4))]
                for s, kb in enumerate((at_first, 64))]
        u_ok, u_free, count = {}, {}, [0]
        lastd = [None, None]

        def up_evac(G, m):
            def evac(half, P, tok):
                rr, uu = sets[G > 1]
                i = count[0] % 2
                count[0] += 1
                c = slice(512 * half, 512 * half + 512)
                a = act.do(lambda e: e.activation(rr[i][:, :], P[:, :], ACT.Relu), tok, lastd[i], *free[0])
                p = pool.do(lambda e: e.tensor_tensor(out=uu[i][:, :], in0=rr[i][:, :], in1=rr[i][:, :], op=ALU.mult), a, lastd[i])
                b = act.do(lambda e: e.activation(uh[G % 2][:, m, c], rr[i][:, :], ACT.Square), a, u_free.get(G - 2))
                lastd[i] = dve.do(lambda e: e.tensor_tensor(out=ul[G % 2][:, m, c], in0=uu[i][:, :],
                                                            in1=uh[G % 2][:, m, c].bitcast(F32), op=ALU.subtract), p, b)
                if m == 1 and half == 1:
                    u_ok[G] = lastd[i]
                return a
            return evac

        def up_group(G):
            for m in range(2):
                yield from feature_major(up, 2 * G + m, hi, lo, up_evac(G, m))

        def down_group(G):
            pe.wait(u_ok[G], u_ok[15] if G == 14 else None)
            ks_ = [2 * G, 2 * G + 1] if G < 14 else [28, 29, 30, 31]
            yield from rows_group(down, ks_, lambda k: (uh[k // 2 % 2][:, k % 2, :], ul[k // 2 % 2][:, k % 2, :]), acc,
                                  (dve.now(), act.now(), pool.now()) if first_copy and G == 0 else (), after if G == 14 else None)
            u_free[G] = pe.now()

        feature_major_start(up, [0, 1, 2, 3], hi, lo, [up_evac(0, 0), up_evac(0, 1), up_evac(1, 0), up_evac(1, 1)], ready, rest)
        free[0] = (pe.now(), act.now(), dve.now(), pool.now())
        for G in range(15):
            if G > 0:
                run(up_group(G + 1))
            run(down_group(G))

    acc2 = at("acc2", FO + 32, [128, NT, D])
    yj = at("yj", FO + 68, [128, D])
    g3 = at("g3", FO + 64, [128, D])
    yhi, ylo = H("y")
    ys, y_ok, yd_ok = {}, {}, {}

    def y_square(t):
        if t == 0:
            ys["dead"] = mark["pre"]
            ys["set"] = (dve.now(), pool.now(), act.now())
            ys["row"] = load("row", g3[:, :], rows[3].partition_broadcast(128), *ys["set"])
        ys["j"] = ys[t] = act.do(lambda e: e.activation(yj[:, :], acc2[:, t, :], ACT.Square, accum_out=st[:, 4 * t:4 * t + 1]),
                                 accd[t], *ys["set"], ys.get("j"))

    def y_residual(t):
        r = rstd(st[:, 4 * t:4 * t + 1], st[:, 4 * t + 1:4 * t + 2], 1.0 / D, EPS, ys[t])
        d = dve.do(lambda e: e.scalar_tensor_tensor(acc2[:, t, :], acc2[:, t, :], st[:, 4 * t + 1:4 * t + 2], g3[:, :],
                                                    ALU.mult, ALU.mult), r, ys["row"])
        ys[t] = pool.do(lambda e: e.tensor_tensor(out=acc[:, t, :], in0=acc[:, t, :], in1=acc2[:, t, :], op=ALU.add), d)

    def y_transpose(t):
        r, y_ok[t] = transpose_split(acc[:, t, :], t, yhi, ylo, (ys[t],), (ys["dead"],))
        a = act.do(lambda e: e.activation(acc[:, t, :], acc[:, t, :], ACT.Copy, scale=ALPHA), r)
        yd_ok[t] = load("yd", yd[t], acc[:, t, :], a)

    mlp1_norm = Pipeline(NT, y_square, y_residual, y_transpose)

    def mlp1_after(t, tok):
        accd[t] = tok
        mlp1_norm.push()

    mlp("w_up", "w_down", hhi2, hlo2, h2_ok, acc2, True, mlp1_after, [z_dead + (mix_end,)], "a", 48, mix.rest())

    q2 = at("q2", FO, [128, 4, T])
    k2 = at("k2", FO + 16, [128, 4, T])
    vhi = [at("vhi", FO + 32, [128, NT, 768], F32R)[:, s, :] for s in range(NT)]
    vlo = [at("vlo", FO + 56, [128, 5, 768], F32R)[:, s, :] for s in range(5)] + \
          [at("vlo5", XO + 16, [128, 3, 768], F32R)[:, s, :] for s in range(3)]
    u2 = at("u2", FO + 32, [128, 4, T])
    pA = at("pA", FO + 48, [128, T])
    pB = at("pB", FO + 52, [128, T])
    pr = at("pr", FO + 58, [128, 64])
    pd = at("pd", XO, [128, 4, T])
    cc = at("cc", FO + 64, [8, T])
    ce = at("ce", FO + 68, [8, T])
    wfr = at("wfr", FO + 72, [128, 64])
    wfh = at("wfh", FO + 72.25, [128, 64], F32R)
    wfl = at("wfl", FO + 72.5, [128, 64], F32R)
    cT = at("cT", FO + 72.75, [128, 64])
    rm = at("rmask", FO + 59, [128, 128])
    pw = at("pw", XO + 29, [128, 4, 128])
    selr = at("selr", XO + 27, [36, 256])
    wf_ok = load("wf", wfr[:, :], wf, retention_end)
    a = act.do(lambda e: e.activation(wfh[:, :], wfr[:, :], ACT.Copy), wf_ok)
    wfs = dve.do(lambda e: e.tensor_tensor(out=wfl[:, :], in0=wfr[:, :], in1=wfh[:, :].bitcast(F32), op=ALU.subtract), a)
    freeF = (pe.now(), act.now(), dve.now(), pool.now())
    feature_major_start("u_2", [0, 1, 2, 3], yhi, ylo, [scaled_to(u2[:, m, :], 1.0, *freeF) for m in range(4)], y_ok, mlp1_norm.rest())
    freeF = (pe.now(), act.now(), dve.now(), pool.now())
    bf_ok = load("bf", st[0:8, 159:160], small["b_f"])
    ps_ok = load("ps", st[:, 152:156], small["pool_scale"])
    mk_ok = load("mask", rm[:, :], cst[:, 128:256], *freeF)
    pr_ok = load("pr", pr[:, :], cst[:, 1284:1348])
    pw_ok = load("pw", pw[:, :, :], poolw, yd_ok[7])
    sel_in = load("sel", selr[:, :], cst[0:36, 1348:1604], yd_ok[7])
    u_in = act.now()
    a = dve.do(lambda e: e.tensor_copy(maskb[:, :], rm[:, :]), mk_ok)
    mask_ok = dve.do(lambda e: e.tensor_copy(identb[:, :], ident[:, :]), a)

    for half in range(2):
        c = slice(512 * half, 512 * half + 512)
        b, P, f = banks.take()
        pe.wait(f, wfs)
        for k in range(8):
            tok = mm3(P[0:8, :], wfh[:, 8 * k:8 * k + 8], wfl[:, 8 * k:8 * k + 8], yhi[:, k, c], ylo[:, k, c], k == 0, k == 7)
        a = act.do(lambda e: e.activation(cc[:, c], P[0:8, :], ACT.Identity, bias=st[0:8, 159:160]), tok, bf_ok, *freeF)
        banks.give(b, a)
    a1 = act.do(lambda e: e.activation(ce[:, :], cc[:, :], ACT.Abs), a)
    a2 = act.do(lambda e: e.activation(ce[:, :], ce[:, :], ACT.Exp, scale=-1.0), a1)
    a2 = act.do(lambda e: e.activation(ce[:, :], ce[:, :], ACT.Ln, bias=1.0), a2)
    d = dve.do(lambda e: e.tensor_scalar(cc[:, :], cc[:, :], 0.0, None, ALU.min), a1)
    d = dve.do(lambda e: e.tensor_tensor(out=ce[:, :], in0=cc[:, :], in1=ce[:, :], op=ALU.subtract), d, a2)
    d = dve.do(lambda e: e.memset(cc[:, :], 1.0), d)
    c_sum = dve.do(lambda e: e.tensor_tensor_scan(cc[:, :], cc[:, :], ce[:, :], 0.0, ALU.mult, ALU.add), d)
    d = dve.do(lambda e: e.tensor_scalar(ce[:, :], cc[:, :], -1.0, None, ALU.mult), c_sum)
    c_st = load("cst_", cd, ce[:, :], d)

    def pool_differences():
        tok = None
        for g, win in enumerate((2, 4, 8, 16)):
            src, width, i = u2[:, g, :], 1, 0
            while width < win:
                dst = (pA, pB)[i % 2]
                a = dve.do(lambda e: e.tensor_tensor(out=dst[:, width:], in0=src[:, width:], in1=src[:, :T - width], op=ALU.add),
                           tok, u_in)
                tok = dve.do(lambda e: e.tensor_copy(dst[:, 0:width], src[:, 0:width]), tok)
                tok = (tok[0], max(tok[1], a[1]))
                src, width, i = dst, 2 * width, i + 1
                yield
            a = dve.do(lambda e: e.tensor_tensor(out=src[:, 0:16], in0=src[:, 0:16], in1=pr[:, 16 * g:16 * g + 16], op=ALU.mult), tok, pr_ok)
            a = dve.do(lambda e: e.tensor_tensor(out=pd[:, g, 0:16], in0=src[:, 0:16], in1=u2[:, g, 0:16], op=ALU.subtract), a, yd_ok[7])
            tok = dve.do(lambda e: e.scalar_tensor_tensor(pd[:, g, 16:], src[:, 16:], 1.0 / win, u2[:, g, 16:], ALU.mult, ALU.subtract))
            yield

    def qk_products():
        for m in range(4):
            yield from feature_major("q_2", m, yhi, ylo, scaled_to(q2[:, m, :], 0.125, *freeF))
            if m == 0:
                b, P, f = banks.take()
                pe.wait(f, c_sum)
                for t in range(NT):
                    tok = pe.do(lambda e: e.transpose(P[:, 8 * t:8 * t + 8], cc[:, 128 * t:128 * t + 128], ident[0:8, 0:8]))
                banks.give(b, dve.do(lambda e: e.tensor_copy(cT[:, :], P[:, 0:64]), tok))
                qk_["cT"] = dve.now()
            yield from feature_major("k_2", m, yhi, ylo, scaled_to(k2[:, m, :], 1.0, *freeF))

    qk_ = {}
    interleave(qk_products(), pool_differences(), 1.5)
    cT_ok = qk_["cT"]
    qk_ok, pd_ok = act.now(), dve.now()

    QS = [[at(f"QS{p}{j}", (HO + 32, XO)[p] + 4 * j, [128, T], F32R) for j in range(2)] for p in range(2)]
    KH = [[at(f"KH{p}{j}", (HO + 40, XO + 8)[p] + 4 * j, [128, T], F32R) for j in range(2)] for p in range(2)]
    KL = [at(f"KL{t}", FO + 16 + 4 * t, [128, T], F32R) for t in range(4)]
    stack_ok = {}

    def stack(t, *tokens):
        for j in range(2):
            own, other = slice(64 * j, 64 * j + 64), slice(64 - 64 * j, 128 - 64 * j)
            q, k = q2[own, t, :], k2[own, t, :]
            a = act.do(lambda e: e.activation(QS[t % 2][j][own, :], q, ACT.Copy), qk_ok, *tokens)
            act.do(lambda e: e.activation(KH[t % 2][j][own, :], k, ACT.Copy))
            b_ = act.do(lambda e: e.activation(KH[t % 2][j][other, :], k, ACT.Copy))
            yield
            pool.do(lambda e: e.tensor_tensor(out=QS[t % 2][j][other, :], in0=q, in1=QS[t % 2][j][own, :].bitcast(F32),
                                              op=ALU.subtract), a, pool.now())
            pool.do(lambda e: e.tensor_tensor(out=KL[t][own, :], in0=k, in1=KH[t % 2][j][own, :].bitcast(F32), op=ALU.subtract),
                    b_, pool.now())
            yield
        stack_ok[t] = (b_, pool.now())

    selm = at("selm", XO + 31, [36, 256], F32R)
    sel_ok = act.do(lambda e: e.activation(selm[:, :], selr[:, :], ACT.Copy), sel_in)
    for V, value in ((vhi, 1.0), (vlo, 0.0)):
        for s in range(NT):
            v = V[s].rearrange("p (a c) -> p a c", a=4)[:, :, 64:128]
            pool.do(lambda e: e.memset(v.bitcast(F32), value), pd_ok, mask_ok, c_st, cT_ok, yd_ok[7])
    ends_ok = pool.now()
    W["limit"] = W["cur"] + 4 + SLOTS
    for vh in range(2):
        def ev(t, P, tok):
            hi_, lo_ = (V[t].rearrange("p (a b c) -> p a b c", a=4, b=3)[:, 2 * vh:2 * vh + 2, 0:3:2, :] for V in (vhi, vlo))
            src = P[:, 0:256].rearrange("p (a b c) -> p a b c", a=2, b=2)
            a = act.do(lambda e: e.activation(hi_, src, ACT.Copy), tok, pd_ok, mask_ok)
            return dve.do(lambda e: e.tensor_tensor(out=lo_, in0=src, in1=hi_.bitcast(F32), op=ALU.subtract), a, c_st, cT_ok)
        run(token_major("v_2", 256 * vh, yhi, ylo, ev))
    v_ok = (dve.now(), ends_ok)
    raw_dead = (act.now(), dve.now())
    y_dead = pe.now()
    run(stack(0, y_dead))

    chi = [at(f"chi{k}", kb, [128, T], F32R) for k, kb in enumerate((HO, HO + 4, HO + 8, HO + 12, FO, FO + 16, FO + 8, FO + 12))]
    clo = [at(f"clo{k}", kb, [128, T], F32R)
           for k, kb in enumerate((HO + 16, HO + 20, HO + 24, HO + 28, FO + 4, HO + 60, FO + 20, FO + 24))]
    cat_ok = {}
    for g in range(4):
        for half in range(2):
            c = slice(512 * half, 512 * half + 512)
            b, P, f = banks.take()
            pe.wait(f, pd_ok, pw_ok)
            tok = pe.do(lambda e: e.matmul(P[:, :], pw[:, g, :], pd[:, g, c], start=True, stop=True))
            s = st[:, 152 + g:153 + g]
            h_ = act.do(lambda e: e.activation(chi[g][:, c], P[:, :], ACT.Copy, scale=s), tok, ps_ok, y_dead)
            l_ = dve.do(lambda e: e.scalar_tensor_tensor(clo[g][:, c], P[:, :], s, chi[g][:, c].bitcast(F32),
                                                         ALU.mult, ALU.subtract), h_)
            banks.give(b, l_)
        cat_ok[g] = l_
    pd_dead = pw_dead = pe.now()

    rl = at("rl", XO + 29, [128, 512])
    ov = at("ov", HO + 54, [128, 512])
    ring = [HO + 56, HO + 58] + [RO + 2 * i for i in range(6)]
    PH = [at(f"PH{i}", ring[2 * i], [128, 512], F32R) for i in range(4)]
    PL = [at(f"PL{i}", ring[2 * i + 1], [128, 512], F32R) for i in range(4)]
    PX = [at(f"PX{i}", ring[2 * i + 1], [128, 512]) for i in range(4)]
    nb = [at("nb0", HO + 48, [128, T]), at("nb1", XO + 25, [128, T])]
    nmr = [at("nmr", HO + 52, [36, 512], F32R)[32 * i:32 * i + 4, :] for i in range(2)]
    nh = at("nh", FO + 72, [128, 8], F32R)
    n4 = at("n4", FO + 72.0625, [128, 16])
    nct = at("nct", FO + 72.25, [128, 64])
    nct_ok = dve.do(lambda e: e.tensor_scalar(nct[:, :], cT[:, :], -1.0, None, ALU.mult), cT_ok, wfs)
    items = [(t, Q) for t in range(4) for Q in range(2)]
    nb_ok, nmr_ok, item_done, fa = {}, {}, {}, {}

    def fetch_nb(t, *tokens):
        for j in range(2):
            nb_ok[2 * t + j] = load(f"nb{j}", nb[j][:, :], cd[2 * t + j].partition_broadcast(128), c_st, *tokens)

    def maxima(idx):
        t, Q = items[idx]
        p, mx = t % 2, st[:, 32 * (idx % 2):32 * (idx % 2) + 16]
        for ii in range(4):
            i = 4 * Q + ii
            for j in range(2):
                own = slice(64 * j, 64 * j + 64)
                for ch in range(Q + 1):
                    w = 512 if ch < Q else 128 * ii + 128
                    qc, kc = slice(128 * i, 128 * i + 128), slice(512 * ch, 512 * ch + w)
                    b, P, f = banks.take()
                    pe.wait(f, *stack_ok[t])
                    pe.run(lambda e: e.matmul(P[:, 0:w], QS[p][j][:, qc], KH[p][j][:, kc], start=True, stop=False))
                    g = lambda e: e.matmul(P[:, 0:w], QS[p][j][own, qc], KL[t][own, kc], start=False, stop=ch < Q)
                    if ch == Q:
                        pe.wait(mask_ok)
                        pe.run(g)
                        tok = pe.do(lambda e: e.matmul(P[:, w - 128:w], identb[:, :], maskb[:, :], start=False, stop=True))
                    else:
                        tok = pe.do(g)
                    mo = mx[:, 8 * ch + 2 * ii + j:8 * ch + 2 * ii + j + 1]
                    d = dve.do(lambda e: e.tensor_tensor_reduce(out=P[:, 0:w], in0=P[:, 0:w], in1=nb[j][:, kc], scale=1.0, scalar=NEG,
                                                                op0=ALU.add, op1=ALU.max, accum_out=mo), tok, nb_ok[2 * t + j])
                    banks.give(b, d)
                yield
        m = mx[:, 8 * Q:8 * Q + 8]
        if Q:
            d = dve.do(lambda e: e.tensor_tensor(out=m, in0=m, in1=mx[:, 0:8], op=ALU.max), d)
            if t < 3:
                fetch_nb(t + 1, d)
        m3 = m.rearrange("p (i j) -> p i j", j=2)
        cq = cT[:, 32 * Q:32 * Q + 32].rearrange("p (i h) -> p i h", h=8)[:, :, 2 * t:2 * t + 2]
        d = dve.do(lambda e: e.tensor_tensor(out=m3, in0=m3, in1=cq, op=ALU.add), d, cT_ok)
        d = dve.do(lambda e: e.tensor_tensor(out=m3, in0=cq, in1=m3, op=ALU.subtract), d)
        h_ = dve.do(lambda e: e.tensor_copy(nh[:, :], m), d)
        n3 = n4[:, :].rearrange("p (a two) -> p a two", two=2)
        dve.do(lambda e: e.tensor_copy(n3[:, :, 0], nh[:, :].bitcast(F32)), h_, fa.get("n4"))
        d = dve.do(lambda e: e.tensor_tensor(out=n3[:, :, 1], in0=m, in1=nh[:, :].bitcast(F32), op=ALU.subtract))
        yield
        b, P, f = banks.take()
        pe.wait(f, d)
        for ii in range(4):
            tok = pe.do(lambda e: e.transpose(P[0:4, 128 * ii:128 * ii + 128], n4[:, 4 * ii:4 * ii + 4], ident[:, :]))
        fa["n4"] = tok
        nmr_ok[idx] = act.do(lambda e: e.activation(nmr[idx % 2][:, :], P[0:4, :], ACT.Copy), tok, item_done.get(idx - 2), y_dead)
        banks.give(b, nmr_ok[idx])

    PHL_free, rl_free, tails = [raw_dead] * 4, [pw_dead, y_dead], []

    def weights(n, idx, j, k):
        t, Q = items[idx]
        p, own = t % 2, slice(64 * j, 64 * j + 64)
        q0 = max(512 * Q, 128 * k)
        w = 512 * Q + 512 - q0
        kc = slice(128 * k, 128 * k + 128)
        diag = q0 == 128 * k
        b, P, f = banks.take()
        pe.wait(f, nmr_ok[idx], sel_ok, *stack_ok[t])
        pe.run(lambda e: e.matmul(P[:, 0:w], selm[32 * (idx % 2):32 * (idx % 2) + 4, 128 * j:128 * j + 128], nmr[idx % 2][:, 512 - w:512], start=True, stop=False))
        pe.run(lambda e: e.matmul(P[:, 0:w], KH[p][j][:, kc], QS[p][j][:, q0:q0 + w], start=False, stop=False))
        g = lambda e: e.matmul(P[:, 0:w], KL[t][own, kc], QS[p][j][own, q0:q0 + w], start=False, stop=not diag)
        if diag:
            pe.run(g)
            tok = pe.do(lambda e: e.matmul(P[:, 0:128], maskb[:, :], identb[:, :], start=False, stop=True))
        else:
            tok = pe.do(g)
        bias = nct[:, 8 * k + 2 * t + j:8 * k + 2 * t + j + 1]
        i = n % 4
        h_ = act.do(lambda e: e.activation(PH[i][:, 0:w], P[:, 0:w], ACT.Exp, bias=bias), tok, nct_ok, y_dead, *PHL_free[i])
        a = act.do(lambda e: e.activation(PX[i][:, 0:w], P[:, 0:w], ACT.Exp, bias=bias))
        banks.give(b, a)
        d = dve.do(lambda e: e.tensor_tensor(out=PL[i][:, 0:w], in0=PX[i][:, 0:w], in1=PH[i][:, 0:w].bitcast(F32), op=ALU.subtract), a)
        return w, (h_, a), (d,)

    def values(n, idx, j, k, made_):
        t, Q = items[idx]
        w, ok, ok_lo = made_
        vc = slice(192 * t + 64 * j, 192 * t + 64 * j + 128)
        last = k == 4 * Q + 3
        ob = 6 + j
        O = banks.t[ob]
        if k == 0:
            pe.wait(banks.freed[ob])
        pe.wait(*v_ok, *ok)
        for V, W_, a, z in ((vhi, PH, k == 0, False), (vlo, PH, False, False), (vhi, PL, False, last)):
            if W_ is PL:
                pe.wait(*ok_lo)
            tok = pe.do(lambda e: e.matmul(O[:, 512 - w:512], V[k][:, vc], W_[n % 4][:, 0:w], start=a, stop=z))
        PHL_free[n % 4] = (tok,)
        if last:
            own, other = slice(64 * j, 64 * j + 64), slice(64 - 64 * j, 128 - 64 * j)
            act.do(lambda e: e.activation(rl[own, :], O[other, :], ACT.Copy), tok, *rl_free)
            a = act.do(lambda e: e.activation(ov[own, :], O[own, :], ACT.Copy))
            banks.give(ob, a)
            if j:
                item_done[idx] = tok
                tails.append(tail(idx, a))

    def tail(idx, a):
        t, Q = items[idx]
        c_ = slice(512 * Q, 512 * Q + 512)
        for q in range(2):
            c = slice(256 * q, 256 * q + 256)
            d = dve.do(lambda e: e.reciprocal(rl[:, c], rl[:, c]), a)
            yield
        d = dve.do(lambda e: e.tensor_tensor(out=ov[:, :], in0=ov[:, :], in1=rl[:, :], op=ALU.mult), d)
        yield
        a = act.do(lambda e: e.activation(chi[4 + t][:, c_], ov[:, :], ACT.Copy), d, y_dead, *stack_ok[max(t, 1)])
        cat_ok[4 + t] = pool.do(lambda e: e.tensor_tensor(out=clo[4 + t][:, c_], in0=ov[:, :], in1=chi[4 + t][:, c_].bitcast(F32),
                                                          op=ALU.subtract), a, pool.now())
        rl_free[:] = [d, cat_ok[4 + t]]

    steps = [(idx, j, k) for idx, (t, Q) in enumerate(items) for j in range(2) for k in range(4 * Q + 4)]
    banks.turn(range(6))
    fetch_nb(0, y_dead, sel_ok)
    interleave(maxima(0), stack(1, pd_dead), 2)
    LAG = 3
    restack = iter(())
    made_ = {}
    side, credit = iter(()), 0.0
    for n in range(len(steps) + LAG):
        if n < len(steps):
            idx, j, k = steps[n]
            t, Q = items[idx]
            if j == 0 and k == 0:
                run(side)
                side = maxima(idx + 1) if idx < 7 else iter(())
                per = 10.0 / (8 * Q + 8 - 1)
            made_[n] = weights(n, idx, j, k)
            if Q == 0 and j == 0 and k == 3 and 0 < t < 3:
                restack = stack(t + 1, item_done[idx - 1])
            next(restack, None)
            credit += per
            while credit >= 1:
                credit -= 1
                next(side, None)
        if n >= LAG:
            values(n - LAG, *steps[n - LAG], made_.pop(n - LAG))
        for g in tails:
            next(g, None)
    for g in tails:
        run(g)
    banks.turn(range(8))
    W["limit"] = NPIECES
    for n in W["late"]:
        fetch(n, pe.now())

    zhi, zlo = H("z")
    lg = at("lg", FO + 32, [128, D])
    lb = at("lb", FO + 36, [128, D])
    lx = [at(f"lx{i}", FO + 40 + 4 * i, [128, D]) for i in range(3)]
    yr = [at(f"yr{i}", FO + 52 + 4 * i, [128, D]) for i in range(3)]
    a_dead = (pe.now(), act.now(), dve.now(), pool.now())
    yr_free, yr_ok = [a_dead] * 3, {}

    def fetch_y(t):
        if t < NT:
            yr_ok[t] = load(f"yr{t % 3}", yr[t % 3][:, :], yd[t], yd_ok[7], *yr_free[t % 3])

    def seed(t):
        if t not in seeded:
            seeded.add(t)
            if t > 0:
                yr_free[(t - 1) % 3] = (dve.now(),)
                fetch_y(t + 2)
        return yr[t % 3], yr_ok[t]

    seeded = set()
    for t in range(3):
        fetch_y(t)
    row_ok = load("row", lg[:, :], rows[4].partition_broadcast(128), *a_dead)
    row_ok = load("row", lb[:, :], rows[5].partition_broadcast(128))
    lns, z_ok, lx_free, z2_ok = {}, {}, [(), (), ()], {}

    def l_stats(t):
        d = accd[t]
        for c in range(2):
            d = dve.do(lambda e: e.bn_stats(st[:, 12 * t + 6 * c:12 * t + 6 * c + 6], acc[:, t, 512 * c:512 * c + 512]), d, dve.now())
        d = dve.do(lambda e: e.bn_aggr(st[:, 96 + 4 * t:98 + 4 * t], st[:, 12 * t:12 * t + 12]), d)
        v = st[:, 97 + 4 * t:98 + 4 * t]
        d = dve.do(lambda e: e.tensor_scalar(v, v, 1.0, LN_EPS, ALU.mult, ALU.add), d)
        lns[t] = act.do(lambda e: e.activation(v, v, ACT.Sqrt), d)

    def l_scale(t, dst, gain, row, *tokens):
        m, v = st[:, 96 + 4 * t:97 + 4 * t], st[:, 97 + 4 * t:98 + 4 * t]
        r = dve.do(lambda e: e.reciprocal(v, v), lns[t])
        r = dve.do(lambda e: e.scalar_tensor_tensor(m, m, -1.0, v, ALU.mult, ALU.mult), r)
        d = act.do(lambda e: e.activation(dst, acc[:, t, :], ACT.Identity, bias=m, scale=v), r, *tokens)
        lns[t] = pool.do(lambda e: e.tensor_tensor(out=dst, in0=dst, in1=gain[:, :], op=ALU.mult), d, row)

    def l_bias(t, dst, bias, row):
        lns[t] = dve.do(lambda e: e.tensor_tensor(out=dst, in0=dst, in1=bias[:, :], op=ALU.add), lns[t], row)

    def l_transpose(t):
        r, z_ok[t] = transpose_split(lx[t % 3], t, zhi, zlo, (lns[t],), (lnx[0],))
        z2_ok[t] = act.do(lambda e: e.activation(acc[:, t, :], lx[t % 3][:, :], ACT.Copy, scale=ALPHA), lns[t])
        lx_free[t % 3] = (r, z2_ok[t])

    lnx = [None]
    ln1 = Pipeline(NT, l_stats, lambda t: l_scale(t, lx[t % 3][:, :], lg, row_ok, *lx_free[t % 3]),
                   lambda t: l_bias(t, lx[t % 3][:, :], lb, row_ok), l_transpose)

    def ln1_after(t, tok):
        accd[t] = tok
        ln1.push()

    clo5 = at("clo5b", FO + 68, [128, T], F32R)
    c5 = pool.do(lambda e: e.tensor_copy(clo5[:, :], clo[5][:, :].bitcast(F32)), cat_ok[5], *a_dead)
    clo[5] = clo5
    for g, ks_ in enumerate(([0, 1], [2, 3], [4, 5, 6, 7])):
        pe.wait(c5 if g == 2 else None, *[cat_ok[k] for k in ks_])
        lnx[0] = pe.now()
        run(rows_group("w_out_2", ks_, lambda k: (chi[k], clo[k]), acc, a_dead if g == 0 else (), ln1_after if g == 2 else None,
                       seed if g == 0 else None))

    fg = at("fg", FO + 32, [128, D])
    fb = at("fb", FO + 36, [128, D])
    outs = []

    def o_out(t):
        outs.append(load("out", out[128 * t:128 * t + 128, :], acc[:, t, :], lns[t]))

    ln2 = Pipeline(NT, l_stats, lambda t: l_scale(t, acc[:, t, :], fg, *frow), lambda t: l_bias(t, acc[:, t, :], fb, *frow), o_out)

    def ln2_after(t, tok):
        if t == 0:
            load("row", fg[:, :], rows[6].partition_broadcast(128), dve.now(), pool.now(), act.now())
            frow.append(load("row", fb[:, :], rows[7].partition_broadcast(128)))
        accd[t] = tok
        ln2.push()

    frow = []
    mlp("w_mlp1", "w_mlp2", zhi, zlo, z_ok, acc, False, ln2_after, [(pe.now(), pool.now())], "b", 52, ln1.rest())
    run(ln2.rest())
    sp.wait(outs[-1])
    assert W["cur"] == NPIECES, W["cur"]

    return descs


def pack(inputs, descs):
    cuts = {}
    edge = np.cumsum([0, 512, 512, 1024, 1024, 512, 128, 128, 1024, 1024])
    w_in = inputs["w_in"][0]
    for name, a, b in zip(("q_r", "k_r", "v_r", "g_r", "q_s", "k_s", "v_s", "gate_r", "gate_s"), edge[:-1], edge[1:]):
        cuts[name] = w_in[:, a:b]
    heads = [h for m in range(4) for h in (m, 4 + m)]
    cuts["q_s"] = cuts["q_s"].reshape(1024, 8, 64)[:, heads].reshape(1024, 512)
    cuts["w_swa_out"] = inputs["w_swa_out"][0].reshape(8, 64, 1024)[heads].reshape(512, 1024)
    w2 = inputs["w_in_2"][0]
    for i, name in enumerate(("u_2", "q_2", "k_2", "v_2")):
        cuts[name] = w2[:, 512 * i:512 * i + 512]
    for name, key in (("w_ret_out",) * 2, ("w_out",) * 2, ("w_up",) * 2, ("w_down",) * 2, ("w_out_2",) * 2,
                      ("w_mlp1", "w_mlp1_2"), ("w_mlp2", "w_mlp2_2")):
        cuts[name] = inputs[key][0]
    wp = np.empty((len(descs), 128, 1024), np.float32)
    for n, d in enumerate(descs):
        w = cuts[d[1]]
        if d[0] == "F":
            wp[n].reshape(128, 8, 128)[:] = w[:, 128 * d[2]:128 * d[2] + 128].reshape(8, 128, 128).transpose(1, 0, 2)
        elif d[0] == "T":
            wp[n].reshape(128, 4, 256)[:] = w[128 * d[3]:128 * d[3] + 512, d[2]:d[2] + 256].reshape(4, 128, 256).transpose(1, 0, 2)
        elif d[0] == "D":
            wp[n] = w[128 * d[2]:128 * d[2] + 128]
        else:
            wp[n].reshape(128, 2, 4, 128)[:] = w[:, 256 * d[2]:256 * d[2] + 256].reshape(4, 128, 2, 128).transpose(1, 2, 0, 3)
    return wp


def kernel(**inputs):
    import concourse.bacc as _bacc
    from concourse.bass_utils import run_bass_kernel_spmd as _run

    inputs = {k: np.asarray(v) for k, v in inputs.items()}
    nc = _bacc.Bacc("TRN2", target_bir_lowering=False, num_devices=1, dynamic_dma_scratch_size=1024)
    cst, swab = constants()
    arrays = {
        "x_d": np.ascontiguousarray(inputs["x"][0]),
        "rows_d": np.concatenate([inputs[n] for n in ("pre_mix_norm", "post_mix_norm", "pre_mlp_norm", "post_mlp_norm",
                                                      "ln1_g_2", "ln1_b_2", "ln2_g_2", "ln2_b_2")]),
        "cst_d": cst,
        "swab_d": swab,
        "sinks_d": np.ascontiguousarray(inputs["sinks"][0]),
        "bf_d": np.ascontiguousarray(inputs["b_f_2"][0].reshape(8, 1)),
        "ps_d": np.ascontiguousarray(inputs["pool_scale_2"][0].reshape(4, 128).T),
        "pw_d": np.ascontiguousarray(inputs["pool_w_2"][0].transpose(1, 0, 2)),
        "wf_d": np.ascontiguousarray(inputs["w_in_2"][0][:, 2048:].reshape(8, 128, 8).transpose(1, 0, 2).reshape(128, 64)),
    }
    I = {n: nc.dram_tensor(n, a.shape, F32, kind="ExternalInput").ap() for n, a in arrays.items()}
    I["wp_d"] = nc.dram_tensor("wp_d", (NPIECES, 128, 1024), F32, kind="ExternalInput").ap()
    out = nc.dram_tensor("out_d", (T, D), F32, kind="ExternalOutput").ap()
    sg = nc.dram_tensor("sg_d", (16, 128, T), F32, kind="Internal").ap()
    cd = nc.dram_tensor("cd_d", (8, T), F32, kind="Internal").ap()
    yd = nc.dram_tensor("yd_d", (NT, 128, D), F32, kind="Internal").ap()
    descs = build(nc, I["wp_d"], I["x_d"], I["rows_d"], {"sinks": I["sinks_d"], "b_f": I["bf_d"], "pool_scale": I["ps_d"]},
                  I["cst_d"], I["swab_d"], I["pw_d"], I["wf_d"], out, sg, cd, yd)
    arrays["wp_d"] = pack(inputs, descs)
    r = _run(nc, [arrays], core_ids=[0])
    return r.results[0]["out_d"].reshape(1, T, D)
```
